# Optimizing a Trainium2 kernel written in Bass

```python
import math
import jax
import jax.numpy as jnp
from jax import lax
import numpy as np

D_MODEL = 1024
BATCH = 1
SEQ = 256
DEPTH = 2

GRID_W = 64
CTX_LEN = 256
HEADS_A = 4
HD_A = 64
VD_A = 2 * HD_A
WIDTH_A = HEADS_A * VD_A
HEADS_B = 4
KV_HEADS_B = 2
REP_B = HEADS_B // KV_HEADS_B
HD_B = 64
WIDTH_B = HEADS_B * HD_B
WINDOW = 128
BLOCK = 128
CONV_CH = 256
CONV_K = 31
MIX_WIDTH = WIDTH_A + WIDTH_B + CONV_CH
SEG_QA = HEADS_A * 2 * HD_A
SEG_KA = HEADS_A * 2 * HD_A
SEG_VA = HEADS_A * VD_A
SEG_QB = HEADS_B * HD_B
SEG_KB = KV_HEADS_B * HD_B
SEG_VB = KV_HEADS_B * HD_B
SEG_UC = 2 * CONV_CH
IN_WIDTH = SEG_QA + SEG_KA + SEG_VA + SEG_QB + SEG_KB + SEG_VB + SEG_UC
SPLIT_POINTS = (SEG_QA,
                SEG_QA + SEG_KA,
                SEG_QA + SEG_KA + SEG_VA,
                SEG_QA + SEG_KA + SEG_VA + SEG_QB,
                SEG_QA + SEG_KA + SEG_VA + SEG_QB + SEG_KB,
                SEG_QA + SEG_KA + SEG_VA + SEG_QB + SEG_KB + SEG_VB)
N_EXPERTS = 16
N_GROUPS = 4
EXPERTS_PER_GROUP = N_EXPERTS // N_GROUPS
TOP_K = 2
EXPERT_FF = 512
ROPE_BASE = 10000.0
EPS = 1e-6
NEG_INF = -1e30

kernel_name = 'hybrid_diffusion_parallel_heads_moe'

def rmsnorm(x, g):
    xf = x.astype(jnp.float32)
    y = xf * lax.rsqrt(jnp.mean(xf * xf, axis=-1, keepdims=True) + EPS)
    return (y * g.astype(jnp.float32)).astype(x.dtype)

def modulate(h, shift, scale):
    return h * (1 + scale) + shift

def axial_rope_tables(n_tok, head_dim):
    rows = n_tok // GRID_W
    row = jnp.repeat(jnp.arange(rows, dtype=jnp.float32), GRID_W)
    col = jnp.tile(jnp.arange(GRID_W, dtype=jnp.float32), rows)
    pos = jnp.stack([row, col], axis=-1)
    n_freq = head_dim // 4
    inv = ROPE_BASE ** (-jnp.arange(n_freq, dtype=jnp.float32) / n_freq)
    ang = pos[:, :, None] * inv[None, None, :]
    return jnp.cos(ang), jnp.sin(ang)

def apply_axial_rope(x, cos, sin):
    shp = x.shape
    nf = shp[-1] // 4
    xr = x.reshape(shp[:-1] + (2, 2, nf))
    x1 = xr[..., 0, :]
    x2 = xr[..., 1, :]
    bshape = (1, shp[1]) + (1,) * (x.ndim - 3) + (2, nf)
    c = cos.reshape(bshape).astype(x.dtype)
    s = sin.reshape(bshape).astype(x.dtype)
    out = jnp.stack([x1 * c - x2 * s, x2 * c + x1 * s], axis=-2)
    return out.reshape(shp)

def diff_softmax_attend(q, k, v, lam):
    s = jnp.einsum('bqhmd,bkhmd->bhmqk', q, k).astype(jnp.float32) * (HD_A ** -0.5)
    p = jax.nn.softmax(s, axis=-1)
    a = p[:, :, 0] - lam * p[:, :, 1]
    return jnp.einsum('bhqk,bkhe->bqhe', a.astype(v.dtype), v)

def diff_attention_latent(q, k_all, v_all, lam):
    B, S = q.shape[:2]
    nb = S // BLOCK
    qb = jnp.moveaxis(q.reshape((B, nb, BLOCK) + q.shape[2:]), 1, 0)
    ob = lax.map(lambda qi: diff_softmax_attend(qi, k_all, v_all, lam), qb)
    return jnp.moveaxis(ob, 0, 1).reshape(B, S, HEADS_A, VD_A)

def diff_head_norm(o, g, lambda_init):
    of = o.astype(jnp.float32)
    y = of * lax.rsqrt(jnp.mean(of * of, axis=-1, keepdims=True) + EPS) * g.astype(jnp.float32)
    y = y * (1.0 - lambda_init)
    return y.reshape(o.shape[:2] + (WIDTH_A,)).astype(o.dtype)

def sink_softmax(scores, sink):
    full = jnp.concatenate([scores, jnp.broadcast_to(sink, scores.shape[:-1] + (1,))], axis=-1)
    return jax.nn.softmax(full, axis=-1)[..., :-1]

def window_sink_gqa_latent(q, k, v, kc, vc, sink):
    B, S = q.shape[:2]
    C = kc.shape[1]
    nb = S // BLOCK
    scale = HD_B ** -0.5
    qb = q.reshape(B, nb, BLOCK, KV_HEADS_B, REP_B, HD_B)
    pad = ((0, 0), (BLOCK, BLOCK), (0, 0), (0, 0))
    kp = jnp.pad(k, pad).reshape(B, nb + 2, BLOCK, KV_HEADS_B, HD_B)
    vp = jnp.pad(v, pad).reshape(B, nb + 2, BLOCK, KV_HEADS_B, HD_B)
    kband = jnp.concatenate([kp[:, :-2], kp[:, 1:-1], kp[:, 2:]], axis=2)
    vband = jnp.concatenate([vp[:, :-2], vp[:, 1:-1], vp[:, 2:]], axis=2)
    s_loc = jnp.einsum('bnqgrd,bnkgd->bngrqk', qb, kband).astype(jnp.float32) * scale
    blk = jnp.arange(nb)[:, None]
    qpos = blk * BLOCK + jnp.arange(BLOCK)[None, :]
    kpos = (blk - 1) * BLOCK + jnp.arange(3 * BLOCK)[None, :]
    valid = (jnp.abs(qpos[:, :, None] - kpos[:, None, :]) <= WINDOW) & (kpos >= 0)[:, None, :] & (kpos < S)[:, None, :]
    s_loc = jnp.where(valid[None, :, None, None], s_loc, NEG_INF)
    s_ctx = jnp.einsum('bnqgrd,bkgd->bngrqk', qb, kc).astype(jnp.float32) * scale
    sk = sink.astype(jnp.float32).reshape(KV_HEADS_B, REP_B)[None, None, :, :, None, None]
    p = sink_softmax(jnp.concatenate([s_ctx, s_loc], axis=-1), sk)
    p_ctx = p[..., :C].astype(v.dtype)
    p_loc = p[..., C:].astype(v.dtype)
    o = jnp.einsum('bngrqk,bkgd->bnqgrd', p_ctx, vc) + jnp.einsum('bngrqk,bnkgd->bnqgrd', p_loc, vband)
    return o.reshape(B, S, WIDTH_B)

def sink_gqa_context(q, k, v, sink):
    B, C = q.shape[:2]
    qg = q.reshape(B, C, KV_HEADS_B, REP_B, HD_B)
    s = jnp.einsum('bqgrd,bkgd->bgrqk', qg, k).astype(jnp.float32) * (HD_B ** -0.5)
    sk = sink.astype(jnp.float32).reshape(KV_HEADS_B, REP_B)[None, :, :, None, None]
    p = sink_softmax(s, sk)
    o = jnp.einsum('bgrqk,bkgd->bqgrd', p.astype(v.dtype), v)
    return o.reshape(B, C, WIDTH_B)

def conv_module(u, w, b, ln_g, ln_b):
    a, g = jnp.split(u, 2, axis=-1)
    z = a * jax.nn.sigmoid(g)
    z = lax.conv_general_dilated(z, w[:, None, :], window_strides=(1,),
                                 padding=[(CONV_K // 2, CONV_K // 2)],
                                 dimension_numbers=('NWC', 'WIO', 'NWC'),
                                 feature_group_count=CONV_CH) + b
    zf = z.astype(jnp.float32)
    mu = jnp.mean(zf, axis=-1, keepdims=True)
    var = jnp.mean(jnp.square(zf - mu), axis=-1, keepdims=True)
    zn = (zf - mu) * lax.rsqrt(var + EPS) * ln_g.astype(jnp.float32) + ln_b.astype(jnp.float32)
    return jax.nn.silu(zn).astype(u.dtype)

def grouped_moe(h, router_w, router_bias, w1, w3, w2):
    n = h.shape[0]
    s = jax.nn.sigmoid((h @ router_w).astype(jnp.float32))
    biased = s + router_bias.astype(jnp.float32)
    grp = lax.top_k(biased.reshape(n, N_GROUPS, EXPERTS_PER_GROUP), TOP_K)[0].sum(-1)
    g_sel = jnp.argmax(grp, axis=-1)
    in_grp = (jnp.arange(N_EXPERTS) // EXPERTS_PER_GROUP)[None, :] == g_sel[:, None]
    _, idx = lax.top_k(jnp.where(in_grp, biased, -jnp.inf), TOP_K)
    sel = jnp.take_along_axis(s, idx, axis=-1)
    wts = sel / jnp.sum(sel, axis=-1, keepdims=True)
    combine = jnp.sum(jax.nn.one_hot(idx, N_EXPERTS, dtype=jnp.float32) * wts[..., None], axis=1).astype(h.dtype)
    out = jnp.zeros_like(h)
    for e in range(N_EXPERTS):
        he = (jax.nn.silu(h @ w1[e]) * (h @ w3[e])) @ w2[e]
        out = out + combine[:, e:e + 1] * he
    return out

def setup_inputs(seed: int = 0) -> dict:
    key = jax.random.key(seed)
    ks = jax.random.split(key, 24)
    D = D_MODEL

    def nrm(k, shape, s):
        return jax.random.normal(k, shape, jnp.float32) * s

    return {
        'x': nrm(ks[0], (BATCH, SEQ, D), 1.0),
        'c': nrm(ks[1], (BATCH, D), 1.0),
        'ctx': nrm(ks[2], (BATCH, CTX_LEN, D), 1.0),
        'c_ctx': nrm(ks[3], (D,), 1.0),
        'w_ada': nrm(ks[4], (DEPTH, D, 6 * D), 0.5 * D ** -0.5),
        'b_ada': nrm(ks[5], (DEPTH, 6 * D), 0.02),
        'g_mix': 1.0 + nrm(ks[6], (DEPTH, D), 0.05),
        'w_in': nrm(ks[7], (DEPTH, D, IN_WIDTH), D ** -0.5),
        'diff_lambda': nrm(ks[8], (DEPTH, 4, HD_A), 0.1),
        'diff_norm_g': 1.0 + nrm(ks[9], (DEPTH, VD_A), 0.05),
        'attn_sink': nrm(ks[10], (DEPTH, HEADS_B), 0.5),
        'conv_w': nrm(ks[11], (DEPTH, CONV_K, CONV_CH), CONV_K ** -0.5),
        'conv_b': nrm(ks[12], (DEPTH, CONV_CH), 0.02),
        'conv_ln_g': 1.0 + nrm(ks[13], (DEPTH, CONV_CH), 0.05),
        'conv_ln_b': nrm(ks[14], (DEPTH, CONV_CH), 0.02),
        'w_out': nrm(ks[15], (DEPTH, MIX_WIDTH, D), MIX_WIDTH ** -0.5),
        'g_ffn': 1.0 + nrm(ks[16], (DEPTH, D), 0.05),
        'router_w': nrm(ks[17], (D, N_EXPERTS), D ** -0.5),
        'router_bias': nrm(ks[18], (N_EXPERTS,), 0.01),
        'w1': nrm(ks[19], (DEPTH, N_EXPERTS, D, EXPERT_FF), D ** -0.5),
        'w3': nrm(ks[20], (DEPTH, N_EXPERTS, D, EXPERT_FF), D ** -0.5),
        'w2': nrm(ks[21], (DEPTH, N_EXPERTS, EXPERT_FF, D), EXPERT_FF ** -0.5),
        'g_final': 1.0 + nrm(ks[22], (D,), 0.05),
    }

def reference(x, c, ctx, c_ctx, w_ada, b_ada, g_mix, w_in, diff_lambda, diff_norm_g, attn_sink,
              conv_w, conv_b, conv_ln_g, conv_ln_b, w_out, g_ffn, router_w, router_bias, w1, w3, w2, g_final):
    B, S, D = x.shape
    C = ctx.shape[1]
    cos, sin = axial_rope_tables(S, HD_A)
    xc = ctx
    silu_c = jax.nn.silu(c)
    silu_cc = jax.nn.silu(c_ctx)
    for l in range(DEPTH):
        last = l == DEPTH - 1
        mod = (silu_c @ w_ada[l] + b_ada[l]).reshape(B, 6, D)
        modc = (silu_cc @ w_ada[l] + b_ada[l]).reshape(6, D)

        h = modulate(rmsnorm(x, g_mix[l]), mod[:, 0, None], mod[:, 1, None])
        hc = modulate(rmsnorm(xc, g_mix[l]), modc[0], modc[1])
        qa, ka, va, qb, kb, vb, uc = jnp.split(h @ w_in[l], SPLIT_POINTS, axis=-1)
        qa_c, ka_c, va_c, qb_c, kb_c, vb_c, uc_c = jnp.split(hc @ w_in[l], SPLIT_POINTS, axis=-1)

        qa = apply_axial_rope(qa.reshape(B, S, HEADS_A, 2, HD_A), cos, sin)
        ka = apply_axial_rope(ka.reshape(B, S, HEADS_A, 2, HD_A), cos, sin)
        va = va.reshape(B, S, HEADS_A, VD_A)
        ka_c = ka_c.reshape(B, C, HEADS_A, 2, HD_A)
        va_c = va_c.reshape(B, C, HEADS_A, VD_A)
        qb = apply_axial_rope(qb.reshape(B, S, HEADS_B, HD_B), cos, sin)
        kb = apply_axial_rope(kb.reshape(B, S, KV_HEADS_B, HD_B), cos, sin)
        vb = vb.reshape(B, S, KV_HEADS_B, HD_B)
        kb_c = kb_c.reshape(B, C, KV_HEADS_B, HD_B)
        vb_c = vb_c.reshape(B, C, KV_HEADS_B, HD_B)

        lambda_init = 0.8 - 0.6 * math.exp(-0.3 * l)
        dl = diff_lambda[l].astype(jnp.float32)
        lam = jnp.exp(jnp.sum(dl[0] * dl[1])) - jnp.exp(jnp.sum(dl[2] * dl[3])) + lambda_init

        k_all = jnp.concatenate([ka_c, ka], axis=1)
        v_all = jnp.concatenate([va_c, va], axis=1)
        o_a = diff_head_norm(diff_attention_latent(qa, k_all, v_all, lam), diff_norm_g[l], lambda_init)
        o_b = window_sink_gqa_latent(qb, kb, vb, kb_c, vb_c, attn_sink[l])
        o_c = conv_module(uc, conv_w[l], conv_b[l], conv_ln_g[l], conv_ln_b[l])
        x = x + mod[:, 2, None] * (jnp.concatenate([o_a, o_b, o_c], axis=-1) @ w_out[l])

        if not last:
            o_ac = diff_head_norm(diff_softmax_attend(qa_c.reshape(B, C, HEADS_A, 2, HD_A), ka_c, va_c, lam),
                                  diff_norm_g[l], lambda_init)
            o_bc = sink_gqa_context(qb_c.reshape(B, C, HEADS_B, HD_B), kb_c, vb_c, attn_sink[l])
            o_cc = conv_module(uc_c, conv_w[l], conv_b[l], conv_ln_g[l], conv_ln_b[l])
            xc = xc + modc[2] * (jnp.concatenate([o_ac, o_bc, o_cc], axis=-1) @ w_out[l])

        h2 = modulate(rmsnorm(x, g_ffn[l]), mod[:, 3, None], mod[:, 4, None])
        if last:
            tokens = h2.reshape(B * S, D)
        else:
            h2c = modulate(rmsnorm(xc, g_ffn[l]), modc[3], modc[4])
            tokens = jnp.concatenate([h2.reshape(B * S, D), h2c.reshape(B * C, D)], axis=0)
        y = grouped_moe(tokens, router_w, router_bias, w1[l], w3[l], w2[l])
        x = x + mod[:, 5, None] * y[:B * S].reshape(B, S, D)
        if not last:
            xc = xc + modc[5] * y[B * S:].reshape(B, C, D)
    return rmsnorm(x, g_final)


_drawn_inputs = setup_inputs


def setup_inputs(seed=0):
    import zlib

    import numpy as np

    out = dict(_drawn_inputs(seed))
    spreads = {}
    factors = {'diff_lambda': 2.881,
     'attn_sink': 25.563,
     'conv_b': 6.345,
     'conv_ln_g': 3.389,
     'conv_ln_b': 8.0,
     'diff_norm_g': 3.422}
    for name, (base, spread) in spreads.items():
        noise = np.random.default_rng([zlib.crc32(name.encode()), seed]).standard_normal(out[name].shape)
        drawn = base * np.exp(spread * noise) if base else spread * noise
        out[name] = jnp.asarray(drawn.astype(out[name].dtype))
    for name, factor in factors.items():
        out[name] = (out[name] * factor).astype(out[name].dtype)
    return out
```

```python
import math
from contextlib import ExitStack

import concourse.bass as bass
import numpy as np
from concourse import mybir

P = 128
D = 1024
KD = D // P
S_LAT = 256
S_CTX = 256
TOK = S_LAT + S_CTX
TILES = TOK // P
DEPTH = 2
GRID_W = 64
HD = 64
BLK_A, BLK_B = 4, 2
BLK = BLK_A + BLK_B
VW = 512 + 128
CH = 256
KCONV = 31
PADC = KCONV // 2
E_N, E_G, E_F = 16, 4, 512
SLOT = 64
JMAX = TOK // SLOT
EPS = 1e-6
BIG = 1e30
NO_ROW = 1 << 20
WINDOW = 128
CHUNK = 512
ADA_N = 6 * D // CHUNK
IN_N = 5
OUT_N = D // CHUNK
UNITS = ADA_N + IN_N + OUT_N + 3 * E_N
RING = 6

C_ID, C_TRI, C_ONE = 0, 128, 256
C_ROPE = 384
C_MASK = C_ROPE + 2 * 128
C_I16 = C_MASK + 2 * 256
C_I4 = C_I16 + 16
C_TOK = C_I4 + 4
C_W = C_TOK + TILES


def routed(l):
    return TOK if l < DEPTH - 1 else S_LAT


def lambda_init(l):
    return 0.8 - 0.6 * math.exp(-0.3 * l)


def constants():
    c = np.zeros((P, C_W), np.float32)
    r = np.arange(P)
    c[:, C_ID:C_ID + P] = np.eye(P)
    c[:, C_TRI:C_TRI + P] = r[:, None] < r[None, :]
    c[:, C_ONE:C_ONE + P] = 1.0
    nf = HD // 4
    inv = (np.float32(10000.0) ** (-np.arange(nf, dtype=np.float32) / np.float32(nf))).astype(np.float32)
    for t in range(S_LAT // P):
        q = t * P + r
        pos = np.stack([q // GRID_W, q % GRID_W], -1).astype(np.float32)
        ang = pos[:, :, None] * inv
        cos, sin = np.cos(ang), np.sin(ang)
        c[:, C_ROPE + t * 128:C_ROPE + t * 128 + 64] = np.stack([cos, cos], 2).reshape(P, 64)
        c[:, C_ROPE + t * 128 + 64:C_ROPE + t * 128 + 128] = np.stack([-sin, sin], 2).reshape(P, 64)
        k = np.arange(S_LAT)
        c[:, C_MASK + t * 256:C_MASK + (t + 1) * 256] = np.where(np.abs(q[:, None] - k) <= WINDOW, 0.0, -BIG)
    c[:, C_I16:C_I16 + 16] = np.arange(16)
    c[:, C_I4:C_I4 + 4] = np.arange(4)
    c[:, C_TOK:C_TOK + TILES] = r[:, None] + P * np.arange(TILES)
    return c


def bank_plan():
    uses, plan, turn = [0] * 8, {}, {}

    def put(key, banks=range(8), bank=None):
        if bank is None:
            name = tuple(banks)
            bank = name[turn.get(name, 0) % len(name)]
            turn[name] = turn.get(name, 0) + 1
        plan[key] = (bank, uses[bank])
        uses[bank] += 1

    for key in ("c", "par", "cw"):
        put((key,))
    for l in range(DEPTH):
        nq = TILES if l == 0 else 2
        put(("ada", l, 0))
        put(("modc", l))
        for g in range(8):
            put(("nT", l, g))
        prev = None
        for job in in_jobs(l):
            put(("in", l) + job)
            if prev:
                put(("inT", l) + prev)
            prev = job if job[0] in ("ka", "b", "qa") else None
        if prev:
            put(("inT", l) + prev)
        put(("mu", l))
        put(("ada", l, 1))
        put(("var", l))
        put(("ada", l, 2))
        for step in attention_steps(l):
            if step[0] == "S":
                for m in range(2):
                    put(("S", l, step[1], m), bank=2 * (step[1] % 2) + m)
            elif step[0] == "T":
                put(("T", l, step[1]), (4, 5))
            elif step[0] == "O":
                put(("O", l, step[1]), (6, 7))
            else:
                put(("MA", l, step[1]), (4, 5))
                put(("MB", l, step[1]), (4, 5))
        for i in range(nq):
            for h in range(OUT_N):
                put(("wo", l, i, h))
            if i >= 1:
                for h in range(2):
                    put(("h2T", l, i - 1, h))
                put(("rt", l, i - 1))
        for h in range(2):
            put(("h2T", l, nq - 1, h))
        put(("rt", l, nq - 1))
        put(("rk", l))
    return plan, uses


def in_jobs(l):
    q_tiles = TILES if l == 0 else 2
    return ([("uc", f) for f in (2, 3, 0, 1)] + [("ka", t) for t in range(TILES)] + [("b", t) for t in range(TILES)]
            + [("va", t) for t in range(TILES)] + [("qa", t) for t in range(q_tiles)])


def units_of(l):
    return [(i, u) for i in range(TILES if l == 0 else 2) for u in range(BLK)]


def t_jobs(l):
    return [(n, m) for n, (_, u) in enumerate(units_of(l)) for m in range(1 if u < BLK_A else 2)]


def attention_steps(l):
    units, tj = units_of(l), t_jobs(l)
    out = [("S", 0)]
    for n in range(len(units)):
        if n + 1 < len(units):
            out.append(("S", n + 1))
        out += [("T", k) for k, (a, _) in enumerate(tj) if a == n]
        out += [("O", k) for k, (a, _) in enumerate(tj) if a == n - 1]
        if units[n][1] == 2 and units[n][0] > 0:
            out.append(("M", units[n][0] - 1))
    out += [("O", k) for k, (a, _) in enumerate(tj) if a == len(units) - 1]
    out.append(("M", units[-1][0]))
    return out


def hybrid_moe_kernel(nc, A):
    fp32, i32 = mybir.dt.float32, mybir.dt.int32
    ALU, ACT, AX = mybir.AluOpType, mybir.ActivationFunctionType, mybir.AxisListType
    PLAN, USES = bank_plan()
    ctx = ExitStack()
    with ctx:
        def sb(name, shape, dt=fp32):
            return ctx.enter_context(nc.sbuf_tensor(name, shape, dt))

        def sem(name):
            return ctx.enter_context(nc.semaphore(name))

        def sems(name, n):
            return [sem(f"{name}_{k}") for k in range(n)]

        ring = sb("ring", [P, RING, KD, CHUNK])
        X = sb("X", [P, TILES, D])
        HT = sb("HT", [P, KD, TOK])
        gate = sb("gate", [P, 2, D])
        cst = sb("cst", [P, C_W])
        SC = sb("SC", [P, KD, 32])
        PC = sb("PC", [P, DEPTH, 15])
        NC = sb("NC", [P, DEPTH, 5])
        CW = sb("CW", [P, 2, DEPTH * KCONV])
        rw = sb("rw", [P, KD, E_N])
        rb = sb("rb", [P, E_N])
        sink = sb("sink", [P, DEPTH, 4])
        lamx = sb("lamx", [P, DEPTH, 2])
        neglam = sb("neglam", [P, DEPTH])
        AB = sb("AB", [P, 2, 2, KD])
        MCOL = sb("MCOL", [P, 2, 2, KD])
        half = sb("half", [P, 1])
        ss = sb("ss", [P, TILES])
        ms = sb("ms", [P, TILES])
        rstd = sb("rstd", [P, TILES])
        mx = sb("mx", [P, 2, 2])
        nm = sb("nm", [P, 2, 2])
        sums = sb("sums", [P, 2, 2])
        es = sb("es", [P, 2, 2])
        rec = sb("rec", [P, 4, 2])
        cf = sb("cf", [P, 2])
        ss4 = sb("ss4", [P, 2, 4])
        ms4 = sb("ms4", [P, 2, 4])
        rs4 = sb("rs4", [P, 2, 4])
        AW = 2560 + 2 * 3072 + 1024 + 1144 + 1024 + 3840
        area = sb("area", [P, AW])
        at = [0]

        def cut(width, start=None):
            if start is not None:
                at[0] = start
            piece = area[:, at[0]:at[0] + width]
            at[0] += width
            assert at[0] <= AW, at[0]
            return piece

        V = cut(TILES * VW, 0).rearrange("p (t w) -> p t w", t=TILES)
        qT = cut(BLK * TOK).rearrange("p (b t) -> p b t", b=BLK)
        kT = cut(BLK * TOK).rearrange("p (b t) -> p b t", b=BLK)
        G = cut(2 * TOK).rearrange("p (c t) -> p c t", c=2)
        ZP_AT = at[0]
        zpad = cut(2 * 2 * (S_LAT + 2 * PADC)).rearrange("p (c s t) -> p c s t", c=2, s=2)
        acc = cut(2 * TOK).rearrange("p (c t) -> p c t", c=2)
        S1 = at[0]
        PB = cut(2048, S1).rearrange("p (b m k) -> p b m k", b=2, m=2)
        aT = cut(1024).rearrange("p (b k) -> p b k", b=2)
        O = [cut(BLK * P), area[:, ZP_AT:ZP_AT + BLK * P]]
        RT = cut(1024, S1).rearrange("p (b k) -> p b k", b=2)
        ST = cut(1024).rearrange("p (b k) -> p b k", b=2)
        bias12 = cut(1024).rearrange("p (b k) -> p b k", b=2)
        mst = cut(512)
        YS = cut(TILES * D, 0).rearrange("p (t d) -> p t d", t=TILES)
        bias0 = cut(512)
        mst0 = cut(512)
        PR = cut(128)
        CR = cut(128)
        CRS = cut(128)
        CWR = cut(256)
        DL = cut(DEPTH * 4 * HD).rearrange("p (l a d) -> p l a d", l=DEPTH, a=4)
        DLP = cut(DEPTH * 2 * HD).rearrange("p (l a d) -> p l a d", l=DEPTH, a=2)
        MR = cut(128)
        SI = cut(512).bitcast(i32)
        BC = cut(2 * 2 * D, 0).rearrange("p (c v d) -> p c v d", c=2, v=2)
        GF = cut(D)
        H2 = cut(TILES * D).rearrange("p (t d) -> p t d", t=TILES)
        hTr = cut(KD * P).rearrange("p (k t) -> p k t", k=KD)
        tmp = cut(2 * CHUNK).rearrange("p (b k) -> p b k", b=2)
        R_AT = at[0]
        RW = 64

        def rt_tile(width):
            return cut(width)

        e_s, e_b, e_v, e_t, e_eq = (rt_tile(RW).rearrange("p (t e) -> p t e", e=E_N) for _ in range(5))
        oh = [rt_tile(RW).rearrange("p (t e) -> p t e", e=E_N) for _ in range(2)]
        MM = rt_tile(RW).rearrange("p (t e) -> p t e", e=E_N)
        hl = rt_tile(4 * 16).rearrange("p (a g) -> p a g", a=4)
        grp, geq, gcd, gone, gneg = (rt_tile(16).rearrange("p (t g) -> p t g", g=E_G) for _ in range(5))
        gm, cm, vm, cmk0, cmk1, w0, w1k, wsum = (rt_tile(TILES) for _ in range(8))
        rkf = rt_tile(2 * TILES).rearrange("p (k t) -> p k t", k=2)
        rowf = rt_tile(2 * TILES).rearrange("p (k t) -> p k t", k=2)
        rki = rt_tile(2 * TILES).bitcast(i32).rearrange("p (k t) -> p k t", k=2)
        ji = rt_tile(2 * TILES).bitcast(i32).rearrange("p (k t) -> p k t", k=2)
        pi = rt_tile(2 * TILES).bitcast(i32).rearrange("p (k t) -> p k t", k=2)
        ROWI = rt_tile(2 * TILES).bitcast(i32).rearrange("p (k t) -> p k t", k=2)
        PLf = rt_tile(2 * TILES * 4).rearrange("p (k t w) -> p k t w", k=2, w=4)
        PLi = PLf.bitcast(i32)
        nbi = rt_tile(E_N).bitcast(i32)
        nb = rt_tile(E_N).bitcast(i32)
        TBf = cut(E_N * JMAX * 4)
        TBi = TBf.bitcast(i32)
        DR = cut(4).bitcast(i32)
        gidx = cut(1).bitcast(i32)
        sidx = cut(1).bitcast(i32)
        xg = cut(D)
        YM_AT = at[0]
        xT = cut(KD * SLOT, 0).rearrange("p (k s) -> p k s", k=KD)
        sg = cut(E_F)
        gg = cut(E_F)
        gT = cut(4 * SLOT).rearrange("p (k s) -> p k s", k=4)
        ym = cut(D)
        Y = cut(2 * TILES * D // 2, 0).rearrange("p (k b d) -> p k b d", k=2, b=2)
        GFIN = cut(D, 4096)

        ps = ctx.enter_context(nc.psum_tensor("ps", [P, 8, CHUNK], fp32))
        B_XT, B_GT, B_W13, B_W2 = 0, 1, 2, 3

        modD = nc.dram_tensor("mod_rows", [DEPTH, 2, 6 * D], fp32).ap()
        h2D = [nc.dram_tensor(f"h2_rows_{l}", [routed(l), D], fp32).ap() for l in range(DEPTH)]
        yD = [nc.dram_tensor(f"expert_rows_{l}", [2 * routed(l), D], fp32).ap() for l in range(DEPTH)]
        slotD = [nc.dram_tensor(f"slot_rows_{l}", [SLOT * E_N * JMAX, 4], i32).ap() for l in range(DEPTH)]

        full = sems("bank_full", 8)
        evict = sems("bank_evicted", 8)
        ring_full = sems("ring_full", RING)
        ring_free = sems("ring_free", RING)
        cst_in = sem("constants_in")
        par_in = sem("parameters_in")
        x_in = sem("x_in")
        c_silu = sem("c_silu")
        setup = sem("setup_done")
        si_out = sem("slot_tables_cleared")
        lam_sum = sem("lambda_sums")
        lam_exp = sem("lambda_exps")
        phase = sem("phase")
        bias_in = sems("bias_in", DEPTH)
        mod_sb = sems("mod_rows_made", DEPTH)
        mod_out = [sems(f"mod_rows_stored_{l}", 3) for l in range(DEPTH)]
        mrow_in = sems("mod_columns_in", DEPTH)
        ss_done = sems("squares_summed", DEPTH)
        rs_done = sems("rstd_made", DEPTH)
        y_done = sems("normed", DEPTH)
        ab_done = sems("columns_made", DEPTH)
        pads = sems("pads_zero", DEPTH)
        g_exp = sems("conv_gate_exp", DEPTH)
        cv_d = sems("conv_done", DEPTH)
        ln_d = sems("ln_centred", DEPTH)
        ln_sq = sems("ln_squares", DEPTH)
        ln_v = sems("ln_variance", DEPTH)
        ln_r = sems("ln_rstd", DEPTH)
        ln_n = sems("ln_normed", DEPTH)
        ln_e = sems("ln_exp", DEPTH)
        nm_done = sems("negmax", DEPTH)
        ex_done = sems("exps_b", DEPTH)
        pr_done = sems("probs", DEPTH)
        o_ss = sems("head_squares", DEPTH)
        o_rs = sems("head_rstd", DEPTH)
        o_done = sems("heads_normed", DEPTH)
        gate_in = sems("gate_in", DEPTH)
        bc_in = sems("ffn_rows_in", DEPTH)
        bc_done = sems("ffn_scale_made", DEPTH)
        x_add = sems("residual_added", DEPTH)
        ss2 = sems("squares2", DEPTH)
        rs2 = sems("rstd2", DEPTH)
        h2_done = sems("h2_made", DEPTH)
        h2_out = sems("h2_stored", DEPTH)
        m_done = sems("choices_made", DEPTH)
        pl_done = sems("slots_made", DEPTH)
        slot_out = sems("slots_scattered", DEPTH)
        tb_in = sems("slot_table_in", DEPTH)
        nb_ready = sems("counts_ready", DEPTH)
        init_m = sems("expert_buffers_filled", DEPTH)
        gath = sems("tokens_gathered", DEPTH)
        xt_full = sems("xT_product", DEPTH)
        xt_rdy = sems("xT_copied", DEPTH)
        gt_full = sems("gT_product", DEPTH)
        gt_rdy = sems("gT_copied", DEPTH)
        w13_full = sems("w13_product", DEPTH)
        si_rdy = sems("silu_made", DEPTH)
        g_rdy = sems("hidden_made", DEPTH)
        w2_full = sems("w2_product", DEPTH)
        y_rdy = sems("y_copied", DEPTH)
        scat = sems("y_scattered", DEPTH)
        y_in = sems("y_in", DEPTH)
        comb = sems("y_added", DEPTH)
        pe_passed = sem("pe_waits_passed")
        pool_passed = sem("pool_waits_passed")
        fin_ss = sem("final_squares")
        fin_rs = sem("final_rstd")
        fin_g = sem("final_gain_in")
        fin_o = sem("final_made")
        stored = sem("output_stored")

        def bank(key):
            return ps[:, PLAN[key][0], :]

        def claim(pe, key):
            b, u = PLAN[key]
            if u:
                pe.wait_ge(evict[b], u)

        def made(ins, key):
            ins.then_inc(full[PLAN[key][0]], 1)

        def wait_made(e, key):
            b, u = PLAN[key]
            e.wait_ge(full[b], u + 1)

        def taken(ins, key):
            ins.then_inc(evict[PLAN[key][0]], 1)

        def wait_taken(e, key):
            b, u = PLAN[key]
            e.wait_ge(evict[b], u + 1)

        def barrier(e, n):
            e.drain().then_inc(phase, 1)
            e.wait_ge(phase, 4 * n)

        def hold(e, semaphore, value, passed):
            e.wait_ge(semaphore, value)
            e.sem_inc(passed, 1)

        def bar(l, k):
            return 6 * l + k

        ident = cst[:, C_ID:C_ID + P]
        tri = cst[:, C_TRI:C_TRI + P]
        ones = cst[:, C_ONE:C_ONE + P]

        U_ADA = [0, 1, 2, 3] + [4 + IN_N + k for k in range(8)]
        U_IN = {"uc": 4, "ka": 5, "b": 6, "va": 7, "qa": 8}
        IN_COL = {"qa": 0, "ka": 1, "va": 2, "b": 3, "uc": 4}
        U_OUT = 4 + IN_N + 8
        U_MOE = U_OUT + OUT_N

        def slot(l, n):
            return (UNITS * l + n) % RING

        def use(l, n):
            return (UNITS * l + n) // RING

        def arrived(e, l, n):
            e.wait_ge(ring_full[slot(l, n)], 16 * (use(l, n) + 1))

        w_ada_v = A["w_ada"].rearrange("l (k p) n -> l p k n", p=P)
        w_in_v = A["w_in"].rearrange("l (k p) n -> l p k n", p=P)
        w_out_v = A["w_out"].rearrange("l (k p) n -> l p k n", p=P)
        w13_v = [A[w].rearrange("l e (k p) n -> l e p k n", p=P) for w in ("w1", "w3")]
        w2_v = A["w2"].rearrange("l e (k p) n -> l e p k n", p=P)

        block = ctx.enter_context(nc.Block())

        @block.sync
        def _(sp):
            def load(l, n, src):
                if use(l, n):
                    sp.wait_ge(ring_free[slot(l, n)], use(l, n))
                sp.dma_start(ring[:, slot(l, n)], src).then_inc(ring_full[slot(l, n)], 16)

            for l in range(DEPTH):
                order = sorted([(U_ADA[j], w_ada_v[l, :, :, j * CHUNK:(j + 1) * CHUNK]) for j in range(ADA_N)]
                               + [(U_IN[s], w_in_v[l, :, :, IN_COL[s] * CHUNK:(IN_COL[s] + 1) * CHUNK]) for s in U_IN]
                               + [(U_OUT + h, w_out_v[l, :, :, h * CHUNK:(h + 1) * CHUNK]) for h in range(OUT_N)],
                               key=lambda x: x[0])
                for n, src in order:
                    load(l, n, src)
                with sp.Fori(0, E_N // 2) as i:
                    for q in range(2):
                        e = 2 * i + q
                        for w in range(3):
                            n = U_MOE + 3 * q + w
                            sp.wait_ge(ring_free[slot(l, n)], i + use(l, n))
                            dst = ring[:, slot(l, n)]
                            if w < 2:
                                src = w13_v[w][l, bass.ds(e, 1)].squeeze(0)
                            else:
                                src = w2_v[l, bass.ds(e, 1)].squeeze(0)
                                dst = dst.rearrange("p k n -> p (k n)").rearrange("p (k n) -> p k n", k=4)
                            sp.dma_start(dst, src).then_inc(ring_full[slot(l, n)], 16)

        @block.gpsimd
        def _(pool):
            g = nc.gpsimd
            g.memset(half[:], -0.5)
            g.memset(SC[:], 0.0)
            sv = SI.rearrange("p (r w) -> p r w", w=4)
            g.memset(sv, 0)
            pool.drain()
            g.memset(sv[:, :, 1:2], NO_ROW)
            pool.drain().then_inc(setup, 1)
            pool.wait_ge(setup, 1)
            for l in range(DEPTH):
                pool.dma_start(slotD[l].rearrange("(p r) w -> p (r w)", p=SLOT), SI[0:SLOT, :]).then_inc(si_out, 16)

            def rsqrt(out, s_, m_, n):
                g.tensor_scalar(m_, s_, 1.0 / n, EPS, ALU.mult, ALU.add)
                pool.drain()
                return g.tensor_tensor(out, m_, half[:].to_broadcast(list(out.shape)), ALU.pow)

            for l in range(DEPTH):
                nq = TILES if l == 0 else 2
                conds = 2 if l == 0 else 1

                def load_bias(dst, q):
                    for j in range(4):
                        col = (4 * q + j) * CHUNK
                        pool.dma_start(dst[32 * j:32 * j + 32, :],
                                       A["b_ada"][l:l + 1, col:col + CHUNK].broadcast_to([32, CHUNK])).then_inc(bias_in[l], 16)

                def store_mod(src, q):
                    pool.wait_ge(mod_sb[l], q + 1)
                    for j in range(4):
                        col = (4 * q + j) * CHUNK
                        pool.dma_start(modD[l, :, col:col + CHUNK], src[32 * j:32 * j + 2, :]).then_inc(mod_out[l][q], 16)

                load_bias(bias0, 0)
                pool.wait_ge(ss_done[l], 1)
                rsqrt(rstd[:, 0:TILES], ss[:], ms[:], D).then_inc(rs_done[l], 1)
                store_mod(mst0, 0)
                pool.wait_ge(mod_out[l][0], 64)
                for cnd in range(2):
                    pool.dma_start(MR[16 * cnd:16 * cnd + 16, :],
                                   modD[l, cnd, 0:2 * D].rearrange("(r n) -> r n", n=P)).then_inc(mrow_in[l], 16)
                if l == 0:
                    pool.wait_ge(si_out, 32)
                barrier(pool, bar(l, 1))
                g.memset(zpad[:, :, :, 0:PADC], 0.0)
                g.memset(zpad[:, :, :, PADC + S_LAT:], 0.0).then_inc(pads[l], 1)
                load_bias(bias12[:, 0], 1)
                load_bias(bias12[:, 1], 2)
                store_mod(mst, 1)
                pool.wait_ge(ln_v[l], 1)
                n_ln = TOK if l == 0 else S_LAT
                g.tensor_tensor(G[:, 1, 0:n_ln], G[:, 0, 0:n_ln], half[:].to_broadcast([P, n_ln]), ALU.pow).then_inc(ln_r[l], 1)
                store_mod(mst, 2)
                for q in (1, 2):
                    pool.wait_ge(mod_out[l][q], 64)
                barrier(pool, bar(l, 2))
                for cnd in range(conds):
                    pool.dma_start(gate[:, cnd], modD[l, cnd:cnd + 1, 2 * D:3 * D].broadcast_to([P, D])).then_inc(gate_in[l], 16)
                for i in range(nq):
                    pool.wait_ge(o_ss[l], i + 1)
                    rsqrt(rs4[:, i % 2], ss4[:, i % 2], ms4[:, i % 2], 2 * HD).then_inc(o_rs[l], 1)
                barrier(pool, bar(l, 3))
                for cnd in range(conds):
                    for v in range(2):
                        pool.dma_start(BC[:, cnd, v], modD[l, cnd:cnd + 1, (3 + v) * D:(4 + v) * D].broadcast_to([P, D])).then_inc(bc_in[l], 16)
                pool.dma_start(GF, A["g_ffn"][l:l + 1, :].broadcast_to([P, D])).then_inc(bc_in[l], 16)
                for i in range(nq):
                    pool.wait_ge(ss2[l], i + 1)
                    rsqrt(rstd[:, i:i + 1], ss[:, i:i + 1], ms[:, i:i + 1], D).then_inc(rs2[l], 1)
                pool.wait_ge(pl_done[l], 1)
                for k in range(2):
                    for i in range(nq):
                        pool.indirect_dma_start(slotD[l], bass.IndirectOffsetOnAxis(ap=ROWI[:, k, i:i + 1], axis=0),
                                                PLi[:, k, i, :], None).then_inc(slot_out[l], 16)
                pool.wait_ge(slot_out[l], 16 * 2 * nq)
                pool.dma_start(TBi[0:SLOT, :], slotD[l].rearrange("(p r) w -> p (r w)", p=SLOT)).then_inc(tb_in[l], 16)
                barrier(pool, bar(l, 4))
                for cnd in range(conds):
                    pool.dma_start(gate[:, cnd], modD[l, cnd:cnd + 1, 5 * D:6 * D].broadcast_to([P, D])).then_inc(gate_in[l], 16)
                g.memset(DR[0:SLOT, :], NO_ROW)
                g.memset(ym[0:SLOT, :], 0.0)
                pool.drain().then_inc(init_m[l], 1)
                pool.wait_ge(tb_in[l], 16)
                pool.wait_ge(h2_out[l], 16 * nq)
                done = pool.alloc_register(f"pool_blocks_{l}")
                pool.reg_mov(done, 0)

                def scatter(b):
                    g.tensor_copy(sidx[0:SLOT, :], DR[0:SLOT, bass.ds((b + 2) % 4, 1)])
                    pool.drain()
                    pool.indirect_dma_start(yD[l], bass.IndirectOffsetOnAxis(ap=sidx[0:SLOT, :], axis=0), ym[0:SLOT, :], None,
                                            bounds_check=2 * routed(l) - 1, oob_is_err=False).then_inc(scat[l], 16)

                def step(col):
                    b = pool.snap(done)
                    hold(pool, xt_full[l], b + 1, pool_passed)
                    pool.reg_add(done, done, 1)
                    g.tensor_copy(gidx[0:SLOT, :], TBi[0:SLOT, bass.ds(4 * col, 1)])
                    g.tensor_copy(DR[0:SLOT, bass.ds(b % 4, 1)], TBi[0:SLOT, bass.ds(4 * col + 1, 1)])
                    pool.drain()
                    pool.indirect_dma_start(xg[0:SLOT, :], None, h2D[l], bass.IndirectOffsetOnAxis(ap=gidx[0:SLOT, :], axis=0)).then_inc(gath[l], 16)
                    hold(pool, y_rdy[l], b + 1, pool_passed)
                    scatter(b)

                with pool.Fori(0, E_N) as e:
                    blocks = pool.value_load(nb[0:1, bass.ds(e, 1)], min_val=0, max_val=JMAX)
                    step(e * JMAX)
                    with pool.If(blocks > 1):
                        with pool.Fori(1, blocks) as j:
                            step(e * JMAX + j)
                b = pool.snap(done)
                hold(pool, y_rdy[l], b + 1, pool_passed)
                scatter(b)
                hold(pool, y_rdy[l], b + 2, pool_passed)
                scatter(b + 1)
                hold(pool, scat[l], 16 * b + 32, pool_passed)
                barrier(pool, bar(l, 5))
                y_v = yD[l].rearrange("(k t p) d -> p k t d", k=2, p=P)
                for a in range(nq // 2):
                    if a:
                        pool.wait_ge(comb[l], 2 * a)
                    for k in range(2):
                        for c2 in range(2):
                            pool.dma_start(Y[:, k, c2], y_v[:, k, 2 * a + c2]).then_inc(y_in[l], 16)
                if l == DEPTH - 1:
                    pool.dma_start(GFIN, A["g_final"].rearrange("(a n) -> a n", a=1).broadcast_to([P, D])).then_inc(fin_g, 16)
                    pool.wait_ge(fin_ss, 1)
                    rsqrt(rstd[:, 0:2], ss[:, 0:2], ms[:, 0:2], D).then_inc(fin_rs, 1)
                barrier(pool, bar(l, 6))

        @block.scalar
        def _(act):
            s = nc.scalar
            act.dma_start(cst[:], A["cst"]).then_inc(cst_in, 16)
            small = 0

            def par(dst, src):
                act.dma_start(dst, src).then_inc(par_in, 16)

            par(CR[0:8, :], A["c"].rearrange("b (r n) -> (b r) n", n=P))
            par(CR[8:16, :], A["c_ctx"].rearrange("(r n) -> r n", n=P))
            for l in range(DEPTH):
                r0 = 15 * l
                for at_, name, rows in ((0, "g_mix", 8), (8, "diff_norm_g", 1), (9, "conv_b", 2), (11, "conv_ln_g", 2), (13, "conv_ln_b", 2)):
                    par(PR[r0 + at_:r0 + at_ + rows, :], A[name][l].rearrange("(r n) -> r n", n=P))
            par(CWR[0:DEPTH * KCONV, :], A["conv_w"].rearrange("l k c -> (l k) c"))
            par(DL.rearrange("p l a d -> p (l a d)"),
                A["diff_lambda"].rearrange("l a d -> (l a d)").rearrange("(o n) -> o n", o=1).broadcast_to([P, DEPTH * 4 * HD]))
            par(rw[:], A["router_w"].rearrange("(k p) e -> p k e", p=P))
            par(rb[:], A["router_bias"].rearrange("(o n) -> o n", o=1).broadcast_to([P, E_N]))
            par(sink[:].rearrange("p l h -> p (l h)"), A["attn_sink"].rearrange("l h -> (l h)").rearrange("(o n) -> o n", o=1).broadcast_to([P, DEPTH * 4]))
            act.dma_start(X[:, 0:2], A["x"].rearrange("b (t p) d -> p (b t) d", p=P)).then_inc(x_in, 16)
            act.dma_start(X[:, 2:4], A["ctx"].rearrange("b (t p) d -> p (b t) d", p=P)).then_inc(x_in, 16)
            act.wait_ge(par_in, 16 * N_PAR)
            s.activation(CRS[0:16, :], CR[0:16, :], ACT.Silu).then_inc(c_silu, 1)
            act.wait_ge(lam_sum, 1)
            s.activation(lamx[:], lamx[:], ACT.Exp).then_inc(lam_exp, 1)

            for l in range(DEPTH):
                nq = TILES if l == 0 else 2
                n_ln = TOK if l == 0 else S_LAT
                if l == 0:
                    act.wait_ge(x_in, 32)
                for t in range(TILES):
                    last = s.activation(YS[:, t], X[:, t], ACT.Square, accum_out=ss[:, t:t + 1])
                last.then_inc(ss_done[l], 1)
                act.wait_ge(ab_done[l], 1)
                for q in range(1, 8, 2):
                    key = ("nT", l, q)
                    wait_made(act, key)
                    cnd, kk = q // 4, 2 * (q % 4)
                    for a in range(2):
                        last = s.activation(HT[:, kk + a, cnd * 256:cnd * 256 + 256], bank(key)[:, a * 256:a * 256 + 256], ACT.Identity,
                                            bias=AB[:, cnd, 0, kk + a:kk + a + 1], scale=AB[:, cnd, 1, kk + a:kk + a + 1])
                    taken(last, key)
                barrier(act, bar(l, 1))

                staged = [j for j in in_jobs(l) if j[0] in ("ka", "b", "qa")]

                def st_free(job):
                    k = staged.index(job)
                    if k >= 2:
                        wait_made(act, ("inT", l) + staged[k - 2])

                def copy_T(job):
                    seg, t = job
                    key = ("inT", l) + job
                    wait_made(act, key)
                    src = bank(key).rearrange("p (b t) -> p b t", b=4)
                    cols = slice(t * P, (t + 1) * P)
                    if seg == "b":
                        if t < 2 or l == 0:
                            s.activation(qT[:, 4:6, cols], src[:, 0:2], ACT.Identity)
                        last = s.activation(kT[:, 4:6, cols], src[:, 2:4], ACT.Identity)
                    else:
                        last = s.activation((qT if seg == "qa" else kT)[:, 0:4, cols], src, ACT.Identity)
                    taken(last, key)

                prev = None
                for job in in_jobs(l):
                    seg, t = job
                    key = ("in", l) + job
                    stg = ST[:, staged.index(job) % 2] if job in staged else None
                    if seg == "uc" and t >= 2:
                        wait_made(act, key)
                        taken(s.activation(G[:, t - 2, 0:n_ln], bank(key)[:, 0:n_ln], ACT.Exp, scale=-1.0), key)
                        if t == 3:
                            act.drain().then_inc(g_exp[l], 1)
                    elif seg == "va":
                        wait_made(act, key)
                        taken(s.activation(V[:, t, 0:512], bank(key), ACT.Identity), key)
                    elif seg in ("ka", "qa") and t >= 2:
                        wait_made(act, key)
                        st_free(job)
                        taken(s.activation(stg, bank(key), ACT.Identity), key)
                    elif seg == "b" and t >= 2:
                        wait_made(act, key)
                        st_free(job)
                        if l == 0:
                            s.activation(stg[:, 0:256], bank(key)[:, 0:256], ACT.Identity)
                        for a in range(2):
                            s.activation(stg[:, 256 + a * 64:].rearrange("p (j d) -> p j d", d=64)[:, 0::2],
                                         bank(key)[:, 256:384].rearrange("p (j d) -> p j d", d=64), ACT.Identity)
                        taken(s.activation(V[:, t, 512:640], bank(key)[:, 384:512], ACT.Identity), key)
                    if prev:
                        copy_T(prev)
                    prev = job if job in staged else None
                if prev:
                    copy_T(prev)
                act.wait_ge(ln_d[l], 1)
                s.activation(G[:, :, 0:n_ln], acc[:, :, 0:n_ln], ACT.Square).then_inc(ln_sq[l], 1)
                act.wait_ge(ln_n[l], 1)
                for c2 in range(2):
                    last = s.activation(G[:, c2, 0:n_ln], acc[:, c2, 0:n_ln], ACT.Exp, bias=NC[:, l, 2 + c2:3 + c2], scale=NC[:, l, c2:c2 + 1])
                last.then_inc(ln_e[l], 1)
                barrier(act, bar(l, 2))

                units, tj = units_of(l), t_jobs(l)

                def exps(n):
                    i, u = units[n]
                    kw = TOK if i < 2 else S_CTX
                    b = n % 2
                    act.wait_ge(nm_done[l], n + 1)
                    if u < BLK_A:
                        prior = [k for k, (a, _) in enumerate(tj) if a == n - 2]
                        if prior:
                            wait_made(act, ("T", l, prior[-1]))
                        for m in range(2):
                            key = ("S", l, n, m)
                            taken(s.activation(PB[:, b, m, 0:kw], bank(key)[:, 0:kw], ACT.Exp, bias=nm[:, b, m:m + 1], scale=HD ** -0.5,
                                               accum_out=sums[:, b, m:m + 1]), key)
                    else:
                        for m in range(2):
                            h = 2 * (u - BLK_A) + m
                            s.activation(es[:, b, m:m + 1], sink[:, l, h:h + 1], ACT.Exp, bias=nm[:, b, m:m + 1])
                            last = s.activation(PB[:, b, m, 0:kw], PB[:, b, m, 0:kw], ACT.Exp, bias=nm[:, b, m:m + 1],
                                                accum_out=sums[:, b, m:m + 1])
                        last.then_inc(ex_done[l], 1)

                def copy_aT(k):
                    n, m = tj[k]
                    kw = TOK if units[n][0] < 2 else S_CTX
                    key = ("T", l, k)
                    wait_made(act, key)
                    if k >= 2:
                        wait_made(act, ("O", l, k - 2))
                    taken(s.activation(aT[:, k % 2, 0:kw], bank(key)[:, 0:kw], ACT.Identity), key)

                def mixed(i):
                    cols = slice(i * P, (i + 1) * P)
                    wait_made(act, ("MA", l, i))
                    taken(s.activation(HT[:, 0:4, cols], bank(("MA", l, i)).rearrange("p (b t) -> p b t", b=4), ACT.Identity,
                                       scale=NC[:, l, 4:5]), ("MA", l, i))
                    wait_made(act, ("MB", l, i))
                    taken(s.activation(HT[:, 4:6, cols], bank(("MB", l, i))[:, 0:256].rearrange("p (b t) -> p b t", b=2), ACT.Identity), ("MB", l, i))

                for step in attention_steps(l):
                    if step[0] == "S":
                        exps(step[1])
                    elif step[0] == "T":
                        copy_aT(step[1])
                    elif step[0] == "M":
                        mixed(step[1])
                barrier(act, bar(l, 3))

                def second(i):
                    act.wait_ge(x_add[l], i + 1)
                    s.activation(H2[:, i], X[:, i], ACT.Square, accum_out=ss[:, i:i + 1]).then_inc(ss2[l], 1)

                def route(i):
                    act.wait_ge(h2_done[l], i + 1)
                    act.dma_start(h2D[l].rearrange("(t p) d -> t p d", p=P)[i], H2[:, i]).then_inc(h2_out[l], 16)
                    for h in range(2):
                        key = ("h2T", l, i, h)
                        wait_made(act, key)
                        if i:
                            wait_made(act, ("rt", l, i - 1))
                        taken(s.activation(hTr[:, 4 * h:4 * h + 4], bank(key).rearrange("p (b t) -> p b t", b=4), ACT.Identity), key)
                    key = ("rt", l, i)
                    wait_made(act, key)
                    taken(s.activation(e_t[:, i], bank(key)[:, 0:E_N], ACT.Exp, scale=-1.0), key)

                for i in range(nq):
                    second(i)
                    if i:
                        route(i - 1)
                route(nq - 1)
                act.drain().then_inc(h2_done[l], 1)
                barrier(act, bar(l, 4))

                act.wait_ge(nb_ready[l], 1)
                done = act.alloc_register(f"act_blocks_{l}")
                act.reg_mov(done, 0)

                def step():
                    b = act.snap(done)
                    act.wait_ge(xt_full[l], b + 2)
                    s.activation(xT.rearrange("p k s -> p (k s)"), ps[:, B_XT, :], ACT.Identity).then_inc(xt_rdy[l], 1)
                    act.wait_ge(w13_full[l], b + 1)
                    s.activation(sg[0:SLOT, :], ps[0:SLOT, B_W13, :], ACT.Silu).then_inc(si_rdy[l], 1)
                    act.reg_add(done, done, 1)

                with act.Fori(0, E_N) as e:
                    blocks = act.value_load(nb[0:1, bass.ds(e, 1)], min_val=0, max_val=JMAX)
                    step()
                    with act.If(blocks > 1):
                        with act.Fori(1, blocks):
                            step()
                barrier(act, bar(l, 5))
                if l == DEPTH - 1:
                    for i in range(2):
                        act.wait_ge(comb[l], i + 1)
                        last = s.activation(area[:, 8192 + i * D:8192 + (i + 1) * D], X[:, i], ACT.Square, accum_out=ss[:, i:i + 1])
                    last.then_inc(fin_ss, 1)
                    for i in range(2):
                        act.wait_ge(fin_o, i + 1)
                        act.dma_start(A["out"].rearrange("b (t p) d -> p (b t) d", p=P)[:, i], X[:, i]).then_inc(stored, 16)
                    act.wait_ge(stored, 32)
                barrier(act, bar(l, 6))

        @block.vector
        def _(dve):
            v = nc.vector
            for key, dst, cols in (("par", PC[:].rearrange("p l a -> p (l a)"), DEPTH * 15), ("cw", None, 0), ("c", None, 0)):
                wait_made(dve, (key,))
                if key == "par":
                    taken(v.tensor_copy(dst, bank((key,))[:, 0:cols]), (key,))
                elif key == "cw":
                    taken(v.tensor_copy(CW[:].rearrange("p c k -> p (c k)"), bank((key,))[:, 0:2 * DEPTH * KCONV]), (key,))
                else:
                    dve.wait_ge(setup, 1)
                    taken(v.tensor_copy(SC[:, :, 0:2], bank((key,))[:, 0:16].rearrange("p (c k) -> p k c", c=2)), (key,))
            dve.drain()
            for l in range(DEPTH):
                v.tensor_scalar(NC[:, l, 0:4], PC[:, l, 11:15], -1.0, None, ALU.mult)
                v.tensor_scalar(NC[:, l, 4:5], PC[:, l, 8:9], 1.0 - lambda_init(l), None, ALU.mult)
            dve.wait_ge(par_in, 16 * N_PAR)
            v.tensor_tensor(DLP, DL[:, :, 0::2], DL[:, :, 1::2], ALU.mult)
            dve.drain()
            v.tensor_reduce(lamx[:], DLP, AX.X, ALU.add).then_inc(lam_sum, 1)
            dve.wait_ge(lam_exp, 1)
            for l in range(DEPTH):
                v.scalar_tensor_tensor(neglam[:, l:l + 1], lamx[:, l, 1:2], -lambda_init(l), lamx[:, l, 0:1], ALU.add, ALU.subtract)
            dve.drain()

            for l in range(DEPTH):
                nq = TILES if l == 0 else 2
                conds = nq // 2
                n_ln = TOK if l == 0 else S_LAT
                n_seq = conds

                def mod_rows(q, bias, dst):
                    key = ("ada", l, q)
                    wait_made(dve, key)
                    dve.wait_ge(bias_in[l], 64 * (1 if q == 0 else 3))
                    if q == 2:
                        dve.wait_ge(mod_out[l][1], 64)
                    taken(v.tensor_tensor(dst, bank(key), bias, ALU.add), key)
                    dve.drain().then_inc(mod_sb[l], 1)

                dve.wait_ge(rs_done[l], 1)
                for t in range(TILES):
                    last = v.tensor_scalar(YS[:, t], X[:, t], rstd[:, t:t + 1], None, ALU.mult)
                last.then_inc(y_done[l], 1)
                mod_rows(0, bias0, mst0)
                key = ("modc", l)
                wait_made(dve, key)
                taken(v.tensor_copy(MCOL[:].rearrange("p c v k -> p (c v k)"), bank(key)[:, 0:32]), key)
                dve.drain()
                v.tensor_copy(AB[:, :, 0], MCOL[:, :, 0])
                v.scalar_tensor_tensor(AB[:, :, 1], MCOL[:, :, 1], 1.0, PC[:, l, 0:8].unsqueeze(1).to_broadcast([P, 2, KD]), ALU.add, ALU.mult)
                dve.drain().then_inc(ab_done[l], 1)
                for q in range(0, 8, 2):
                    key = ("nT", l, q)
                    wait_made(dve, key)
                    cnd, kk = q // 4, 2 * (q % 4)
                    for a in range(2):
                        last = v.tensor_scalar(HT[:, kk + a, cnd * 256:cnd * 256 + 256], bank(key)[:, a * 256:a * 256 + 256],
                                               AB[:, cnd, 1, kk + a:kk + a + 1], AB[:, cnd, 0, kk + a:kk + a + 1], ALU.mult, ALU.add)
                    taken(last, key)
                barrier(dve, bar(l, 1))

                staged = [j for j in in_jobs(l) if j[0] in ("ka", "b", "qa")]

                def conv_taps():
                    for k in range(KCONV):
                        for c2 in range(2):
                            src = zpad[:, c2, 0:n_seq, k:k + S_LAT]
                            dst = acc[:, c2, 0:n_ln].rearrange("p (s t) -> p s t", s=n_seq)
                            w = CW[:, c2, l * KCONV + k:l * KCONV + k + 1]
                            if k == 0:
                                v.tensor_scalar(dst, src, w, PC[:, l, 9 + c2:10 + c2], ALU.mult, ALU.add)
                            else:
                                v.scalar_tensor_tensor(dst, src, w, dst, ALU.mult, ALU.add)
                            if c2 == 1:
                                dve.drain()
                            yield

                taps = conv_taps()

                def conv(n):
                    for _ in range(n):
                        next(taps, None)

                def rope(job, n_heads, outs):
                    key = ("in", l) + job
                    t = job[1]
                    w = n_heads * HD
                    cosv = cst[:, C_ROPE + t * 128:C_ROPE + t * 128 + 64].unsqueeze(1).to_broadcast([P, n_heads, 64])
                    x_ = bank(key)[:, 0:w]
                    v.tensor_tensor(RT[:, 0, 0:w].rearrange("p (h d) -> p h d", d=64), x_.rearrange("p (h d) -> p h d", d=64), cosv, ALU.mult)
                    xs = x_.rearrange("p (h a f) -> p h a f", a=4, f=16)
                    r1 = RT[:, 1, 0:w].rearrange("p (h a f) -> p h a f", a=4, f=16)
                    sn = cst[:, C_ROPE + t * 128 + 64:C_ROPE + t * 128 + 128].rearrange("p (a f) -> p a f", f=16).unsqueeze(1)
                    for hh in range(2):
                        v.tensor_tensor(r1[:, :, hh::2], xs[:, :, 1 - hh::2], sn[:, :, hh::2].to_broadcast([P, n_heads, 2, 16]), ALU.mult)
                    dve.drain()
                    last = None
                    for dst, c0, c1 in outs:
                        a0, a1 = RT[:, 0, c0:c1], RT[:, 1, c0:c1]
                        if len(dst.shape) == 3:
                            a0, a1 = (a_.rearrange("p (j d) -> p j d", d=64) for a_ in (a0, a1))
                        last = v.tensor_tensor(dst, a0, a1, ALU.add)
                    return last

                dve.wait_ge(pads[l], 1)
                plan_taps = iter((10, 10, 24, 8, 6, 8))
                for job in in_jobs(l):
                    seg, t = job
                    key = ("in", l) + job
                    if seg == "uc" and t < 2:
                        if t == 0:
                            dve.wait_ge(g_exp[l], 1)
                            v.tensor_scalar(G[:, :, 0:n_ln], G[:, :, 0:n_ln], 1.0, None, ALU.add)
                            dve.drain()
                            v.reciprocal(G[:, :, 0:n_ln], G[:, :, 0:n_ln])
                            dve.drain()
                        wait_made(dve, key)
                        taken(v.tensor_tensor(zpad[:, t, 0:n_seq, PADC:PADC + S_LAT], bank(key)[:, 0:n_ln].rearrange("p (s t) -> p s t", s=n_seq),
                                              G[:, t, 0:n_ln].rearrange("p (s t) -> p s t", s=n_seq), ALU.mult), key)
                        if t == 1:
                            dve.drain()
                    elif seg in ("ka", "b", "qa") and t < 2:
                        conv(next(plan_taps))
                        wait_made(dve, key)
                        k = staged.index(job)
                        if k >= 2:
                            wait_made(dve, ("inT", l) + staged[k - 2])
                        stg = ST[:, k % 2]
                        if seg == "b":
                            v.tensor_copy(V[:, t, 512:640], bank(key)[:, 384:512])
                            dup = [stg[:, 256 + a * 64:].rearrange("p (j d) -> p j d", d=64)[:, 0::2] for a in range(2)]
                            last = rope(job, 6, [(stg[:, 0:256], 0, 256), (dup[0], 256, 384), (dup[1], 256, 384)])
                        else:
                            last = rope(job, 8, [(stg, 0, 512)])
                        taken(last, key)
                conv(2 * KCONV)
                dve.drain().then_inc(cv_d[l], 1)
                key = ("mu", l)
                wait_made(dve, key)
                for c2 in range(2):
                    last = v.scalar_tensor_tensor(acc[:, c2, 0:n_ln], bank(key)[:, 0:n_ln], -1.0 / CH, acc[:, c2, 0:n_ln], ALU.mult, ALU.add)
                taken(last, key)
                dve.drain().then_inc(ln_d[l], 1)
                mod_rows(1, bias12[:, 0], mst)
                key = ("var", l)
                wait_made(dve, key)
                taken(v.tensor_scalar(G[:, 0, 0:n_ln], bank(key)[:, 0:n_ln], 1.0 / CH, EPS, ALU.mult, ALU.add), key)
                dve.drain().then_inc(ln_v[l], 1)
                dve.wait_ge(ln_r[l], 1)
                for c2 in range(2):
                    last = v.tensor_tensor(acc[:, c2, 0:n_ln], acc[:, c2, 0:n_ln], G[:, 1, 0:n_ln], ALU.mult)
                last.then_inc(ln_n[l], 1)
                mod_rows(2, bias12[:, 1], mst)
                dve.wait_ge(ln_e[l], 1)
                v.tensor_scalar(G[:, :, 0:n_ln], G[:, :, 0:n_ln], 1.0, None, ALU.add)
                for c2 in range(2):
                    v.tensor_scalar(acc[:, c2, 0:n_ln], acc[:, c2, 0:n_ln], PC[:, l, 11 + c2:12 + c2], PC[:, l, 13 + c2:14 + c2], ALU.mult, ALU.add)
                dve.drain()
                v.reciprocal(G[:, :, 0:n_ln], G[:, :, 0:n_ln])
                dve.drain()
                wait_made(dve, ("in", l) + in_jobs(l)[-1])
                v.tensor_tensor(HT[:, 6:8, 0:n_ln], acc[:, :, 0:n_ln], G[:, :, 0:n_ln], ALU.mult)
                barrier(dve, bar(l, 2))

                units, tj = units_of(l), t_jobs(l)

                def maxima(n):
                    i, u = units[n]
                    kw = TOK if i < 2 else S_CTX
                    b = n % 2
                    pair = ps[:, 2 * b:2 * b + 2, :]
                    for m in range(2):
                        wait_made(dve, ("S", l, n, m))
                    if u < BLK_A:
                        v.tensor_reduce(mx[:, b], pair[:, :, 0:kw], AX.X, ALU.max)
                        dve.drain()
                        v.tensor_scalar(nm[:, b], mx[:, b], -HD ** -0.5, None, ALU.mult).then_inc(nm_done[l], 1)
                        return
                    prior = [k for k, (a, _) in enumerate(tj) if a == n - 2]
                    wait_made(dve, ("T", l, prior[-1]))
                    for m in range(2):
                        if i < 2:
                            v.scalar_tensor_tensor(PB[:, b, m, 0:256], pair[:, m, 0:256], HD ** -0.5,
                                                   cst[:, C_MASK + i * 256:C_MASK + (i + 1) * 256], ALU.mult, ALU.add)
                        last = v.tensor_scalar(PB[:, b, m, kw - 256:kw], pair[:, m, kw - 256:kw], HD ** -0.5, None, ALU.mult)
                        taken(last, ("S", l, n, m))
                    dve.drain()
                    v.tensor_reduce(mx[:, b], PB[:, b, :, 0:kw], AX.X, ALU.max)
                    dve.drain()
                    h = 2 * (u - BLK_A)
                    v.tensor_tensor(mx[:, b], mx[:, b], sink[:, l, h:h + 2], ALU.max)
                    dve.drain()
                    v.tensor_scalar(nm[:, b], mx[:, b], -1.0, None, ALU.mult).then_inc(nm_done[l], 1)

                def probs(n):
                    i, u = units[n]
                    kw = TOK if i < 2 else S_CTX
                    b = n % 2
                    if u < BLK_A:
                        wait_taken(dve, ("S", l, n, 1))
                        v.reciprocal(rec[:, n % 4], sums[:, b])
                        dve.drain()
                        v.scalar_tensor_tensor(cf[:, b:b + 1], sums[:, b, 0:1], neglam[:, l:l + 1], rec[:, n % 4, 1:2], ALU.mult, ALU.mult)
                        dve.drain()
                        v.scalar_tensor_tensor(PB[:, b, 0, 0:kw], PB[:, b, 1, 0:kw], cf[:, b:b + 1], PB[:, b, 0, 0:kw], ALU.mult, ALU.add).then_inc(pr_done[l], 1)
                    else:
                        dve.wait_ge(ex_done[l], sum(1 for _, x_ in units[:n + 1] if x_ >= BLK_A))
                        v.tensor_tensor(sums[:, b], sums[:, b], es[:, b], ALU.add)
                        dve.drain()
                        v.reciprocal(rec[:, n % 4], sums[:, b]).then_inc(pr_done[l], 1)

                def take_o(k):
                    n, m = tj[k]
                    i, u = units[n]
                    key = ("O", l, k)
                    wait_made(dve, key)
                    if u == 0 and i >= 2:
                        wait_made(dve, ("MB", l, i - 2))
                    w = P if u < BLK_A else HD
                    taken(v.tensor_scalar(O[i % 2][:, u * P + m * HD:u * P + m * HD + w], bank(key)[:, 0:w], rec[:, n % 4, m:m + 1], None, ALU.mult), key)
                    if u == BLK - 1 and m == 1:
                        dve.drain()
                        v.tensor_tensor(G[:, 0], O[i % 2][:, 0:512], O[i % 2][:, 0:512], ALU.mult)
                        dve.drain()
                        v.tensor_reduce(ss4[:, i % 2], G[:, 0].rearrange("p (h d) -> p h d", h=4), AX.X, ALU.add).then_inc(o_ss[l], 1)

                def head_norm(i):
                    dve.wait_ge(o_rs[l], i + 1)
                    oa = O[i % 2][:, 0:512].rearrange("p (h d) -> p h d", h=4)
                    v.tensor_tensor(oa, oa, rs4[:, i % 2].unsqueeze(2).to_broadcast([P, 4, P]), ALU.mult).then_inc(o_done[l], 1)

                for st_ in attention_steps(l):
                    if st_[0] == "S":
                        maxima(st_[1])
                        if st_[1]:
                            probs(st_[1] - 1)
                    elif st_[0] == "O":
                        if st_[1] == [k for k, (a, _) in enumerate(tj) if a == len(units) - 1][0]:
                            pass
                        take_o(st_[1])
                    elif st_[0] == "T" and tj[st_[1]] == (len(units) - 1, 0):
                        probs(len(units) - 1)
                    elif st_[0] == "M":
                        head_norm(st_[1])
                barrier(dve, bar(l, 3))

                def add_out(i):
                    cnd = i // 2
                    if i == 0:
                        dve.wait_ge(gate_in[l], 16 * conds)
                    for h in range(OUT_N):
                        key = ("wo", l, i, h)
                        wait_made(dve, key)
                        taken(v.tensor_tensor(tmp[:, h], bank(key), gate[:, cnd, h * CHUNK:(h + 1) * CHUNK], ALU.mult), key)
                    dve.drain()
                    v.tensor_tensor(X[:, i], X[:, i], tmp.rearrange("p b k -> p (b k)"), ALU.add)
                    dve.drain().then_inc(x_add[l], 1)

                def make_h2(i):
                    cnd = i // 2
                    dve.wait_ge(rs2[l], i + 1)
                    v.scalar_tensor_tensor(H2[:, i], X[:, i], rstd[:, i:i + 1], BC[:, cnd, 1], ALU.mult, ALU.mult)
                    dve.drain()
                    v.tensor_tensor(H2[:, i], H2[:, i], BC[:, cnd, 0], ALU.add).then_inc(h2_done[l], 1)

                dve.wait_ge(bc_in[l], 16 * (2 * conds + 1))
                for cnd in range(conds):
                    v.scalar_tensor_tensor(BC[:, cnd, 1], BC[:, cnd, 1], 1.0, GF, ALU.add, ALU.mult)
                dve.drain()
                for i in range(nq):
                    add_out(i)
                    if i:
                        make_h2(i - 1)
                make_h2(nq - 1)

                def T3(x_, n=E_N):
                    return x_[:, 0:nq]

                def over(x_, n):
                    return x_[:, 0:nq].unsqueeze(2).to_broadcast([P, nq, n])

                def consts(c0, n):
                    return cst[:, c0:c0 + n].unsqueeze(1).to_broadcast([P, nq, n])

                dve.wait_ge(h2_done[l], nq + 1)
                v.tensor_scalar(T3(e_s), T3(e_t), 1.0, None, ALU.add)
                dve.drain()
                v.reciprocal(T3(e_s), T3(e_s))
                dve.drain()
                v.tensor_tensor(T3(e_b), T3(e_s), rb[:].unsqueeze(1).to_broadcast([P, nq, E_N]), ALU.add)
                dve.drain()
                four = T3(e_b).rearrange("p t (g e) -> p (t g) e", e=4)
                ng = nq * E_G
                for a in range(2):
                    for o_, op in ((0, ALU.max), (1, ALU.min)):
                        v.tensor_tensor(hl[:, 2 * o_ + a, 0:ng], four[:, :, 2 * a], four[:, :, 2 * a + 1], op)
                dve.drain()
                gv = T3(grp).rearrange("p t g -> p (t g)")
                v.tensor_tensor(gv, hl[:, 0, 0:ng], hl[:, 1, 0:ng], ALU.max)
                v.tensor_tensor(T3(geq).rearrange("p t g -> p (t g)"), hl[:, 0, 0:ng], hl[:, 1, 0:ng], ALU.min)
                v.tensor_tensor(T3(gcd).rearrange("p t g -> p (t g)"), hl[:, 2, 0:ng], hl[:, 3, 0:ng], ALU.max)
                dve.drain()
                v.tensor_tensor(T3(geq), T3(geq), T3(gcd), ALU.max)
                dve.drain()
                v.tensor_tensor(T3(grp), T3(grp), T3(geq), ALU.add)
                dve.drain()

                def first_max(val, n, c_iota, mxv, eq, cand, low, out):
                    v.tensor_reduce(mxv[:, 0:nq], T3(val), AX.X, ALU.max)
                    dve.drain()
                    v.tensor_tensor(T3(eq), T3(val), over(mxv, n), ALU.is_ge)
                    dve.drain()
                    v.scalar_tensor_tensor(T3(cand), T3(eq), -float(n), consts(c_iota, n), ALU.mult, ALU.add)
                    dve.drain()
                    v.tensor_reduce(low[:, 0:nq], T3(cand), AX.X, ALU.min)
                    dve.drain()
                    v.tensor_tensor(T3(out), T3(cand), over(low, n), ALU.is_equal)
                    dve.drain()

                first_max(grp, E_G, C_I4, gm, geq, gcd, cm, gone)
                v.tensor_scalar(T3(gneg), T3(gone), BIG, -BIG, ALU.mult, ALU.add)
                e4 = [T3(x_).rearrange("p t (g e) -> p (t g) e", e=4) for x_ in (e_v, e_b)]
                gb = [T3(x_).rearrange("p t g -> p (t g)").unsqueeze(2).to_broadcast([P, ng, 4]) for x_ in (gone, gneg)]
                dve.drain()
                v.tensor_tensor(e4[0], e4[1], gb[0], ALU.mult)
                dve.drain()
                v.tensor_tensor(e4[0], e4[0], gb[1], ALU.add)
                dve.drain()
                first_max(e_v, E_N, C_I16, vm, e_eq, e_t, cmk0, oh[0])
                v.scalar_tensor_tensor(T3(e_v), T3(oh[0]), -3.0 * BIG, T3(e_v), ALU.mult, ALU.add)
                dve.drain()
                first_max(e_v, E_N, C_I16, vm, e_eq, e_t, cmk1, oh[1])
                v.tensor_tensor(T3(MM), T3(oh[0]), T3(oh[1]), ALU.add).then_inc(m_done[l], 1)
                for k, wk in ((0, w0), (1, w1k)):
                    v.tensor_tensor(T3(e_t), T3(e_s), T3(oh[k]), ALU.mult)
                    dve.drain()
                    v.tensor_reduce(wk[:, 0:nq], T3(e_t), AX.X, ALU.add)
                    dve.drain()
                v.tensor_tensor(wsum[:, 0:nq], w0[:, 0:nq], w1k[:, 0:nq], ALU.add)
                dve.drain()
                v.reciprocal(wsum[:, 0:nq], wsum[:, 0:nq])
                v.memset(PLi[:, :, :, 3:4], 0)
                dve.drain()
                for k, wk in ((0, w0), (1, w1k)):
                    v.tensor_tensor(PLf[:, k, 0:nq, 2], wk[:, 0:nq], wsum[:, 0:nq], ALU.mult)
                    v.tensor_copy(PLi[:, k, 0:nq, 0], cst[:, C_TOK:C_TOK + nq])
                    v.tensor_scalar(PLi[:, k, 0:nq, 1], cst[:, C_TOK:C_TOK + nq], float(k * routed(l)), None, ALU.add)
                key = ("rk", l)
                wait_made(dve, key)
                for k in range(2):
                    v.tensor_tensor(T3(e_t), bank(key)[:, 0:nq * E_N].rearrange("p (t e) -> p t e", e=E_N), T3(oh[k]), ALU.mult)
                    dve.drain()
                    v.tensor_reduce(rkf[:, k, 0:nq], T3(e_t), AX.X, ALU.add)
                    dve.drain()
                taken(v.tensor_copy(nbi[0:1, :], bank(key)[0:1, TILES * E_N:(TILES + 1) * E_N]), key)
                v.tensor_copy(rki[:, :, 0:nq], rkf[:, :, 0:nq])
                dve.drain()
                v.tensor_scalar(nbi[0:1, :], nbi[0:1, :], float(SLOT - 1), None, ALU.add)
                v.tensor_scalar(ji[:, :, 0:nq], rki[:, :, 0:nq], 6, None, ALU.arith_shift_right)
                v.tensor_scalar(pi[:, :, 0:nq], rki[:, :, 0:nq], SLOT - 1, None, ALU.bitwise_and)
                dve.drain()
                v.tensor_scalar(nb[0:1, :], nbi[0:1, :], 6, None, ALU.arith_shift_right)
                v.scalar_tensor_tensor(rowf[:, :, 0:nq], pi[:, :, 0:nq], float(E_N * JMAX), ji[:, :, 0:nq], ALU.mult, ALU.add)
                dve.drain()
                for k, low in ((0, cmk0), (1, cmk1)):
                    v.scalar_tensor_tensor(rowf[:, k, 0:nq], low[:, 0:nq], float(JMAX), rowf[:, k, 0:nq], ALU.mult, ALU.add)
                dve.drain()
                v.tensor_scalar(ROWI[:, :, 0:nq], rowf[:, :, 0:nq], float(E_N * JMAX), None, ALU.add)
                dve.drain().then_inc(pl_done[l], 1)
                barrier(dve, bar(l, 4))
                dve.drain().then_inc(nb_ready[l], 1)

                dve.wait_ge(init_m[l], 1)
                dve.wait_ge(tb_in[l], 16)
                dve.sem_inc(y_rdy[l], 2)
                done = dve.alloc_register(f"dve_blocks_{l}")
                dve.reg_mov(done, 0)

                def copy_gT(b):
                    dve.wait_ge(gt_full[l], b)
                    v.tensor_copy(gT.rearrange("p k s -> p (k s)"), ps[:, B_GT, 0:4 * SLOT]).then_inc(gt_rdy[l], 1)

                def copy_y(b):
                    dve.wait_ge(w2_full[l], b)
                    dve.wait_ge(scat[l], 16 * b + 16)
                    v.tensor_copy(ym[0:SLOT, 0:CHUNK], ps[0:SLOT, B_W2, :])
                    v.tensor_copy(ym[0:SLOT, CHUNK:D], ps[SLOT:P, B_W2, :]).then_inc(y_rdy[l], 1)

                def step(col, first=False):
                    b = dve.snap(done)
                    if not first:
                        copy_gT(b)
                    dve.wait_ge(si_rdy[l], b + 1)
                    v.scalar_tensor_tensor(gg[0:SLOT, :], sg[0:SLOT, :], TBf[0:SLOT, bass.ds(4 * col + 2, 1)], ps[SLOT:P, B_W13, :],
                                           ALU.mult, ALU.mult).then_inc(g_rdy[l], 1)
                    if not first:
                        copy_y(b)
                    dve.reg_add(done, done, 1)

                def expert(e, first=False):
                    blocks = dve.value_load(nb[0:1, bass.ds(e, 1)], min_val=0, max_val=JMAX)
                    step(e * JMAX, first)
                    with dve.If(blocks > 1):
                        with dve.Fori(1, blocks) as j:
                            step(e * JMAX + j)

                expert(0, True)
                with dve.Fori(1, E_N) as e:
                    expert(e)
                b = dve.snap(done)
                copy_gT(b)
                copy_y(b)
                barrier(dve, bar(l, 5))

                dve.wait_ge(gate_in[l], 32 * conds)
                for i in range(nq):
                    a, c2 = i // 2, i % 2
                    dve.wait_ge(y_in[l], 64 * (a + 1))
                    v.tensor_tensor(Y[:, 0, c2], Y[:, 0, c2], Y[:, 1, c2], ALU.add)
                    dve.drain()
                    v.tensor_tensor(Y[:, 0, c2], Y[:, 0, c2], gate[:, a], ALU.mult)
                    dve.drain()
                    v.tensor_tensor(X[:, i], X[:, i], Y[:, 0, c2], ALU.add).then_inc(comb[l], 1)
                if l == DEPTH - 1:
                    dve.wait_ge(fin_rs, 1)
                    dve.wait_ge(fin_g, 16)
                    for i in range(2):
                        v.scalar_tensor_tensor(X[:, i], X[:, i], rstd[:, i:i + 1], GFIN, ALU.mult, ALU.mult).then_inc(fin_o, 1)
                barrier(dve, bar(l, 6))

        @block.tensor
        def _(pe):
            t_ = nc.tensor

            def mm(out, lhsT, rhs, first, last_):
                return t_.matmul(out, lhsT, rhs, start=first, stop=last_)

            pe.wait_ge(cst_in, 16)
            pe.wait_ge(par_in, 16 * N_PAR)
            made(t_.transpose(bank(("par",))[:, 0:DEPTH * 15], PR[0:DEPTH * 15, :], ident[0:DEPTH * 15, 0:DEPTH * 15]), ("par",))
            nk = DEPTH * KCONV
            for c2 in range(2):
                last = t_.transpose(bank(("cw",))[:, c2 * nk:(c2 + 1) * nk], CWR[0:nk, c2 * P:(c2 + 1) * P], ident[0:nk, 0:nk])
            made(last, ("cw",))
            pe.wait_ge(c_silu, 1)
            made(t_.transpose(bank(("c",))[:, 0:16], CRS[0:16, :], ident[0:16, 0:16]), ("c",))
            wait_taken(pe, ("c",))

            def ada(l, q):
                key = ("ada", l, q)
                claim(pe, key)
                for j in range(4):
                    arrived(pe, l, U_ADA[4 * q + j])
                for k in range(KD):
                    for j in range(4):
                        last = mm(bank(key)[32 * j:32 * j + 32, :], SC[:, k], ring[:, slot(l, U_ADA[4 * q + j]), k], k == 0, k == KD - 1)
                made(last, key)
                for j in range(4):
                    pe.drain().then_inc(ring_free[slot(l, U_ADA[4 * q + j])], 1)

            for l in range(DEPTH):
                nq = TILES if l == 0 else 2
                n_ln = TOK if l == 0 else S_LAT
                ada(l, 0)
                pe.wait_ge(mrow_in[l], 32)
                claim(pe, ("modc", l))
                made(t_.transpose(bank(("modc", l))[:, 0:32], MR[0:32, :], ident[0:32, 0:32]), ("modc", l))
                pe.wait_ge(y_done[l], 1)
                for q in range(8):
                    key = ("nT", l, q)
                    claim(pe, key)
                    cnd, kk = q // 4, 2 * (q % 4)
                    for a in range(2):
                        for t in range(2):
                            last = t_.transpose(bank(key)[:, a * 256 + t * P:a * 256 + (t + 1) * P],
                                                YS[:, 2 * cnd + t, (kk + a) * P:(kk + a + 1) * P], ident)
                    made(last, key)
                barrier(pe, bar(l, 1))

                def transposes(job):
                    key = ("inT", l) + job
                    wait_taken(pe, ("in", l) + job)
                    claim(pe, key)
                    stg = ST[:, staged.index(job) % 2]
                    for b in range(2 if job[0] == "b" and job[1] >= 2 and l else 0, 4):
                        last = t_.transpose(bank(key)[:, b * P:(b + 1) * P], stg[:, b * P:(b + 1) * P], ident)
                    made(last, key)

                staged = [j for j in in_jobs(l) if j[0] in ("ka", "b", "qa")]
                prev, jobs = None, in_jobs(l)
                for x_, job in enumerate(jobs):
                    seg, t = job
                    key = ("in", l) + job
                    unit = ring[:, slot(l, U_IN[seg])]
                    if x_ == 0 or jobs[x_ - 1][0] != seg:
                        arrived(pe, l, U_IN[seg])
                    claim(pe, key)
                    for k in range(KD):
                        if seg == "uc":
                            last = mm(bank(key)[:, 0:n_ln], unit[:, k, t * P:(t + 1) * P], HT[:, k, 0:n_ln], k == 0, k == KD - 1)
                        elif seg == "b" and l and t >= 2:
                            last = mm(bank(key)[:, 256:512], HT[:, k, t * P:(t + 1) * P], unit[:, k, 256:512], k == 0, k == KD - 1)
                        else:
                            last = mm(bank(key), HT[:, k, t * P:(t + 1) * P], unit[:, k], k == 0, k == KD - 1)
                    made(last, key)
                    if x_ == len(jobs) - 1 or jobs[x_ + 1][0] != seg:
                        pe.drain().then_inc(ring_free[slot(l, U_IN[seg])], 1)
                    if prev:
                        transposes(prev)
                    prev = job if job in staged else None
                if prev:
                    transposes(prev)
                pe.wait_ge(cv_d[l], 1)
                claim(pe, ("mu", l))
                for c2 in range(2):
                    last = mm(bank(("mu", l))[:, 0:n_ln], ones, acc[:, c2, 0:n_ln], c2 == 0, c2 == 1)
                made(last, ("mu", l))
                ada(l, 1)
                pe.wait_ge(ln_sq[l], 1)
                claim(pe, ("var", l))
                for c2 in range(2):
                    last = mm(bank(("var", l))[:, 0:n_ln], ones, G[:, c2, 0:n_ln], c2 == 0, c2 == 1)
                made(last, ("var", l))
                ada(l, 2)
                barrier(pe, bar(l, 2))

                units, tj = units_of(l), t_jobs(l)
                for st_ in attention_steps(l):
                    what, x_ = st_
                    if what == "S":
                        i, u = units[x_]
                        k0 = 0 if i < 2 else S_LAT
                        for m in range(2):
                            claim(pe, ("S", l, x_, m))
                        for m in range(2):
                            rows = slice(64 * m, 64 * m + 64)
                            made(mm(bank(("S", l, x_, m))[:, 0:TOK - k0], qT[rows, u, i * P:(i + 1) * P], kT[rows, u, k0:TOK], True, True), ("S", l, x_, m))
                    elif what == "T":
                        n, m = tj[x_]
                        i, u = units[n]
                        key = ("T", l, x_)
                        pe.wait_ge(pr_done[l], n + 1)
                        claim(pe, key)
                        for kt in range(4 if i < 2 else 2):
                            last = t_.transpose(bank(key)[:, kt * P:(kt + 1) * P], PB[:, n % 2, m, kt * P:(kt + 1) * P], ident)
                        made(last, key)
                    elif what == "O":
                        n, m = tj[x_]
                        i, u = units[n]
                        key = ("O", l, x_)
                        wait_taken(pe, ("T", l, x_))
                        claim(pe, key)
                        c0, w = (u * P, P) if u < BLK_A else (512 + (u - BLK_A) * HD, HD)
                        nkt = 4 if i < 2 else 2
                        for kt in range(nkt):
                            last = mm(bank(key)[:, 0:w], aT[:, x_ % 2, kt * P:(kt + 1) * P], V[:, 4 - nkt + kt, c0:c0 + w], kt == 0, kt == nkt - 1)
                        made(last, key)
                    else:
                        pe.wait_ge(o_done[l], x_ + 1)
                        for name, b0, b1 in (("MA", 0, 4), ("MB", 4, 6)):
                            key = (name, l, x_)
                            claim(pe, key)
                            for b in range(b0, b1):
                                last = t_.transpose(bank(key)[:, (b - b0) * P:(b - b0 + 1) * P], O[x_ % 2][:, b * P:(b + 1) * P], ident)
                            made(last, key)
                barrier(pe, bar(l, 3))

                def route(i):
                    pe.wait_ge(h2_done[l], i + 1)
                    for h in range(2):
                        key = ("h2T", l, i, h)
                        claim(pe, key)
                        for b in range(4):
                            k = 4 * h + b
                            last = t_.transpose(bank(key)[:, b * P:(b + 1) * P], H2[:, i, k * P:(k + 1) * P], ident)
                        made(last, key)
                    for h in range(2):
                        wait_taken(pe, ("h2T", l, i, h))
                    key = ("rt", l, i)
                    claim(pe, key)
                    for k in range(KD):
                        last = mm(bank(key)[:, 0:E_N], hTr[:, k], rw[:, k], k == 0, k == KD - 1)
                    made(last, key)

                for h in range(OUT_N):
                    arrived(pe, l, U_OUT + h)
                for i in range(nq):
                    for h in range(OUT_N):
                        key = ("wo", l, i, h)
                        claim(pe, key)
                        for k in range(KD):
                            last = mm(bank(key), HT[:, k, i * P:(i + 1) * P], ring[:, slot(l, U_OUT + h), k], k == 0, k == KD - 1)
                        made(last, key)
                        if i == nq - 1:
                            pe.drain().then_inc(ring_free[slot(l, U_OUT + h)], 1)
                    if i:
                        route(i - 1)
                route(nq - 1)
                key = ("rk", l)
                pe.wait_ge(m_done[l], 1)
                claim(pe, key)
                for i in range(nq):
                    out = bank(key)[:, i * E_N:(i + 1) * E_N]
                    for j in range(i):
                        mm(out, ones, MM[:, j], j == 0, False)
                    mm(out, tri, MM[:, i], i == 0, True)
                for i in range(nq):
                    last = mm(bank(key)[:, TILES * E_N:(TILES + 1) * E_N], ones, MM[:, i], i == 0, i == nq - 1)
                made(last, key)
                barrier(pe, bar(l, 4))

                pe.wait_ge(nb_ready[l], 1)
                pe.sem_inc(xt_full[l], 1)
                done = pe.alloc_register(f"pe_blocks_{l}")
                pe.reg_mov(done, 0)

                def gT_product(b, free=()):
                    hold(pe, g_rdy[l], b, pe_passed)
                    for k in range(4):
                        last = t_.transpose(ps[:, B_GT, k * SLOT:(k + 1) * SLOT], gg[0:SLOT, k * P:(k + 1) * P], ident[0:SLOT, 0:SLOT])
                        if k < len(free):
                            last.then_inc(ring_free[free[k]], 1)
                    last.then_inc(gt_full[l], 1)

                def w2_product(b, sl, until=None):
                    pe.wait_ge(gt_rdy[l], b)
                    pe.wait_ge(y_rdy[l], b + 1)
                    if until is not None:
                        pe.wait_ge(ring_full[sl], until)
                    w = ring[:, sl].rearrange("p k n -> p (k n)").rearrange("p (k n) -> p k n", k=4)
                    for k in range(4):
                        for h in range(2):
                            last = mm(ps[64 * h:64 * h + 64, B_W2, :], gT[:, k], w[:, k, h * CHUNK:(h + 1) * CHUNK], k == 0, k == 3)
                    last.then_inc(w2_full[l], 1)

                def step(slots, prev_slot, waits, free=(), first=False):
                    b = pe.snap(done)
                    hold(pe, gath[l], 16 * b + 16, pe_passed)
                    for k in range(KD):
                        last = t_.transpose(ps[:, B_XT, k * SLOT:(k + 1) * SLOT], xg[0:SLOT, k * P:(k + 1) * P], ident[0:SLOT, 0:SLOT])
                        if k < len(free):
                            last.then_inc(ring_free[free[k]], 1)
                    last.then_inc(xt_full[l], 1)
                    if not first:
                        gT_product(b)
                    pe.wait_ge(xt_rdy[l], b + 1)
                    if waits:
                        for q in range(2):
                            pe.wait_ge(ring_full[slots[q]], waits[q])
                    for k in range(KD):
                        for h in range(2):
                            last = mm(ps[64 * h:64 * h + 64, B_W13, :], xT[:, k], ring[:, slots[h], k], k == 0, k == KD - 1)
                    last.then_inc(w13_full[l], 1)
                    if not first:
                        w2_product(b, prev_slot, waits[2] if waits else None)
                    pe.reg_add(done, done, 1)

                def expert(i, q, first=False):
                    e = 2 * i + q
                    n = [U_MOE + 3 * q + w for w in range(3)]
                    sl = [slot(l, x_) for x_ in n]
                    waits = [16 * (use(l, x_) + i) + 16 for x_ in n[:2]]
                    before = n[0] - 1
                    waits.append(16 * (use(l, before) + i) + 16)
                    free = []
                    if not first:
                        free = [slot(l, n[0] - 3), slot(l, n[0] - 2)]
                        if not (isinstance(i, int) and e < 2):
                            free.append(slot(l, n[0] - 4))
                    blocks = pe.value_load(nb[0:1, bass.ds(e, 1)], min_val=0, max_val=JMAX)
                    step(sl, slot(l, before), waits, free, first)
                    with pe.If(blocks > 1):
                        hold(pe, ring_full[sl[2]], 16 * (use(l, n[2]) + i) + 16, pe_passed)
                        with pe.Fori(1, blocks):
                            step(sl, sl[2], None)

                expert(0, 0, True)
                expert(0, 1)
                with pe.Fori(1, E_N // 2) as i:
                    for q in range(2):
                        expert(i, q)
                b = pe.snap(done)
                n15 = U_MOE + 3 * E_N - 3
                gT_product(b, [slot(l, n15), slot(l, n15 + 1), slot(l, n15 - 1)])
                w2_product(b, slot(l, n15 + 2), 16 * use(l, n15 + 2) + 16)
                pe.drain().then_inc(ring_free[slot(l, n15 + 2)], 1)
                barrier(pe, bar(l, 5))
                barrier(pe, bar(l, 6))


N_PAR = 2 + 5 * DEPTH + 5

_NAMES = ["x", "c", "ctx", "c_ctx", "w_ada", "b_ada", "g_mix", "w_in", "diff_lambda", "diff_norm_g", "attn_sink", "conv_w", "conv_b",
          "conv_ln_g", "conv_ln_b", "w_out", "g_ffn", "router_w", "router_bias", "w1", "w3", "w2", "g_final"]


def kernel(**inputs):
    import concourse.bacc as bacc
    from concourse.bass_utils import run_bass_kernel_spmd

    nc = bacc.Bacc("TRN2", target_bir_lowering=False, num_devices=1)
    arrays, A = {}, {}
    for name in _NAMES:
        a = np.ascontiguousarray(inputs[name])
        arrays[f"in_{name}"] = a
        A[name] = nc.dram_tensor(f"in_{name}", a.shape, mybir.dt.from_np(a.dtype), kind="ExternalInput").ap()
    arrays["in_cst"] = constants()
    A["cst"] = nc.dram_tensor("in_cst", arrays["in_cst"].shape, mybir.dt.float32, kind="ExternalInput").ap()
    A["out"] = nc.dram_tensor("out", (1, S_LAT, D), mybir.dt.float32, kind="ExternalOutput").ap()
    hybrid_moe_kernel(nc, A)
    return run_bass_kernel_spmd(nc, [arrays], core_ids=[0]).results[0]["out"]
```

```python
import math
from contextlib import ExitStack

import concourse.bass as bass
import numpy as np
from concourse import mybir

P = 128
D = 1024
KD = D // P
S_LAT = 256
S_CTX = 256
TOK = S_LAT + S_CTX
TILES = TOK // P
DEPTH = 2
GRID_W = 64
HD = 64
BLK_A, BLK_B = 4, 2
BLK = BLK_A + BLK_B
VW = 512 + 128
CH = 256
KCONV = 31
PADC = KCONV // 2
E_N, E_G, E_F = 16, 4, 512
SLOT = 64
JMAX = TOK // SLOT
EPS = 1e-6
BIG = 1e30
NO_ROW = 1 << 20
WINDOW = 128
CHUNK = 512
ADA_N = 6 * D // CHUNK
IN_N = 5
OUT_N = D // CHUNK
FRONT_N = ADA_N + IN_N + OUT_N
RING = 6
GROUPS = 3
EXTRA = 3 * GROUPS - RING

C_ID, C_TRI, C_ONE = 0, 128, 256
C_ROPE = 384
C_MASK = C_ROPE + 2 * 128
C_I16 = C_MASK + 2 * 256
C_I4 = C_I16 + 16
C_TOK = C_I4 + 4
C_W = C_TOK + TILES


def routed(l):
    return TOK if l < DEPTH - 1 else S_LAT


def lambda_init(l):
    return 0.8 - 0.6 * math.exp(-0.3 * l)


def constants():
    c = np.zeros((P, C_W), np.float32)
    r = np.arange(P)
    c[:, C_ID:C_ID + P] = np.eye(P)
    c[:, C_TRI:C_TRI + P] = r[:, None] < r[None, :]
    c[:, C_ONE:C_ONE + P] = 1.0
    nf = HD // 4
    inv = (np.float32(10000.0) ** (-np.arange(nf, dtype=np.float32) / np.float32(nf))).astype(np.float32)
    for t in range(S_LAT // P):
        q = t * P + r
        pos = np.stack([q // GRID_W, q % GRID_W], -1).astype(np.float32)
        ang = pos[:, :, None] * inv
        cos, sin = np.cos(ang), np.sin(ang)
        c[:, C_ROPE + t * 128:C_ROPE + t * 128 + 64] = np.stack([cos, cos], 2).reshape(P, 64)
        c[:, C_ROPE + t * 128 + 64:C_ROPE + t * 128 + 128] = np.stack([-sin, sin], 2).reshape(P, 64)
        k = np.arange(S_LAT)
        c[:, C_MASK + t * 256:C_MASK + (t + 1) * 256] = np.where(np.abs(q[:, None] - k) <= WINDOW, 0.0, -BIG)
    c[:, C_I16:C_I16 + 16] = np.arange(16)
    c[:, C_I4:C_I4 + 4] = np.arange(4)
    c[:, C_TOK:C_TOK + TILES] = r[:, None] + P * np.arange(TILES)
    return c


def bank_plan():
    uses, plan, turn = [0] * 8, {}, {}

    def put(key, banks=range(8), bank=None):
        if bank is None:
            name = tuple(banks)
            bank = name[turn.get(name, 0) % len(name)]
            turn[name] = turn.get(name, 0) + 1
        plan[key] = (bank, uses[bank])
        uses[bank] += 1

    for key in ("c", "par", "cw"):
        put((key,))
    for l in range(DEPTH):
        nq = TILES if l == 0 else 2
        put(("ada", l, 0))
        put(("modc", l))
        for g in range(8):
            put(("nT", l, g))
        prev = None
        for job in in_jobs(l):
            put(("in", l) + job)
            if prev:
                put(("inT", l) + prev)
            prev = job if job[0] in ("ka", "b", "qa") else None
        if prev:
            put(("inT", l) + prev)
        put(("mu", l))
        put(("ada", l, 1))
        put(("var", l))
        put(("ada", l, 2))
        for step in attention_steps(l):
            if step[0] == "S":
                for m in range(2):
                    put(("S", l, step[1], m), bank=2 * (step[1] % 2) + m)
            elif step[0] == "T":
                put(("T", l, step[1]), (4, 5))
            elif step[0] == "O":
                put(("O", l, step[1]), (6, 7))
            else:
                put(("MA", l, step[1]), (4, 5))
                put(("MB", l, step[1]), (4, 5))
        for i in range(nq):
            for h in range(OUT_N):
                put(("wo", l, i, h))
            if i >= 1:
                for h in range(2):
                    put(("h2T", l, i - 1, h))
                put(("rt", l, i - 1))
        for h in range(2):
            put(("h2T", l, nq - 1, h))
        put(("rt", l, nq - 1))
        put(("rk", l))
    return plan, uses


def ring_plan():
    uses, at, front, experts = [0] * (RING + EXTRA), 0, [], []
    for _ in range(DEPTH):
        row = []
        for _ in range(FRONT_N):
            row.append((at, uses[at]))
            uses[at] += 1
            at = (at + 1) % RING
        front.append(row)
        groups = [[(at + 3 * g_ + w) % RING for w in range(3)] for g_ in range(2)] + [list(range(RING, RING + EXTRA))]
        experts.append((groups, list(uses)))
        for e in range(E_N):
            for x in groups[e % GROUPS]:
                uses[x] += 1
        at = (at + 3) % RING
    return front, experts


def in_jobs(l):
    q_tiles = TILES if l == 0 else 2
    return ([("uc", f) for f in (2, 3, 0, 1)] + [("ka", t) for t in range(TILES)] + [("b", t) for t in range(TILES)]
            + [("va", t) for t in range(TILES)] + [("qa", t) for t in range(q_tiles)])


def units_of(l):
    return [(i, u) for i in range(TILES if l == 0 else 2) for u in range(BLK)]


def t_jobs(l):
    return [(n, m) for n, (_, u) in enumerate(units_of(l)) for m in range(1 if u < BLK_A else 2)]


def attention_steps(l):
    units, tj = units_of(l), t_jobs(l)
    out = [("S", 0), ("S", 1)]
    for n in range(len(units)):
        if n + 2 < len(units):
            out.append(("S", n + 2))
        out += [("T", k) for k, (a, _) in enumerate(tj) if a == n]
        out += [("O", k) for k, (a, _) in enumerate(tj) if a == n - 1]
        if units[n][1] == 2 and units[n][0] > 0:
            out.append(("M", units[n][0] - 1))
    out += [("O", k) for k, (a, _) in enumerate(tj) if a == len(units) - 1]
    out.append(("M", units[-1][0]))
    return out


def hybrid_moe_kernel(nc, A):
    fp32, i32 = mybir.dt.float32, mybir.dt.int32
    ALU, ACT, AX = mybir.AluOpType, mybir.ActivationFunctionType, mybir.AxisListType
    PLAN, USES = bank_plan()
    ctx = ExitStack()
    with ctx:
        def sb(name, shape, dt=fp32):
            return ctx.enter_context(nc.sbuf_tensor(name, shape, dt))

        def sem(name):
            return ctx.enter_context(nc.semaphore(name))

        def sems(name, n):
            return [sem(f"{name}_{k}") for k in range(n)]

        ring = sb("ring", [P, RING, KD, CHUNK])
        X = sb("X", [P, TILES, D])
        HT = sb("HT", [P, KD, TOK])
        gate = sb("gate", [P, 2, D])
        cst = sb("cst", [P, C_W])
        SC = sb("SC", [P, KD, 32])
        PC = sb("PC", [P, DEPTH, 15])
        NC = sb("NC", [P, DEPTH, 5])
        CW = sb("CW", [P, 2, DEPTH * KCONV])
        rw = sb("rw", [P, KD, E_N])
        rb = sb("rb", [P, E_N])
        sink = sb("sink", [P, DEPTH, 4])
        lamx = sb("lamx", [P, DEPTH, 2])
        neglam = sb("neglam", [P, DEPTH])
        AB = sb("AB", [P, 2, 2, KD])
        MCOL = sb("MCOL", [P, 2, 2, KD])
        half = sb("half", [P, 1])
        ss = sb("ss", [P, TILES])
        ms = sb("ms", [P, TILES])
        rstd = sb("rstd", [P, TILES])
        mx = sb("mx", [P, 2, 2])
        nm = sb("nm", [P, 2, 2])
        sums = sb("sums", [P, 2, 2])
        es = sb("es", [P, 2, 2])
        rec = sb("rec", [P, 4, 2])
        cf = sb("cf", [P, 2])
        ss4 = sb("ss4", [P, 2, 4])
        ms4 = sb("ms4", [P, 2, 4])
        rs4 = sb("rs4", [P, 2, 4])
        AW = 2560 + 2 * 3072 + 1024 + 1144 + 1024 + 3840
        area = sb("area", [P, AW])
        at = [0]

        def cut(width, start=None):
            if start is not None:
                at[0] = start
            piece = area[:, at[0]:at[0] + width]
            at[0] += width
            assert at[0] <= AW, at[0]
            return piece

        V = cut(TILES * VW, 0).rearrange("p (t w) -> p t w", t=TILES)
        qT = cut(BLK * TOK).rearrange("p (b t) -> p b t", b=BLK)
        kT = cut(BLK * TOK).rearrange("p (b t) -> p b t", b=BLK)
        G = cut(2 * TOK).rearrange("p (c t) -> p c t", c=2)
        ZP_AT = at[0]
        zpad = cut(2 * 2 * (S_LAT + 2 * PADC)).rearrange("p (c s t) -> p c s t", c=2, s=2)
        acc = cut(2 * TOK).rearrange("p (c t) -> p c t", c=2)
        S1 = at[0]
        PB = cut(2048, S1).rearrange("p (b m k) -> p b m k", b=2, m=2)
        aT = cut(1024).rearrange("p (b k) -> p b k", b=2)
        O = [cut(BLK * P), area[:, ZP_AT:ZP_AT + BLK * P]]
        RT = cut(1024, S1).rearrange("p (b k) -> p b k", b=2)
        ST = cut(1024).rearrange("p (b k) -> p b k", b=2)
        bias12 = cut(1024).rearrange("p (b k) -> p b k", b=2)
        mst = cut(512)
        YS = cut(TILES * D, 0).rearrange("p (t d) -> p t d", t=TILES)
        bias0 = cut(512)
        mst0 = cut(512)
        PR = cut(128)
        CR = cut(128)
        CRS = cut(128)
        CWR = cut(256)
        DL = cut(DEPTH * 4 * HD).rearrange("p (l a d) -> p l a d", l=DEPTH, a=4)
        DLP = cut(DEPTH * 2 * HD).rearrange("p (l a d) -> p l a d", l=DEPTH, a=2)
        MR = cut(128)
        SI = cut(512).bitcast(i32)
        BC = cut(2 * 2 * D, 0).rearrange("p (c v d) -> p c v d", c=2, v=2)
        GF = cut(D)
        H2 = cut(TILES * D).rearrange("p (t d) -> p t d", t=TILES)
        hTr = cut(KD * P).rearrange("p (k t) -> p k t", k=KD)
        tmp = cut(2 * CHUNK).rearrange("p (b k) -> p b k", b=2)
        R_AT = at[0]
        RW = 64

        def rt_tile(width):
            return cut(width)

        e_s, e_b, e_v, e_t, e_eq = (rt_tile(RW).rearrange("p (t e) -> p t e", e=E_N) for _ in range(5))
        oh = [rt_tile(RW).rearrange("p (t e) -> p t e", e=E_N) for _ in range(2)]
        MM = rt_tile(RW).rearrange("p (t e) -> p t e", e=E_N)
        hl = rt_tile(4 * 16).rearrange("p (a g) -> p a g", a=4)
        grp, geq, gcd, gone, gneg = (rt_tile(16).rearrange("p (t g) -> p t g", g=E_G) for _ in range(5))
        gm, cm, vm, cmk0, cmk1, w0, w1k, wsum = (rt_tile(TILES) for _ in range(8))
        rkf = rt_tile(2 * TILES).rearrange("p (k t) -> p k t", k=2)
        rowf = rt_tile(2 * TILES).rearrange("p (k t) -> p k t", k=2)
        rki = rt_tile(2 * TILES).bitcast(i32).rearrange("p (k t) -> p k t", k=2)
        ji = rt_tile(2 * TILES).bitcast(i32).rearrange("p (k t) -> p k t", k=2)
        pi = rt_tile(2 * TILES).bitcast(i32).rearrange("p (k t) -> p k t", k=2)
        ROWI = rt_tile(2 * TILES).bitcast(i32).rearrange("p (k t) -> p k t", k=2)
        PLf = rt_tile(2 * TILES * 4).rearrange("p (k t w) -> p k t w", k=2, w=4)
        PLi = PLf.bitcast(i32)
        nbi = rt_tile(E_N).bitcast(i32)
        nb = rt_tile(E_N).bitcast(i32)
        TBf = cut(E_N * JMAX * 4)
        TBi = TBf.bitcast(i32)
        DR = cut(4).bitcast(i32)
        gidx = cut(1).bitcast(i32)
        sidx = cut(1).bitcast(i32)
        xg = cut(D)
        YM_AT = at[0]
        xT = cut(KD * SLOT, 0).rearrange("p (k s) -> p k s", k=KD)
        sg = cut(E_F)
        gg = cut(E_F)
        gT = cut(4 * SLOT).rearrange("p (k s) -> p k s", k=4)
        ym = cut(D)
        EX_AT = at[0]
        assert EX_AT + 2 * 4096 <= R_AT
        Y = cut(2 * TILES * D // 2, 0).rearrange("p (k b d) -> p k b d", k=2, b=2)
        GFIN = cut(D, 4096)

        ps = ctx.enter_context(nc.psum_tensor("ps", [P, 8, CHUNK], fp32))
        B_XT, B_GT, B_W13, B_W2 = 0, 1, 2, 3

        modD = nc.dram_tensor("mod_rows", [DEPTH, 2, 6 * D], fp32).ap()
        h2D = [nc.dram_tensor(f"h2_rows_{l}", [routed(l), D], fp32).ap() for l in range(DEPTH)]
        yD = [nc.dram_tensor(f"expert_rows_{l}", [2 * routed(l), D], fp32).ap() for l in range(DEPTH)]
        slotD = [nc.dram_tensor(f"slot_rows_{l}", [SLOT * E_N * JMAX, 4], i32).ap() for l in range(DEPTH)]

        full = sems("bank_full", 8)
        evict = sems("bank_evicted", 8)
        ring_full = sems("ring_full", RING + EXTRA)
        ring_free = sems("ring_free", RING + EXTRA)
        cst_in = sem("constants_in")
        par_in = sem("parameters_in")
        x_in = sem("x_in")
        c_silu = sem("c_silu")
        setup = sem("setup_done")
        si_out = sem("slot_tables_cleared")
        lam_sum = sem("lambda_sums")
        lam_exp = sem("lambda_exps")
        phase = sem("phase")
        bias_in = sems("bias_in", DEPTH)
        mod_sb = sems("mod_rows_made", DEPTH)
        mod_out = [sems(f"mod_rows_stored_{l}", 3) for l in range(DEPTH)]
        mrow_in = sems("mod_columns_in", DEPTH)
        ss_done = sem("squares_summed")
        rs_done = sem("rstd_made")
        y_done = sem("normed")
        ab_done = sem("columns_made")
        pads = sem("pads_zero")
        g_exp = sem("conv_gate_exp")
        cv_d = sem("conv_done")
        ln_d = sem("ln_centred")
        ln_sq = sem("ln_squares")
        ln_v = sem("ln_variance")
        ln_r = sem("ln_rstd")
        ln_n = sem("ln_normed")
        ln_e = sem("ln_exp")
        nm_done = sems("negmax", DEPTH)
        ex_done = sems("exps_b", DEPTH)
        pr_done = sems("probs", DEPTH)
        o_ss = sems("head_squares", DEPTH)
        o_rs = sems("head_rstd", DEPTH)
        o_done = sems("heads_normed", DEPTH)
        gate_in = sems("gate_in", DEPTH)
        bc_in = sems("ffn_rows_in", DEPTH)
        bc_done = sems("ffn_scale_made", DEPTH)
        x_add = sems("residual_added", DEPTH)
        ss2 = sems("squares2", DEPTH)
        rs2 = sems("rstd2", DEPTH)
        h2_done = sems("h2_made", DEPTH)
        h2_out = sems("h2_stored", DEPTH)
        m_done = sem("choices_made")
        pl_done = sem("slots_made")
        slot_out = sems("slots_scattered", DEPTH)
        tb_in = sems("slot_table_in", DEPTH)
        nb_ready = sem("counts_ready")
        init_m = sem("expert_buffers_filled")
        gath = sems("tokens_gathered", DEPTH)
        xt_full = sems("xT_product", DEPTH)
        xt_rdy = sems("xT_copied", DEPTH)
        gt_full = sems("gT_product", DEPTH)
        gt_rdy = sems("gT_copied", DEPTH)
        w13_full = sems("w13_product", DEPTH)
        si_rdy = sems("silu_made", DEPTH)
        g_rdy = sems("hidden_made", DEPTH)
        w2_full = sems("w2_product", DEPTH)
        y_rdy = sems("y_copied", DEPTH)
        scat = sems("y_scattered", DEPTH)
        y_in = sems("y_in", DEPTH)
        comb = sems("y_added", DEPTH)
        pool_chain = sem("pool_chain")
        gidx_set = sems("gather_rows_set", DEPTH)
        sidx_set = sems("scatter_rows_set", DEPTH)
        sp_passed = sem("sp_waits_passed")
        pe_passed = sem("pe_waits_passed")
        pool_passed = sem("pool_waits_passed")
        fin_ss = sem("final_squares")
        fin_rs = sem("final_rstd")
        fin_g = sem("final_gain_in")
        fin_o = sem("final_made")
        stored = sem("output_stored")

        def bank(key):
            return ps[:, PLAN[key][0], :]

        def claim(pe, key):
            b, u = PLAN[key]
            if u:
                pe.wait_ge(evict[b], u)

        def made(ins, key):
            ins.then_inc(full[PLAN[key][0]], 1)

        def wait_made(e, key):
            b, u = PLAN[key]
            e.wait_ge(full[b], u + 1)

        def taken(ins, key):
            ins.then_inc(evict[PLAN[key][0]], 1)

        def wait_taken(e, key):
            b, u = PLAN[key]
            e.wait_ge(evict[b], u + 1)

        def barrier(e, n):
            e.drain().then_inc(phase, 1)
            e.wait_ge(phase, 4 * n)

        def hold(e, semaphore, value, passed):
            e.wait_ge(semaphore, value)
            e.sem_inc(passed, 1)

        def bar(l, k):
            return 6 * l + k

        ident = cst[:, C_ID:C_ID + P]
        tri = cst[:, C_TRI:C_TRI + P]
        ones = cst[:, C_ONE:C_ONE + P]

        U_ADA = [0, 1, 2, 3] + [4 + IN_N + k for k in range(8)]
        U_IN = {"uc": 4, "ka": 5, "b": 6, "va": 7, "qa": 8}
        IN_COL = {"qa": 0, "ka": 1, "va": 2, "b": 3, "uc": 4}
        U_OUT = 4 + IN_N + 8

        FRONT, EXPERTS = ring_plan()
        extra = [HT[:].rearrange("p k t -> p (k t)"), area[:, EX_AT:EX_AT + 4096], area[:, EX_AT + 4096:EX_AT + 8192]]

        def unit_of_slot(x):
            return ring[:, x] if x < RING else extra[x - RING].rearrange("p (k n) -> p k n", k=KD)

        def slot(l, n):
            return FRONT[l][n][0]

        def use(l, n):
            return FRONT[l][n][1]

        def arrived(e, l, n):
            e.wait_ge(ring_full[slot(l, n)], 16 * (use(l, n) + 1))

        def expert_slots(l, e):
            return EXPERTS[l][0][e % GROUPS]

        def expert_uses(l, e, x, turn=0):
            return EXPERTS[l][1][x] + e // GROUPS + turn

        w_ada_v = A["w_ada"].rearrange("l (k p) n -> l p k n", p=P)
        w_in_v = A["w_in"].rearrange("l (k p) n -> l p k n", p=P)
        w_out_v = A["w_out"].rearrange("l (k p) n -> l p k n", p=P)
        w13_v = [A[w].rearrange("l e (k p) n -> l e p k n", p=P) for w in ("w1", "w3")]
        w2_v = A["w2"].rearrange("l e (k p) n -> l e p k n", p=P)

        block = ctx.enter_context(nc.Block())

        @block.sync
        def _(sp):
            def load(l, n, src):
                if use(l, n):
                    sp.wait_ge(ring_free[slot(l, n)], use(l, n))
                sp.dma_start(ring[:, slot(l, n)], src).then_inc(ring_full[slot(l, n)], 16)

            sp.dma_start(X[:, 0:2], A["x"].rearrange("b (t p) d -> p (b t) d", p=P)).then_inc(x_in, 16)
            sp.dma_start(X[:, 2:4], A["ctx"].rearrange("b (t p) d -> p (b t) d", p=P)).then_inc(x_in, 16)
            for l in range(DEPTH):
                order = sorted([(U_ADA[j], w_ada_v[l, :, :, j * CHUNK:(j + 1) * CHUNK]) for j in range(ADA_N)]
                               + [(U_IN[s], w_in_v[l, :, :, IN_COL[s] * CHUNK:(IN_COL[s] + 1) * CHUNK]) for s in U_IN]
                               + [(U_OUT + h, w_out_v[l, :, :, h * CHUNK:(h + 1) * CHUNK]) for h in range(OUT_N)],
                               key=lambda x: x[0])
                for n, src in order:
                    load(l, n, src)
                def load_expert(e, turn, at_e):
                    for w, x in enumerate(expert_slots(l, e)):
                        n = expert_uses(l, e, x, turn)
                        if not (isinstance(turn, int) and e < 2):
                            y, ey = (expert_slots(l, e - 1)[w + 1], e - 1) if w < 2 else (expert_slots(l, e)[0], e)
                            hold(sp, ring_full[y], 16 * expert_uses(l, ey, y, turn) + 16, sp_passed)
                        if not isinstance(n, int) or n > 0:
                            hold(sp, ring_free[x], n, sp_passed)
                        src = w13_v[w][l, bass.ds(at_e, 1)].squeeze(0) if w < 2 else w2_v[l, bass.ds(at_e, 1)].squeeze(0)
                        dst = unit_of_slot(x)
                        if w == 2:
                            dst = dst.rearrange("p k n -> p (k n)").rearrange("p (k n) -> p k n", k=4)
                        sp.dma_start(dst, src).then_inc(ring_full[x], 16)

                for e in range(GROUPS + 1):
                    if e == 2:
                        sp.wait_ge(phase, 4 * bar(l, 4))
                        sp.wait_ge(h2_out[l], 16 * (routed(l) // P))
                    load_expert(e, 0, e)
                with sp.Fori(1, (E_N - 1) // GROUPS) as i:
                    for q in range(GROUPS):
                        load_expert(1 + q, i, 3 * i + 1 + q)

        @block.gpsimd
        def _(pool):
            g = nc.gpsimd
            chain = [0]

            def link(ins):
                chain[0] += 1
                ins.then_inc(pool_chain, 1)
                pool.wait_ge(pool_chain, chain[0])

            g.memset(half[:], -0.5)
            g.memset(SC[:], 0.0)
            sv = SI.rearrange("p (r w) -> p r w", w=4)
            link(g.memset(sv, 0))
            g.memset(sv[:, :, 0:2], NO_ROW)
            pool.drain().then_inc(setup, 1)
            pool.wait_ge(setup, 1)
            for l in range(DEPTH):
                pool.dma_start(slotD[l].rearrange("(p r) w -> p (r w)", p=SLOT), SI[0:SLOT, :]).then_inc(si_out, 16)

            def rsqrt(out, s_, m_, n):
                link(g.tensor_scalar(m_, s_, 1.0 / n, EPS, ALU.mult, ALU.add))
                return g.tensor_tensor(out, m_, half[:].to_broadcast(list(out.shape)), ALU.pow)

            for l in range(DEPTH):
                nq = TILES if l == 0 else 2
                conds = 2 if l == 0 else 1

                def load_bias(dst, q):
                    for j in range(4):
                        col = (4 * q + j) * CHUNK
                        pool.dma_start(dst[32 * j:32 * j + 32, :],
                                       A["b_ada"][l:l + 1, col:col + CHUNK].broadcast_to([32, CHUNK])).then_inc(bias_in[l], 16)

                def store_mod(src, q):
                    pool.wait_ge(mod_sb[l], q + 1)
                    for j in range(4):
                        col = (4 * q + j) * CHUNK
                        pool.dma_start(modD[l, :, col:col + CHUNK], src[32 * j:32 * j + 2, :]).then_inc(mod_out[l][q], 16)

                load_bias(bias0, 0)
                pool.wait_ge(ss_done, l + 1)
                rsqrt(rstd[:, 0:TILES], ss[:], ms[:], D).then_inc(rs_done, 1)
                store_mod(mst0, 0)
                pool.wait_ge(mod_out[l][0], 64)
                for cnd in range(2):
                    pool.dma_start(MR[16 * cnd:16 * cnd + 16, :],
                                   modD[l, cnd, 0:2 * D].rearrange("(r n) -> r n", n=P)).then_inc(mrow_in[l], 16)
                if l == 0:
                    pool.wait_ge(si_out, 32)
                barrier(pool, bar(l, 1))
                g.memset(zpad[:, :, :, 0:PADC], 0.0)
                g.memset(zpad[:, :, :, PADC + S_LAT:], 0.0).then_inc(pads, 1)
                load_bias(bias12[:, 0], 1)
                load_bias(bias12[:, 1], 2)
                store_mod(mst, 1)
                store_mod(mst, 2)
                for q in (1, 2):
                    pool.wait_ge(mod_out[l][q], 64)
                barrier(pool, bar(l, 2))
                for cnd in range(conds):
                    pool.dma_start(gate[:, cnd], modD[l, cnd:cnd + 1, 2 * D:3 * D].broadcast_to([P, D])).then_inc(gate_in[l], 16)
                for i in range(nq):
                    pool.wait_ge(o_ss[l], i + 1)
                    rsqrt(rs4[:, i % 2], ss4[:, i % 2], ms4[:, i % 2], 2 * HD).then_inc(o_rs[l], 1)
                barrier(pool, bar(l, 3))
                for cnd in range(conds):
                    for v in range(2):
                        pool.dma_start(BC[:, cnd, v], modD[l, cnd:cnd + 1, (3 + v) * D:(4 + v) * D].broadcast_to([P, D])).then_inc(bc_in[l], 16)
                pool.dma_start(GF, A["g_ffn"][l:l + 1, :].broadcast_to([P, D])).then_inc(bc_in[l], 16)
                for i in range(nq):
                    pool.wait_ge(ss2[l], i + 1)
                    rsqrt(rstd[:, i:i + 1], ss[:, i:i + 1], ms[:, i:i + 1], D).then_inc(rs2[l], 1)
                pool.wait_ge(pl_done, l + 1)
                for k in range(2):
                    for i in range(nq):
                        pool.indirect_dma_start(slotD[l], bass.IndirectOffsetOnAxis(ap=ROWI[:, k, i:i + 1], axis=0),
                                                PLi[:, k, i, :], None).then_inc(slot_out[l], 16)
                pool.wait_ge(slot_out[l], 16 * 2 * nq)
                pool.dma_start(TBi[0:SLOT, :], slotD[l].rearrange("(p r) w -> p (r w)", p=SLOT)).then_inc(tb_in[l], 16)
                barrier(pool, bar(l, 4))
                for cnd in range(conds):
                    pool.dma_start(gate[:, cnd], modD[l, cnd:cnd + 1, 5 * D:6 * D].broadcast_to([P, D])).then_inc(gate_in[l], 16)
                g.memset(DR[0:SLOT, :], NO_ROW)
                g.memset(ym[0:SLOT, :], 0.0)
                g.memset(xg[0:SLOT, :], 0.0)
                pool.drain().then_inc(init_m, 1)
                pool.wait_ge(tb_in[l], 16)
                pool.wait_ge(h2_out[l], 16 * nq)
                done = pool.alloc_register(f"pool_blocks_{l}")
                pool.reg_mov(done, 0)

                def scatter(b):
                    g.tensor_copy(sidx[0:SLOT, :], DR[0:SLOT, bass.ds((b + 2) % 4, 1)]).then_inc(sidx_set[l], 1)
                    hold(pool, sidx_set[l], b + 1, pool_passed)
                    pool.indirect_dma_start(yD[l], bass.IndirectOffsetOnAxis(ap=sidx[0:SLOT, :], axis=0), ym[0:SLOT, :], None,
                                            bounds_check=2 * routed(l) - 1, oob_is_err=False).then_inc(scat[l], 16)

                def step(col):
                    b = pool.snap(done)
                    hold(pool, xt_full[l], b + 1, pool_passed)
                    pool.reg_add(done, done, 1)
                    g.tensor_copy(gidx[0:SLOT, :], TBi[0:SLOT, bass.ds(4 * col, 1)]).then_inc(gidx_set[l], 1)
                    g.tensor_copy(DR[0:SLOT, bass.ds(b % 4, 1)], TBi[0:SLOT, bass.ds(4 * col + 1, 1)]).then_inc(gidx_set[l], 1)
                    hold(pool, gidx_set[l], 2 * b + 2, pool_passed)
                    pool.indirect_dma_start(xg[0:SLOT, :], None, h2D[l], bass.IndirectOffsetOnAxis(ap=gidx[0:SLOT, :], axis=0),
                                            bounds_check=routed(l) - 1, oob_is_err=False).then_inc(gath[l], 16)
                    hold(pool, y_rdy[l], b + 1, pool_passed)
                    scatter(b)

                with pool.Fori(0, E_N) as e:
                    blocks = pool.value_load(nb[0:1, bass.ds(e, 1)], min_val=0, max_val=JMAX)
                    step(e * JMAX)
                    with pool.If(blocks > 1):
                        with pool.Fori(1, blocks) as j:
                            step(e * JMAX + j)
                b = pool.snap(done)
                hold(pool, y_rdy[l], b + 1, pool_passed)
                scatter(b)
                hold(pool, y_rdy[l], b + 2, pool_passed)
                scatter(b + 1)
                hold(pool, scat[l], 16 * b + 32, pool_passed)
                barrier(pool, bar(l, 5))
                y_v = yD[l].rearrange("(k t p) d -> p k t d", k=2, p=P)
                for a in range(nq // 2):
                    if a:
                        pool.wait_ge(comb[l], 2 * a)
                    for k in range(2):
                        for c2 in range(2):
                            pool.dma_start(Y[:, k, c2], y_v[:, k, 2 * a + c2]).then_inc(y_in[l], 16)
                if l == DEPTH - 1:
                    pool.dma_start(GFIN, A["g_final"].rearrange("(a n) -> a n", a=1).broadcast_to([P, D])).then_inc(fin_g, 16)
                    pool.wait_ge(fin_ss, 1)
                    rsqrt(rstd[:, 0:2], ss[:, 0:2], ms[:, 0:2], D).then_inc(fin_rs, 1)
                barrier(pool, bar(l, 6))

        @block.scalar
        def _(act):
            s = nc.scalar
            act.dma_start(cst[:], A["cst"]).then_inc(cst_in, 16)
            small = 0

            def par(dst, src):
                act.dma_start(dst, src).then_inc(par_in, 16)

            par(CR[0:8, :], A["c"].rearrange("b (r n) -> (b r) n", n=P))
            par(CR[8:16, :], A["c_ctx"].rearrange("(r n) -> r n", n=P))
            for l in range(DEPTH):
                r0 = 15 * l
                for at_, name, rows in ((0, "g_mix", 8), (8, "diff_norm_g", 1), (9, "conv_b", 2), (11, "conv_ln_g", 2), (13, "conv_ln_b", 2)):
                    par(PR[r0 + at_:r0 + at_ + rows, :], A[name][l].rearrange("(r n) -> r n", n=P))
            par(CWR[0:DEPTH * KCONV, :], A["conv_w"].rearrange("l k c -> (l k) c"))
            par(DL.rearrange("p l a d -> p (l a d)"),
                A["diff_lambda"].rearrange("l a d -> (l a d)").rearrange("(o n) -> o n", o=1).broadcast_to([P, DEPTH * 4 * HD]))
            par(rw[:], A["router_w"].rearrange("(k p) e -> p k e", p=P))
            par(rb[:], A["router_bias"].rearrange("(o n) -> o n", o=1).broadcast_to([P, E_N]))
            par(sink[:].rearrange("p l h -> p (l h)"), A["attn_sink"].rearrange("l h -> (l h)").rearrange("(o n) -> o n", o=1).broadcast_to([P, DEPTH * 4]))
            act.wait_ge(par_in, 16 * N_PAR)
            s.activation(CRS[0:16, :], CR[0:16, :], ACT.Silu).then_inc(c_silu, 1)
            act.wait_ge(lam_sum, 1)
            s.activation(lamx[:], lamx[:], ACT.Exp).then_inc(lam_exp, 1)

            for l in range(DEPTH):
                nq = TILES if l == 0 else 2
                n_ln = TOK if l == 0 else S_LAT
                if l == 0:
                    act.wait_ge(x_in, 32)
                for t in range(TILES):
                    last = s.activation(YS[:, t], X[:, t], ACT.Square, accum_out=ss[:, t:t + 1])
                last.then_inc(ss_done, 1)
                act.wait_ge(ab_done, l + 1)
                for q in range(1, 8, 2):
                    key = ("nT", l, q)
                    wait_made(act, key)
                    cnd, kk = q // 4, 2 * (q % 4)
                    for a in range(2):
                        last = s.activation(HT[:, kk + a, cnd * 256:cnd * 256 + 256], bank(key)[:, a * 256:a * 256 + 256], ACT.Identity,
                                            bias=AB[:, cnd, 0, kk + a:kk + a + 1], scale=AB[:, cnd, 1, kk + a:kk + a + 1])
                    taken(last, key)
                barrier(act, bar(l, 1))

                staged = [j for j in in_jobs(l) if j[0] in ("ka", "b", "qa")]

                def st_free(job):
                    k = staged.index(job)
                    if k >= 2:
                        wait_made(act, ("inT", l) + staged[k - 2])

                def copy_T(job):
                    seg, t = job
                    key = ("inT", l) + job
                    wait_made(act, key)
                    src = bank(key).rearrange("p (b t) -> p b t", b=4)
                    cols = slice(t * P, (t + 1) * P)
                    if seg == "b":
                        if t < 2 or l == 0:
                            s.activation(qT[:, 4:6, cols], src[:, 0:2], ACT.Identity)
                        last = s.activation(kT[:, 4:6, cols], src[:, 2:4], ACT.Identity)
                    else:
                        last = s.activation((qT if seg == "qa" else kT)[:, 0:4, cols], src, ACT.Identity)
                    taken(last, key)

                prev = None
                for job in in_jobs(l):
                    seg, t = job
                    key = ("in", l) + job
                    stg = ST[:, staged.index(job) % 2] if job in staged else None
                    if seg == "uc" and t >= 2:
                        wait_made(act, key)
                        taken(s.activation(G[:, t - 2, 0:n_ln], bank(key)[:, 0:n_ln], ACT.Exp, scale=-1.0), key)
                        if t == 3:
                            act.drain().then_inc(g_exp, 1)
                    elif seg == "va":
                        wait_made(act, key)
                        taken(s.activation(V[:, t, 0:512], bank(key), ACT.Identity), key)
                    elif seg in ("ka", "qa") and t >= 2:
                        wait_made(act, key)
                        st_free(job)
                        taken(s.activation(stg, bank(key), ACT.Identity), key)
                    elif seg == "b" and t >= 2:
                        wait_made(act, key)
                        st_free(job)
                        if l == 0:
                            s.activation(stg[:, 0:256], bank(key)[:, 0:256], ACT.Identity)
                        for a in range(2):
                            s.activation(stg[:, 256 + a * 64:].rearrange("p (j d) -> p j d", d=64)[:, 0::2],
                                         bank(key)[:, 256:384].rearrange("p (j d) -> p j d", d=64), ACT.Identity)
                        taken(s.activation(V[:, t, 512:640], bank(key)[:, 384:512], ACT.Identity), key)
                    if prev:
                        copy_T(prev)
                    prev = job if job in staged else None
                if prev:
                    copy_T(prev)
                act.wait_ge(ln_d, l + 1)
                s.activation(G[:, :, 0:n_ln], acc[:, :, 0:n_ln], ACT.Square).then_inc(ln_sq, 1)
                act.wait_ge(ln_v, l + 1)
                s.activation(G[:, 1, 0:n_ln], G[:, 0, 0:n_ln], ACT.Sqrt).then_inc(ln_r, 1)
                act.wait_ge(ln_n, l + 1)
                for c2 in range(2):
                    last = s.activation(G[:, c2, 0:n_ln], acc[:, c2, 0:n_ln], ACT.Exp, bias=NC[:, l, 2 + c2:3 + c2], scale=NC[:, l, c2:c2 + 1])
                last.then_inc(ln_e, 1)
                barrier(act, bar(l, 2))

                units, tj = units_of(l), t_jobs(l)

                def exps(n):
                    i, u = units[n]
                    kw = TOK if i < 2 else S_CTX
                    b = n % 2
                    act.wait_ge(nm_done[l], n + 1)
                    if u < BLK_A:
                        prior = [k for k, (a, _) in enumerate(tj) if a == n - 2]
                        if prior:
                            wait_made(act, ("T", l, prior[-1]))
                        for m in range(2):
                            key = ("S", l, n, m)
                            taken(s.activation(PB[:, b, m, 0:kw], bank(key)[:, 0:kw], ACT.Exp, bias=nm[:, b, m:m + 1], scale=HD ** -0.5,
                                               accum_out=sums[:, b, m:m + 1]), key)
                    else:
                        for m in range(2):
                            h = 2 * (u - BLK_A) + m
                            s.activation(es[:, b, m:m + 1], sink[:, l, h:h + 1], ACT.Exp, bias=nm[:, b, m:m + 1])
                            last = s.activation(PB[:, b, m, 0:kw], PB[:, b, m, 0:kw], ACT.Exp, bias=nm[:, b, m:m + 1],
                                                accum_out=sums[:, b, m:m + 1])
                        last.then_inc(ex_done[l], 1)

                def copy_aT(k):
                    n, m = tj[k]
                    kw = TOK if units[n][0] < 2 else S_CTX
                    key = ("T", l, k)
                    wait_made(act, key)
                    if k >= 2:
                        wait_made(act, ("O", l, k - 2))
                    taken(s.activation(aT[:, k % 2, 0:kw], bank(key)[:, 0:kw], ACT.Identity), key)

                def mixed(i):
                    cols = slice(i * P, (i + 1) * P)
                    wait_made(act, ("MA", l, i))
                    taken(s.activation(HT[:, 0:4, cols], bank(("MA", l, i)).rearrange("p (b t) -> p b t", b=4), ACT.Identity,
                                       scale=NC[:, l, 4:5]), ("MA", l, i))
                    wait_made(act, ("MB", l, i))
                    taken(s.activation(HT[:, 4:6, cols], bank(("MB", l, i))[:, 0:256].rearrange("p (b t) -> p b t", b=2), ACT.Identity), ("MB", l, i))

                exps(0)
                exps(1)
                for st_ in attention_steps(l):
                    if st_[0] == "T":
                        copy_aT(st_[1])
                        n, m = tj[st_[1]]
                        if n + 2 < len(units) and m == (0 if units[n][1] < BLK_A else 1):
                            exps(n + 2)
                    elif st_[0] == "M":
                        mixed(st_[1])
                barrier(act, bar(l, 3))

                def second(i):
                    act.wait_ge(x_add[l], i + 1)
                    s.activation(H2[:, i], X[:, i], ACT.Square, accum_out=ss[:, i:i + 1]).then_inc(ss2[l], 1)

                def route(i):
                    act.wait_ge(h2_done[l], i + 1)
                    act.dma_start(h2D[l].rearrange("(t p) d -> t p d", p=P)[i], H2[:, i]).then_inc(h2_out[l], 16)
                    for h in range(2):
                        key = ("h2T", l, i, h)
                        wait_made(act, key)
                        if i:
                            wait_made(act, ("rt", l, i - 1))
                        taken(s.activation(hTr[:, 4 * h:4 * h + 4], bank(key).rearrange("p (b t) -> p b t", b=4), ACT.Identity), key)
                    key = ("rt", l, i)
                    wait_made(act, key)
                    taken(s.activation(e_t[:, i], bank(key)[:, 0:E_N], ACT.Exp, scale=-1.0), key)

                for i in range(nq):
                    second(i)
                    if i:
                        route(i - 1)
                route(nq - 1)
                act.drain().then_inc(h2_done[l], 1)
                barrier(act, bar(l, 4))

                act.wait_ge(nb_ready, l + 1)
                done = act.alloc_register(f"act_blocks_{l}")
                act.reg_mov(done, 0)

                def step():
                    b = act.snap(done)
                    act.wait_ge(w13_full[l], b + 1)
                    s.activation(sg[0:SLOT, :], ps[0:SLOT, B_W13, :], ACT.Silu).then_inc(si_rdy[l], 1)
                    act.reg_add(done, done, 1)

                with act.Fori(0, E_N) as e:
                    blocks = act.value_load(nb[0:1, bass.ds(e, 1)], min_val=0, max_val=JMAX)
                    step()
                    with act.If(blocks > 1):
                        with act.Fori(1, blocks):
                            step()
                barrier(act, bar(l, 5))
                if l == DEPTH - 1:
                    for i in range(2):
                        act.wait_ge(comb[l], i + 1)
                        last = s.activation(area[:, 8192 + i * D:8192 + (i + 1) * D], X[:, i], ACT.Square, accum_out=ss[:, i:i + 1])
                    last.then_inc(fin_ss, 1)
                    for i in range(2):
                        act.wait_ge(fin_o, i + 1)
                        act.dma_start(A["out"].rearrange("b (t p) d -> p (b t) d", p=P)[:, i], X[:, i]).then_inc(stored, 16)
                    act.wait_ge(stored, 32)
                barrier(act, bar(l, 6))

        @block.vector
        def _(dve):
            v = nc.vector
            for key, dst, cols in (("par", PC[:].rearrange("p l a -> p (l a)"), DEPTH * 15), ("cw", None, 0), ("c", None, 0)):
                wait_made(dve, (key,))
                if key == "par":
                    taken(v.tensor_copy(dst, bank((key,))[:, 0:cols]), (key,))
                elif key == "cw":
                    taken(v.tensor_copy(CW[:].rearrange("p c k -> p (c k)"), bank((key,))[:, 0:2 * DEPTH * KCONV]), (key,))
                else:
                    dve.wait_ge(setup, 1)
                    taken(v.tensor_copy(SC[:, :, 0:2], bank((key,))[:, 0:16].rearrange("p (c k) -> p k c", c=2)), (key,))
            dve.drain()
            for l in range(DEPTH):
                v.tensor_scalar(NC[:, l, 0:4], PC[:, l, 11:15], -1.0, None, ALU.mult)
                v.tensor_scalar(NC[:, l, 4:5], PC[:, l, 8:9], 1.0 - lambda_init(l), None, ALU.mult)
            dve.wait_ge(par_in, 16 * N_PAR)
            v.tensor_tensor(DLP, DL[:, :, 0::2], DL[:, :, 1::2], ALU.mult)
            dve.drain()
            v.tensor_reduce(lamx[:], DLP, AX.X, ALU.add).then_inc(lam_sum, 1)
            dve.wait_ge(lam_exp, 1)
            for l in range(DEPTH):
                v.scalar_tensor_tensor(neglam[:, l:l + 1], lamx[:, l, 1:2], -lambda_init(l), lamx[:, l, 0:1], ALU.add, ALU.subtract)
            dve.drain()

            for l in range(DEPTH):
                nq = TILES if l == 0 else 2
                conds = nq // 2
                n_ln = TOK if l == 0 else S_LAT
                n_seq = conds

                def mod_rows(q, bias, dst):
                    key = ("ada", l, q)
                    wait_made(dve, key)
                    dve.wait_ge(bias_in[l], 64 * (1 if q == 0 else 3))
                    if q == 2:
                        dve.wait_ge(mod_out[l][1], 64)
                    taken(v.tensor_tensor(dst, bank(key), bias, ALU.add), key)
                    dve.drain().then_inc(mod_sb[l], 1)

                dve.wait_ge(rs_done, l + 1)
                for t in range(TILES):
                    last = v.tensor_scalar(YS[:, t], X[:, t], rstd[:, t:t + 1], None, ALU.mult)
                last.then_inc(y_done, 1)
                mod_rows(0, bias0, mst0)
                key = ("modc", l)
                wait_made(dve, key)
                taken(v.tensor_copy(MCOL[:].rearrange("p c v k -> p (c v k)"), bank(key)[:, 0:32]), key)
                dve.drain()
                v.tensor_copy(AB[:, :, 0], MCOL[:, :, 0])
                v.scalar_tensor_tensor(AB[:, :, 1], MCOL[:, :, 1], 1.0, PC[:, l, 0:8].unsqueeze(1).to_broadcast([P, 2, KD]), ALU.add, ALU.mult)
                dve.drain().then_inc(ab_done, 1)
                for q in range(0, 8, 2):
                    key = ("nT", l, q)
                    wait_made(dve, key)
                    cnd, kk = q // 4, 2 * (q % 4)
                    for a in range(2):
                        last = v.tensor_scalar(HT[:, kk + a, cnd * 256:cnd * 256 + 256], bank(key)[:, a * 256:a * 256 + 256],
                                               AB[:, cnd, 1, kk + a:kk + a + 1], AB[:, cnd, 0, kk + a:kk + a + 1], ALU.mult, ALU.add)
                    taken(last, key)
                barrier(dve, bar(l, 1))

                staged = [j for j in in_jobs(l) if j[0] in ("ka", "b", "qa")]

                def conv_taps():
                    for k in range(KCONV):
                        for c2 in range(2):
                            src = zpad[:, c2, 0:n_seq, k:k + S_LAT]
                            dst = acc[:, c2, 0:n_ln].rearrange("p (s t) -> p s t", s=n_seq)
                            w = CW[:, c2, l * KCONV + k:l * KCONV + k + 1]
                            if k == 0:
                                v.tensor_scalar(dst, src, w, PC[:, l, 9 + c2:10 + c2], ALU.mult, ALU.add)
                            else:
                                v.scalar_tensor_tensor(dst, src, w, dst, ALU.mult, ALU.add)
                            if c2 == 1:
                                dve.drain()
                            yield

                taps = conv_taps()

                def conv(n):
                    for _ in range(n):
                        next(taps, None)

                def rope(job, n_heads, outs):
                    key = ("in", l) + job
                    t = job[1]
                    w = n_heads * HD
                    cosv = cst[:, C_ROPE + t * 128:C_ROPE + t * 128 + 64].unsqueeze(1).to_broadcast([P, n_heads, 64])
                    x_ = bank(key)[:, 0:w]
                    v.tensor_tensor(RT[:, 0, 0:w].rearrange("p (h d) -> p h d", d=64), x_.rearrange("p (h d) -> p h d", d=64), cosv, ALU.mult)
                    xs = x_.rearrange("p (h a f) -> p h a f", a=4, f=16)
                    r1 = RT[:, 1, 0:w].rearrange("p (h a f) -> p h a f", a=4, f=16)
                    sn = cst[:, C_ROPE + t * 128 + 64:C_ROPE + t * 128 + 128].rearrange("p (a f) -> p a f", f=16).unsqueeze(1)
                    for hh in range(2):
                        v.tensor_tensor(r1[:, :, hh::2], xs[:, :, 1 - hh::2], sn[:, :, hh::2].to_broadcast([P, n_heads, 2, 16]), ALU.mult)
                    dve.drain()
                    last = None
                    for dst, c0, c1 in outs:
                        a0, a1 = RT[:, 0, c0:c1], RT[:, 1, c0:c1]
                        if len(dst.shape) == 3:
                            a0, a1 = (a_.rearrange("p (j d) -> p j d", d=64) for a_ in (a0, a1))
                        last = v.tensor_tensor(dst, a0, a1, ALU.add)
                    return last

                dve.wait_ge(pads, l + 1)
                plan_taps = iter((10, 10, 24, 8, 6, 8))
                for job in in_jobs(l):
                    seg, t = job
                    key = ("in", l) + job
                    if seg == "uc" and t < 2:
                        if t == 0:
                            dve.wait_ge(g_exp, l + 1)
                            v.tensor_scalar(G[:, :, 0:n_ln], G[:, :, 0:n_ln], 1.0, None, ALU.add)
                            dve.drain()
                            v.reciprocal(G[:, :, 0:n_ln], G[:, :, 0:n_ln])
                            dve.drain()
                        wait_made(dve, key)
                        taken(v.tensor_tensor(zpad[:, t, 0:n_seq, PADC:PADC + S_LAT], bank(key)[:, 0:n_ln].rearrange("p (s t) -> p s t", s=n_seq),
                                              G[:, t, 0:n_ln].rearrange("p (s t) -> p s t", s=n_seq), ALU.mult), key)
                        if t == 1:
                            dve.drain()
                    elif seg in ("ka", "b", "qa") and t < 2:
                        conv(next(plan_taps))
                        wait_made(dve, key)
                        k = staged.index(job)
                        if k >= 2:
                            wait_made(dve, ("inT", l) + staged[k - 2])
                        stg = ST[:, k % 2]
                        if seg == "b":
                            v.tensor_copy(V[:, t, 512:640], bank(key)[:, 384:512])
                            dup = [stg[:, 256 + a * 64:].rearrange("p (j d) -> p j d", d=64)[:, 0::2] for a in range(2)]
                            last = rope(job, 6, [(stg[:, 0:256], 0, 256), (dup[0], 256, 384), (dup[1], 256, 384)])
                        else:
                            last = rope(job, 8, [(stg, 0, 512)])
                        taken(last, key)
                conv(2 * KCONV)
                dve.drain().then_inc(cv_d, 1)
                key = ("mu", l)
                wait_made(dve, key)
                for c2 in range(2):
                    last = v.scalar_tensor_tensor(acc[:, c2, 0:n_ln], bank(key)[:, 0:n_ln], -1.0 / CH, acc[:, c2, 0:n_ln], ALU.mult, ALU.add)
                taken(last, key)
                dve.drain().then_inc(ln_d, 1)
                mod_rows(1, bias12[:, 0], mst)
                key = ("var", l)
                wait_made(dve, key)
                taken(v.tensor_scalar(G[:, 0, 0:n_ln], bank(key)[:, 0:n_ln], 1.0 / CH, EPS, ALU.mult, ALU.add), key)
                dve.drain().then_inc(ln_v, 1)
                dve.wait_ge(ln_r, l + 1)
                v.reciprocal(G[:, 1, 0:n_ln], G[:, 1, 0:n_ln])
                dve.drain()
                for c2 in range(2):
                    last = v.tensor_tensor(acc[:, c2, 0:n_ln], acc[:, c2, 0:n_ln], G[:, 1, 0:n_ln], ALU.mult)
                last.then_inc(ln_n, 1)
                mod_rows(2, bias12[:, 1], mst)
                dve.wait_ge(ln_e, l + 1)
                v.tensor_scalar(G[:, :, 0:n_ln], G[:, :, 0:n_ln], 1.0, None, ALU.add)
                for c2 in range(2):
                    v.tensor_scalar(acc[:, c2, 0:n_ln], acc[:, c2, 0:n_ln], PC[:, l, 11 + c2:12 + c2], PC[:, l, 13 + c2:14 + c2], ALU.mult, ALU.add)
                dve.drain()
                v.reciprocal(G[:, :, 0:n_ln], G[:, :, 0:n_ln])
                dve.drain()
                wait_made(dve, ("in", l) + in_jobs(l)[-1])
                v.tensor_tensor(HT[:, 6:8, 0:n_ln], acc[:, :, 0:n_ln], G[:, :, 0:n_ln], ALU.mult)
                barrier(dve, bar(l, 2))

                units, tj = units_of(l), t_jobs(l)

                def maxima(n):
                    i, u = units[n]
                    kw = TOK if i < 2 else S_CTX
                    b = n % 2
                    pair = ps[:, 2 * b:2 * b + 2, :]
                    for m in range(2):
                        wait_made(dve, ("S", l, n, m))
                    if u < BLK_A:
                        v.tensor_reduce(mx[:, b], pair[:, :, 0:kw], AX.X, ALU.max)
                        dve.drain()
                        v.tensor_scalar(nm[:, b], mx[:, b], -HD ** -0.5, None, ALU.mult).then_inc(nm_done[l], 1)
                        return
                    prior = [k for k, (a, _) in enumerate(tj) if a == n - 2]
                    wait_made(dve, ("T", l, prior[-1]))
                    for m in range(2):
                        if i < 2:
                            v.scalar_tensor_tensor(PB[:, b, m, 0:256], pair[:, m, 0:256], HD ** -0.5,
                                                   cst[:, C_MASK + i * 256:C_MASK + (i + 1) * 256], ALU.mult, ALU.add)
                        last = v.tensor_scalar(PB[:, b, m, kw - 256:kw], pair[:, m, kw - 256:kw], HD ** -0.5, None, ALU.mult)
                        taken(last, ("S", l, n, m))
                    dve.drain()
                    v.tensor_reduce(mx[:, b], PB[:, b, :, 0:kw], AX.X, ALU.max)
                    dve.drain()
                    h = 2 * (u - BLK_A)
                    v.tensor_tensor(mx[:, b], mx[:, b], sink[:, l, h:h + 2], ALU.max)
                    dve.drain()
                    v.tensor_scalar(nm[:, b], mx[:, b], -1.0, None, ALU.mult).then_inc(nm_done[l], 1)

                def probs(n):
                    i, u = units[n]
                    kw = TOK if i < 2 else S_CTX
                    b = n % 2
                    if u < BLK_A:
                        wait_taken(dve, ("S", l, n, 1))
                        v.reciprocal(rec[:, n % 4], sums[:, b])
                        dve.drain()
                        v.scalar_tensor_tensor(cf[:, b:b + 1], sums[:, b, 0:1], neglam[:, l:l + 1], rec[:, n % 4, 1:2], ALU.mult, ALU.mult)
                        dve.drain()
                        v.scalar_tensor_tensor(PB[:, b, 0, 0:kw], PB[:, b, 1, 0:kw], cf[:, b:b + 1], PB[:, b, 0, 0:kw], ALU.mult, ALU.add).then_inc(pr_done[l], 1)
                    else:
                        dve.wait_ge(ex_done[l], sum(1 for _, x_ in units[:n + 1] if x_ >= BLK_A))
                        v.tensor_tensor(sums[:, b], sums[:, b], es[:, b], ALU.add)
                        dve.drain()
                        v.reciprocal(rec[:, n % 4], sums[:, b]).then_inc(pr_done[l], 1)

                def take_o(k):
                    n, m = tj[k]
                    i, u = units[n]
                    key = ("O", l, k)
                    wait_made(dve, key)
                    if u == 0 and i >= 2:
                        wait_made(dve, ("MB", l, i - 2))
                    w = P if u < BLK_A else HD
                    taken(v.tensor_scalar(O[i % 2][:, u * P + m * HD:u * P + m * HD + w], bank(key)[:, 0:w], rec[:, n % 4, m:m + 1], None, ALU.mult), key)
                    if u == BLK - 1 and m == 1:
                        dve.drain()
                        v.tensor_tensor(G[:, 0], O[i % 2][:, 0:512], O[i % 2][:, 0:512], ALU.mult)
                        dve.drain()
                        v.tensor_reduce(ss4[:, i % 2], G[:, 0].rearrange("p (h d) -> p h d", h=4), AX.X, ALU.add).then_inc(o_ss[l], 1)

                def head_norm(i):
                    dve.wait_ge(o_rs[l], i + 1)
                    oa = O[i % 2][:, 0:512].rearrange("p (h d) -> p h d", h=4)
                    v.tensor_tensor(oa, oa, rs4[:, i % 2].unsqueeze(2).to_broadcast([P, 4, P]), ALU.mult).then_inc(o_done[l], 1)

                maxima(0)
                maxima(1)
                for st_ in attention_steps(l):
                    if st_[0] == "T" and tj[st_[1]][1] == 0:
                        n = tj[st_[1]][0]
                        probs(n)
                        if n + 2 < len(units):
                            maxima(n + 2)
                    elif st_[0] == "O":
                        take_o(st_[1])
                    elif st_[0] == "M":
                        head_norm(st_[1])
                barrier(dve, bar(l, 3))

                def add_out(i):
                    cnd = i // 2
                    if i == 0:
                        dve.wait_ge(gate_in[l], 16 * conds)
                    for h in range(OUT_N):
                        key = ("wo", l, i, h)
                        wait_made(dve, key)
                        taken(v.tensor_tensor(tmp[:, h], bank(key), gate[:, cnd, h * CHUNK:(h + 1) * CHUNK], ALU.mult), key)
                    dve.drain()
                    v.tensor_tensor(X[:, i], X[:, i], tmp.rearrange("p b k -> p (b k)"), ALU.add)
                    dve.drain().then_inc(x_add[l], 1)

                def make_h2(i):
                    cnd = i // 2
                    dve.wait_ge(rs2[l], i + 1)
                    v.scalar_tensor_tensor(H2[:, i], X[:, i], rstd[:, i:i + 1], BC[:, cnd, 1], ALU.mult, ALU.mult)
                    dve.drain()
                    v.tensor_tensor(H2[:, i], H2[:, i], BC[:, cnd, 0], ALU.add).then_inc(h2_done[l], 1)

                dve.wait_ge(bc_in[l], 16 * (2 * conds + 1))
                for cnd in range(conds):
                    v.scalar_tensor_tensor(BC[:, cnd, 1], BC[:, cnd, 1], 1.0, GF, ALU.add, ALU.mult)
                dve.drain()
                for i in range(nq):
                    add_out(i)
                    if i:
                        make_h2(i - 1)
                make_h2(nq - 1)

                def T3(x_, n=E_N):
                    return x_[:, 0:nq]

                def over(x_, n):
                    return x_[:, 0:nq].unsqueeze(2).to_broadcast([P, nq, n])

                def consts(c0, n):
                    return cst[:, c0:c0 + n].unsqueeze(1).to_broadcast([P, nq, n])

                dve.wait_ge(h2_done[l], nq + 1)
                v.tensor_scalar(T3(e_s), T3(e_t), 1.0, None, ALU.add)
                dve.drain()
                v.reciprocal(T3(e_s), T3(e_s))
                dve.drain()
                v.tensor_tensor(T3(e_b), T3(e_s), rb[:].unsqueeze(1).to_broadcast([P, nq, E_N]), ALU.add)
                dve.drain()
                four = T3(e_b).rearrange("p t (g e) -> p (t g) e", e=4)
                ng = nq * E_G
                for a in range(2):
                    for o_, op in ((0, ALU.max), (1, ALU.min)):
                        v.tensor_tensor(hl[:, 2 * o_ + a, 0:ng], four[:, :, 2 * a], four[:, :, 2 * a + 1], op)
                dve.drain()
                gv = T3(grp).rearrange("p t g -> p (t g)")
                v.tensor_tensor(gv, hl[:, 0, 0:ng], hl[:, 1, 0:ng], ALU.max)
                v.tensor_tensor(T3(geq).rearrange("p t g -> p (t g)"), hl[:, 0, 0:ng], hl[:, 1, 0:ng], ALU.min)
                v.tensor_tensor(T3(gcd).rearrange("p t g -> p (t g)"), hl[:, 2, 0:ng], hl[:, 3, 0:ng], ALU.max)
                dve.drain()
                v.tensor_tensor(T3(geq), T3(geq), T3(gcd), ALU.max)
                dve.drain()
                v.tensor_tensor(T3(grp), T3(grp), T3(geq), ALU.add)
                dve.drain()

                def first_max(val, n, c_iota, mxv, eq, cand, low, out):
                    v.tensor_reduce(mxv[:, 0:nq], T3(val), AX.X, ALU.max)
                    dve.drain()
                    v.tensor_tensor(T3(eq), T3(val), over(mxv, n), ALU.is_ge)
                    dve.drain()
                    v.scalar_tensor_tensor(T3(cand), T3(eq), -float(n), consts(c_iota, n), ALU.mult, ALU.add)
                    dve.drain()
                    v.tensor_reduce(low[:, 0:nq], T3(cand), AX.X, ALU.min)
                    dve.drain()
                    v.tensor_tensor(T3(out), T3(cand), over(low, n), ALU.is_equal)
                    dve.drain()

                first_max(grp, E_G, C_I4, gm, geq, gcd, cm, gone)
                v.tensor_scalar(T3(gneg), T3(gone), BIG, -BIG, ALU.mult, ALU.add)
                e4 = [T3(x_).rearrange("p t (g e) -> p (t g) e", e=4) for x_ in (e_v, e_b)]
                gb = [T3(x_).rearrange("p t g -> p (t g)").unsqueeze(2).to_broadcast([P, ng, 4]) for x_ in (gone, gneg)]
                dve.drain()
                v.tensor_tensor(e4[0], e4[1], gb[0], ALU.mult)
                dve.drain()
                v.tensor_tensor(e4[0], e4[0], gb[1], ALU.add)
                dve.drain()
                first_max(e_v, E_N, C_I16, vm, e_eq, e_t, cmk0, oh[0])
                v.scalar_tensor_tensor(T3(e_v), T3(oh[0]), -3.0 * BIG, T3(e_v), ALU.mult, ALU.add)
                dve.drain()
                first_max(e_v, E_N, C_I16, vm, e_eq, e_t, cmk1, oh[1])
                v.tensor_tensor(T3(MM), T3(oh[0]), T3(oh[1]), ALU.add).then_inc(m_done, 1)
                for k, wk in ((0, w0), (1, w1k)):
                    v.tensor_tensor(T3(e_t), T3(e_s), T3(oh[k]), ALU.mult)
                    dve.drain()
                    v.tensor_reduce(wk[:, 0:nq], T3(e_t), AX.X, ALU.add)
                    dve.drain()
                v.tensor_tensor(wsum[:, 0:nq], w0[:, 0:nq], w1k[:, 0:nq], ALU.add)
                dve.drain()
                v.reciprocal(wsum[:, 0:nq], wsum[:, 0:nq])
                v.memset(PLi[:, :, :, 3:4], 0)
                dve.drain()
                for k, wk in ((0, w0), (1, w1k)):
                    v.tensor_tensor(PLf[:, k, 0:nq, 2], wk[:, 0:nq], wsum[:, 0:nq], ALU.mult)
                    v.tensor_copy(PLi[:, k, 0:nq, 0], cst[:, C_TOK:C_TOK + nq])
                    v.tensor_scalar(PLi[:, k, 0:nq, 1], cst[:, C_TOK:C_TOK + nq], float(k * routed(l)), None, ALU.add)
                key = ("rk", l)
                wait_made(dve, key)
                for k in range(2):
                    v.tensor_tensor(T3(e_t), bank(key)[:, 0:nq * E_N].rearrange("p (t e) -> p t e", e=E_N), T3(oh[k]), ALU.mult)
                    dve.drain()
                    v.tensor_reduce(rkf[:, k, 0:nq], T3(e_t), AX.X, ALU.add)
                    dve.drain()
                taken(v.tensor_copy(nbi[0:1, :], bank(key)[0:1, TILES * E_N:(TILES + 1) * E_N]), key)
                v.tensor_copy(rki[:, :, 0:nq], rkf[:, :, 0:nq])
                dve.drain()
                v.tensor_scalar(nbi[0:1, :], nbi[0:1, :], float(SLOT - 1), None, ALU.add)
                v.tensor_scalar(ji[:, :, 0:nq], rki[:, :, 0:nq], 6, None, ALU.arith_shift_right)
                v.tensor_scalar(pi[:, :, 0:nq], rki[:, :, 0:nq], SLOT - 1, None, ALU.bitwise_and)
                dve.drain()
                v.tensor_scalar(nb[0:1, :], nbi[0:1, :], 6, None, ALU.arith_shift_right)
                v.scalar_tensor_tensor(rowf[:, :, 0:nq], pi[:, :, 0:nq], float(E_N * JMAX), ji[:, :, 0:nq], ALU.mult, ALU.add)
                dve.drain()
                for k, low in ((0, cmk0), (1, cmk1)):
                    v.scalar_tensor_tensor(rowf[:, k, 0:nq], low[:, 0:nq], float(JMAX), rowf[:, k, 0:nq], ALU.mult, ALU.add)
                dve.drain()
                v.tensor_scalar(ROWI[:, :, 0:nq], rowf[:, :, 0:nq], float(E_N * JMAX), None, ALU.add)
                dve.drain().then_inc(pl_done, 1)
                barrier(dve, bar(l, 4))
                dve.drain().then_inc(nb_ready, 1)

                dve.wait_ge(init_m, l + 1)
                dve.wait_ge(tb_in[l], 16)
                dve.sem_inc(y_rdy[l], 1)
                done = dve.alloc_register(f"dve_blocks_{l}")
                dve.reg_mov(done, 0)

                def copy_gT(b):
                    dve.wait_ge(gt_full[l], b)
                    v.tensor_copy(gT.rearrange("p k s -> p (k s)"), ps[:, B_GT, 0:4 * SLOT]).then_inc(gt_rdy[l], 1)

                def copy_y(b):
                    dve.wait_ge(w2_full[l], b)
                    dve.wait_ge(scat[l], 16 * b + 16)
                    v.tensor_copy(ym[0:SLOT, 0:CHUNK], ps[0:SLOT, B_W2, :])
                    v.tensor_copy(ym[0:SLOT, CHUNK:D], ps[SLOT:P, B_W2, :]).then_inc(y_rdy[l], 1)

                def step(col, first=False):
                    b = dve.snap(done)
                    dve.wait_ge(xt_full[l], b + 2)
                    v.tensor_copy(xT.rearrange("p k s -> p (k s)"), ps[:, B_XT, :]).then_inc(xt_rdy[l], 1)
                    if not first:
                        copy_gT(b)
                    dve.wait_ge(si_rdy[l], b + 1)
                    v.scalar_tensor_tensor(gg[0:SLOT, :], sg[0:SLOT, :], TBf[0:SLOT, bass.ds(4 * col + 2, 1)], ps[SLOT:P, B_W13, :],
                                           ALU.mult, ALU.mult).then_inc(g_rdy[l], 1)
                    if first:
                        dve.wait_ge(scat[l], 16)
                        dve.sem_inc(y_rdy[l], 1)
                    else:
                        copy_y(b)
                    dve.reg_add(done, done, 1)

                def expert(e, first=False):
                    blocks = dve.value_load(nb[0:1, bass.ds(e, 1)], min_val=0, max_val=JMAX)
                    step(e * JMAX, first)
                    with dve.If(blocks > 1):
                        with dve.Fori(1, blocks) as j:
                            step(e * JMAX + j)

                expert(0, True)
                with dve.Fori(1, E_N) as e:
                    expert(e)
                b = dve.snap(done)
                copy_gT(b)
                copy_y(b)
                barrier(dve, bar(l, 5))

                dve.wait_ge(gate_in[l], 32 * conds)
                for i in range(nq):
                    a, c2 = i // 2, i % 2
                    dve.wait_ge(y_in[l], 64 * (a + 1))
                    v.tensor_tensor(Y[:, 0, c2], Y[:, 0, c2], Y[:, 1, c2], ALU.add)
                    dve.drain()
                    v.tensor_tensor(Y[:, 0, c2], Y[:, 0, c2], gate[:, a], ALU.mult)
                    dve.drain()
                    v.tensor_tensor(X[:, i], X[:, i], Y[:, 0, c2], ALU.add).then_inc(comb[l], 1)
                if l == DEPTH - 1:
                    dve.wait_ge(fin_rs, 1)
                    dve.wait_ge(fin_g, 16)
                    for i in range(2):
                        v.scalar_tensor_tensor(X[:, i], X[:, i], rstd[:, i:i + 1], GFIN, ALU.mult, ALU.mult).then_inc(fin_o, 1)
                barrier(dve, bar(l, 6))

        @block.tensor
        def _(pe):
            t_ = nc.tensor

            def mm(out, lhsT, rhs, first, last_):
                return t_.matmul(out, lhsT, rhs, start=first, stop=last_)

            pe.wait_ge(cst_in, 16)
            pe.wait_ge(par_in, 16 * N_PAR)
            made(t_.transpose(bank(("par",))[:, 0:DEPTH * 15], PR[0:DEPTH * 15, :], ident[0:DEPTH * 15, 0:DEPTH * 15]), ("par",))
            nk = DEPTH * KCONV
            for c2 in range(2):
                last = t_.transpose(bank(("cw",))[:, c2 * nk:(c2 + 1) * nk], CWR[0:nk, c2 * P:(c2 + 1) * P], ident[0:nk, 0:nk])
            made(last, ("cw",))
            pe.wait_ge(c_silu, 1)
            made(t_.transpose(bank(("c",))[:, 0:16], CRS[0:16, :], ident[0:16, 0:16]), ("c",))
            wait_taken(pe, ("c",))

            def ada(l, q):
                key = ("ada", l, q)
                claim(pe, key)
                for j in range(4):
                    arrived(pe, l, U_ADA[4 * q + j])
                for k in range(KD):
                    for j in range(4):
                        last = mm(bank(key)[32 * j:32 * j + 32, :], SC[:, k], ring[:, slot(l, U_ADA[4 * q + j]), k], k == 0, k == KD - 1)
                made(last, key)
                for j in range(4):
                    pe.drain().then_inc(ring_free[slot(l, U_ADA[4 * q + j])], 1)

            for l in range(DEPTH):
                nq = TILES if l == 0 else 2
                n_ln = TOK if l == 0 else S_LAT
                ada(l, 0)
                pe.wait_ge(mrow_in[l], 32)
                claim(pe, ("modc", l))
                made(t_.transpose(bank(("modc", l))[:, 0:32], MR[0:32, :], ident[0:32, 0:32]), ("modc", l))
                pe.wait_ge(y_done, l + 1)
                for q in range(8):
                    key = ("nT", l, q)
                    claim(pe, key)
                    cnd, kk = q // 4, 2 * (q % 4)
                    for a in range(2):
                        for t in range(2):
                            last = t_.transpose(bank(key)[:, a * 256 + t * P:a * 256 + (t + 1) * P],
                                                YS[:, 2 * cnd + t, (kk + a) * P:(kk + a + 1) * P], ident)
                    made(last, key)
                barrier(pe, bar(l, 1))

                def transposes(job):
                    key = ("inT", l) + job
                    wait_taken(pe, ("in", l) + job)
                    claim(pe, key)
                    stg = ST[:, staged.index(job) % 2]
                    for b in range(2 if job[0] == "b" and job[1] >= 2 and l else 0, 4):
                        last = t_.transpose(bank(key)[:, b * P:(b + 1) * P], stg[:, b * P:(b + 1) * P], ident)
                    made(last, key)

                staged = [j for j in in_jobs(l) if j[0] in ("ka", "b", "qa")]
                prev, jobs = None, in_jobs(l)
                for x_, job in enumerate(jobs):
                    seg, t = job
                    key = ("in", l) + job
                    unit = ring[:, slot(l, U_IN[seg])]
                    if x_ == 0 or jobs[x_ - 1][0] != seg:
                        arrived(pe, l, U_IN[seg])
                    claim(pe, key)
                    for k in range(KD):
                        if seg == "uc":
                            last = mm(bank(key)[:, 0:n_ln], unit[:, k, t * P:(t + 1) * P], HT[:, k, 0:n_ln], k == 0, k == KD - 1)
                        elif seg == "b" and l and t >= 2:
                            last = mm(bank(key)[:, 256:512], HT[:, k, t * P:(t + 1) * P], unit[:, k, 256:512], k == 0, k == KD - 1)
                        else:
                            last = mm(bank(key), HT[:, k, t * P:(t + 1) * P], unit[:, k], k == 0, k == KD - 1)
                    made(last, key)
                    if x_ == len(jobs) - 1 or jobs[x_ + 1][0] != seg:
                        pe.drain().then_inc(ring_free[slot(l, U_IN[seg])], 1)
                    if prev:
                        transposes(prev)
                    prev = job if job in staged else None
                if prev:
                    transposes(prev)
                pe.wait_ge(cv_d, l + 1)
                claim(pe, ("mu", l))
                for c2 in range(2):
                    last = mm(bank(("mu", l))[:, 0:n_ln], ones, acc[:, c2, 0:n_ln], c2 == 0, c2 == 1)
                made(last, ("mu", l))
                ada(l, 1)
                pe.wait_ge(ln_sq, l + 1)
                claim(pe, ("var", l))
                for c2 in range(2):
                    last = mm(bank(("var", l))[:, 0:n_ln], ones, G[:, c2, 0:n_ln], c2 == 0, c2 == 1)
                made(last, ("var", l))
                ada(l, 2)
                barrier(pe, bar(l, 2))

                units, tj = units_of(l), t_jobs(l)
                for st_ in attention_steps(l):
                    what, x_ = st_
                    if what == "S":
                        i, u = units[x_]
                        k0 = 0 if i < 2 else S_LAT
                        for m in range(2):
                            claim(pe, ("S", l, x_, m))
                        for m in range(2):
                            rows = slice(64 * m, 64 * m + 64)
                            made(mm(bank(("S", l, x_, m))[:, 0:TOK - k0], qT[rows, u, i * P:(i + 1) * P], kT[rows, u, k0:TOK], True, True), ("S", l, x_, m))
                    elif what == "T":
                        n, m = tj[x_]
                        i, u = units[n]
                        key = ("T", l, x_)
                        pe.wait_ge(pr_done[l], n + 1)
                        claim(pe, key)
                        for kt in range(4 if i < 2 else 2):
                            last = t_.transpose(bank(key)[:, kt * P:(kt + 1) * P], PB[:, n % 2, m, kt * P:(kt + 1) * P], ident)
                        made(last, key)
                    elif what == "O":
                        n, m = tj[x_]
                        i, u = units[n]
                        key = ("O", l, x_)
                        wait_taken(pe, ("T", l, x_))
                        claim(pe, key)
                        c0, w = (u * P, P) if u < BLK_A else (512 + (u - BLK_A) * HD, HD)
                        nkt = 4 if i < 2 else 2
                        for kt in range(nkt):
                            last = mm(bank(key)[:, 0:w], aT[:, x_ % 2, kt * P:(kt + 1) * P], V[:, 4 - nkt + kt, c0:c0 + w], kt == 0, kt == nkt - 1)
                        made(last, key)
                    else:
                        pe.wait_ge(o_done[l], x_ + 1)
                        for name, b0, b1 in (("MA", 0, 4), ("MB", 4, 6)):
                            key = (name, l, x_)
                            claim(pe, key)
                            for b in range(b0, b1):
                                last = t_.transpose(bank(key)[:, (b - b0) * P:(b - b0 + 1) * P], O[x_ % 2][:, b * P:(b + 1) * P], ident)
                            made(last, key)
                barrier(pe, bar(l, 3))

                def route(i):
                    pe.wait_ge(h2_done[l], i + 1)
                    for h in range(2):
                        key = ("h2T", l, i, h)
                        claim(pe, key)
                        for b in range(4):
                            k = 4 * h + b
                            last = t_.transpose(bank(key)[:, b * P:(b + 1) * P], H2[:, i, k * P:(k + 1) * P], ident)
                        made(last, key)
                    for h in range(2):
                        wait_taken(pe, ("h2T", l, i, h))
                    key = ("rt", l, i)
                    claim(pe, key)
                    for k in range(KD):
                        last = mm(bank(key)[:, 0:E_N], hTr[:, k], rw[:, k], k == 0, k == KD - 1)
                    made(last, key)

                for h in range(OUT_N):
                    arrived(pe, l, U_OUT + h)
                for i in range(nq):
                    for h in range(OUT_N):
                        key = ("wo", l, i, h)
                        claim(pe, key)
                        for k in range(KD):
                            last = mm(bank(key), HT[:, k, i * P:(i + 1) * P], ring[:, slot(l, U_OUT + h), k], k == 0, k == KD - 1)
                        made(last, key)
                        if i == nq - 1:
                            pe.drain().then_inc(ring_free[slot(l, U_OUT + h)], 1)
                    if i:
                        route(i - 1)
                route(nq - 1)
                key = ("rk", l)
                pe.wait_ge(m_done, l + 1)
                claim(pe, key)
                for i in range(nq):
                    out = bank(key)[:, i * E_N:(i + 1) * E_N]
                    for j in range(i):
                        mm(out, ones, MM[:, j], j == 0, False)
                    mm(out, tri, MM[:, i], i == 0, True)
                for i in range(nq):
                    last = mm(bank(key)[:, TILES * E_N:(TILES + 1) * E_N], ones, MM[:, i], i == 0, i == nq - 1)
                made(last, key)
                barrier(pe, bar(l, 4))

                pe.wait_ge(nb_ready, l + 1)
                pe.sem_inc(xt_full[l], 1)
                done = pe.alloc_register(f"pe_blocks_{l}")
                pe.reg_mov(done, 0)

                def gT_product(b, free=()):
                    hold(pe, g_rdy[l], b, pe_passed)
                    for k in range(4):
                        last = t_.transpose(ps[:, B_GT, k * SLOT:(k + 1) * SLOT], gg[0:SLOT, k * P:(k + 1) * P], ident[0:SLOT, 0:SLOT])
                        if k < len(free):
                            last.then_inc(ring_free[free[k]], 1)
                    last.then_inc(gt_full[l], 1)

                def w2_product(b, sl, until=None):
                    pe.wait_ge(gt_rdy[l], b)
                    pe.wait_ge(y_rdy[l], b + 1)
                    if until is not None:
                        pe.wait_ge(ring_full[sl], until)
                    w = unit_of_slot(sl).rearrange("p k n -> p (k n)").rearrange("p (k n) -> p k n", k=4)
                    for k in range(4):
                        for h in range(2):
                            last = mm(ps[64 * h:64 * h + 64, B_W2, :], gT[:, k], w[:, k, h * CHUNK:(h + 1) * CHUNK], k == 0, k == 3)
                    last.then_inc(w2_full[l], 1)

                def step(slots, prev_slot, waits, free=(), first=False):
                    b = pe.snap(done)
                    hold(pe, gath[l], 16 * b + 16, pe_passed)
                    for k in range(KD):
                        last = t_.transpose(ps[:, B_XT, k * SLOT:(k + 1) * SLOT], xg[0:SLOT, k * P:(k + 1) * P], ident[0:SLOT, 0:SLOT])
                        if k < len(free):
                            last.then_inc(ring_free[free[k]], 1)
                    last.then_inc(xt_full[l], 1)
                    if not first:
                        gT_product(b)
                    pe.wait_ge(xt_rdy[l], b + 1)
                    if waits:
                        for q in range(2):
                            pe.wait_ge(ring_full[slots[q]], waits[q])
                    for k in range(KD):
                        for h in range(2):
                            last = mm(ps[64 * h:64 * h + 64, B_W13, :], xT[:, k], unit_of_slot(slots[h])[:, k], k == 0, k == KD - 1)
                    last.then_inc(w13_full[l], 1)
                    if not first:
                        w2_product(b, prev_slot, waits[2] if waits else None)
                    pe.reg_add(done, done, 1)

                def expert(e, turn, at_e, first=False):
                    sl, before = expert_slots(l, e), expert_slots(l, e - 1)
                    waits = [16 * expert_uses(l, e, x, turn) + 16 for x in sl[:2]]
                    free = []
                    if not first:
                        waits.append(16 * expert_uses(l, e - 1, before[2], turn) + 16)
                        free = [before[0], before[1]]
                        if not (isinstance(turn, int) and e < 2):
                            free.append(expert_slots(l, e - 2)[2])
                    else:
                        waits.append(None)
                    blocks = pe.value_load(nb[0:1, bass.ds(at_e, 1)], min_val=0, max_val=JMAX)
                    step(sl, before[2], waits, free, first)
                    with pe.If(blocks > 1):
                        hold(pe, ring_full[sl[2]], 16 * expert_uses(l, e, sl[2], turn) + 16, pe_passed)
                        with pe.Fori(1, blocks):
                            step(sl, sl[2], None)

                expert(0, 0, 0, True)
                for e in range(1, GROUPS + 1):
                    expert(e, 0, e)
                with pe.Fori(1, (E_N - 1) // GROUPS) as i:
                    for q in range(GROUPS):
                        expert(1 + q, i, 3 * i + 1 + q)
                b = pe.snap(done)
                last_e = E_N - 1
                sl = expert_slots(l, last_e)
                gT_product(b, [sl[0], sl[1], expert_slots(l, last_e - 1)[2]])
                w2_product(b, sl[2], 16 * expert_uses(l, last_e, sl[2]) + 16)
                pe.drain().then_inc(ring_free[sl[2]], 1)
                barrier(pe, bar(l, 5))
                barrier(pe, bar(l, 6))


N_PAR = 2 + 5 * DEPTH + 5

_NAMES = ["x", "c", "ctx", "c_ctx", "w_ada", "b_ada", "g_mix", "w_in", "diff_lambda", "diff_norm_g", "attn_sink", "conv_w", "conv_b",
          "conv_ln_g", "conv_ln_b", "w_out", "g_ffn", "router_w", "router_bias", "w1", "w3", "w2", "g_final"]


def kernel(**inputs):
    import concourse.bacc as bacc
    from concourse.bass_utils import run_bass_kernel_spmd

    nc = bacc.Bacc("TRN2", target_bir_lowering=False, num_devices=1)
    arrays, A = {}, {}
    for name in _NAMES:
        a = np.ascontiguousarray(inputs[name])
        arrays[f"in_{name}"] = a
        A[name] = nc.dram_tensor(f"in_{name}", a.shape, mybir.dt.from_np(a.dtype), kind="ExternalInput").ap()
    arrays["in_cst"] = constants()
    A["cst"] = nc.dram_tensor("in_cst", arrays["in_cst"].shape, mybir.dt.float32, kind="ExternalInput").ap()
    A["out"] = nc.dram_tensor("out", (1, S_LAT, D), mybir.dt.float32, kind="ExternalOutput").ap()
    hybrid_moe_kernel(nc, A)
    return run_bass_kernel_spmd(nc, [arrays], core_ids=[0]).results[0]["out"]
```

```python
import math
from contextlib import ExitStack

import concourse.bass as bass
import numpy as np
from concourse import mybir

P = 128
D = 1024
KD = D // P
S_LAT = 256
S_CTX = 256
TOK = S_LAT + S_CTX
TILES = TOK // P
DEPTH = 2
GRID_W = 64
HD = 64
BLK_A, BLK_B = 4, 2
BLK = BLK_A + BLK_B
VW = 512 + 128
CH = 256
KCONV = 31
PADC = KCONV // 2
E_N, E_G, E_F = 16, 4, 512
SLOT = 64
JMAX = TOK // SLOT
EPS = 1e-6
BIG = 1e30
NO_ROW = 1 << 20
WINDOW = 128
CHUNK = 512
QUADS = 6 * D // CHUNK // 4
OUT_N = D // CHUNK
RING = 6
GROUPS = 3
EXTRA = 3 * GROUPS - RING

C_ID, C_TRI, C_ONE = 0, 128, 256
C_ROPE = 384
C_MASK = C_ROPE + 2 * 128
C_I16 = C_MASK + 2 * 256
C_I4 = C_I16 + 16
C_TOK = C_I4 + 4
C_W = C_TOK + TILES


def routed(l):
    return TOK if l < DEPTH - 1 else S_LAT


def lambda_init(l):
    return 0.8 - 0.6 * math.exp(-0.3 * l)


def constants():
    c = np.zeros((P, C_W), np.float32)
    r = np.arange(P)
    c[:, C_ID:C_ID + P] = np.eye(P)
    c[:, C_TRI:C_TRI + P] = r[:, None] < r[None, :]
    c[:, C_ONE:C_ONE + P] = 1.0
    nf = HD // 4
    inv = (np.float32(10000.0) ** (-np.arange(nf, dtype=np.float32) / np.float32(nf))).astype(np.float32)
    for t in range(S_LAT // P):
        q = t * P + r
        pos = np.stack([q // GRID_W, q % GRID_W], -1).astype(np.float32)
        ang = pos[:, :, None] * inv
        cos, sin = np.cos(ang), np.sin(ang)
        c[:, C_ROPE + t * 128:C_ROPE + t * 128 + 64] = np.stack([cos, cos], 2).reshape(P, 64)
        c[:, C_ROPE + t * 128 + 64:C_ROPE + t * 128 + 128] = np.stack([-sin, sin], 2).reshape(P, 64)
        k = np.arange(S_LAT)
        c[:, C_MASK + t * 256:C_MASK + (t + 1) * 256] = np.where(np.abs(q[:, None] - k) <= WINDOW, 0.0, -BIG)
    c[:, C_I16:C_I16 + 16] = np.arange(16)
    c[:, C_I4:C_I4 + 4] = np.arange(4)
    c[:, C_TOK:C_TOK + TILES] = r[:, None] + P * np.arange(TILES)
    return c


SUMS_AFTER = {("va", 0): "mu", ("va", 2): "var"}


def bank_plan():
    uses, plan, turn = [0] * 8, {}, {}

    def put(key, banks=range(8), bank=None):
        if bank is None:
            name = tuple(banks)
            bank = name[turn.get(name, 0) % len(name)]
            turn[name] = turn.get(name, 0) + 1
        plan[key] = (bank, uses[bank])
        uses[bank] += 1

    put(("c",))
    for l in range(DEPTH):
        nq = TILES if l == 0 else 2
        for g in range(8):
            if l == 0 and g == 4:
                for key in (("par",), ("cw",), ("ada", 0, 0), ("modc", 0)):
                    put(key)
            put(("nT", l, g))
        prev = None
        for job in in_jobs(l):
            put(("in", l) + job)
            if prev:
                put(("inT", l) + prev)
            prev = job if job[0] in ("ka", "b", "qa") else None
            if quad_after(l, job):
                put(("ada",) + quad_after(l, job))
            if job in SUMS_AFTER:
                put((SUMS_AFTER[job], l))
        if prev:
            put(("inT", l) + prev)
        if l == 0:
            put(("modc", 1))
        for step in attention_steps(l):
            if step[0] == "S":
                for m in range(2):
                    put(("S", l, step[1], m), bank=2 * (step[1] % 2) + m)
            elif step[0] == "T":
                put(("T", l, step[1]), (4, 5))
            elif step[0] == "O":
                put(("O", l, step[1]), (6, 7))
            else:
                put(("MA", l, step[1]), (4, 5))
                put(("MB", l, step[1]), (4, 5))
        for i in range(nq):
            for h in range(OUT_N):
                put(("wo", l, i, h))
            if i >= 1:
                for h in range(2):
                    put(("h2T", l, i - 1, h))
                put(("rt", l, i - 1))
        for h in range(2):
            put(("h2T", l, nq - 1, h))
        put(("rt", l, nq - 1))
        put(("rk", l))
    return plan, uses


def ring_plan():
    uses, at, front, experts = [0] * (RING + EXTRA), 0, [], []
    for l in range(DEPTH):
        row = {}
        for name in front_units(l):
            row[name] = (at, uses[at])
            uses[at] += 1
            at = (at + 1) % RING
        front.append(row)
        groups = [[(at + 3 * g_ + w) % RING for w in range(3)] for g_ in range(2)] + [list(range(RING, RING + EXTRA))]
        experts.append((groups, list(uses)))
        for e in range(E_N):
            for x in groups[e % GROUPS]:
                uses[x] += 1
        at = (at + 3) % RING
    return front, experts


def in_jobs(l):
    q_tiles = TILES if l == 0 else 2
    return ([("uc", f) for f in (2, 3, 0, 1)] + [("ka", t) for t in range(TILES)] + [("b", t) for t in range(TILES)]
            + [("va", t) for t in range(TILES)] + [("qa", t) for t in range(q_tiles)])


def quad_after(l, job):
    last_of = {"uc": (0, 1), "ka": (0, 2), "b": (1, 0), "va": (1, 1), "qa": (1, 2)}
    last = {j[0]: j for j in in_jobs(l)}
    return last_of[job[0]] if l == 0 and last[job[0]] == job else None


def front_units(l):
    out = [("ada", 0, j) for j in range(4)] if l == 0 else []
    for seg in ("uc", "ka", "b", "va", "qa"):
        out.append((seg,))
        job = [j for j in in_jobs(l) if j[0] == seg][-1]
        if quad_after(l, job):
            la, q = quad_after(l, job)
            out += [("ada", la, 4 * q + j) for j in range(4)]
    return out + [("out", h) for h in range(OUT_N)]


def units_of(l):
    return [(i, u) for i in range(TILES if l == 0 else 2) for u in range(BLK)]


def t_jobs(l):
    return [(n, m) for n, (_, u) in enumerate(units_of(l)) for m in range(1 if u < BLK_A else 2)]


def attention_steps(l):
    units, tj = units_of(l), t_jobs(l)
    out = [("S", 0), ("S", 1)]
    for n in range(len(units)):
        if n + 2 < len(units):
            out.append(("S", n + 2))
        out += [("T", k) for k, (a, _) in enumerate(tj) if a == n]
        out += [("O", k) for k, (a, _) in enumerate(tj) if a == n - 1]
        if units[n][1] == 2 and units[n][0] > 0:
            out.append(("M", units[n][0] - 1))
    out += [("O", k) for k, (a, _) in enumerate(tj) if a == len(units) - 1]
    out.append(("M", units[-1][0]))
    return out


def hybrid_moe_kernel(nc, A):
    fp32, i32 = mybir.dt.float32, mybir.dt.int32
    ALU, ACT, AX = mybir.AluOpType, mybir.ActivationFunctionType, mybir.AxisListType
    PLAN, USES = bank_plan()
    ctx = ExitStack()
    with ctx:
        def sb(name, shape, dt=fp32):
            return ctx.enter_context(nc.sbuf_tensor(name, shape, dt))

        def sem(name):
            return ctx.enter_context(nc.semaphore(name))

        def sems(name, n):
            return [sem(f"{name}_{k}") for k in range(n)]

        ring = sb("ring", [P, RING, KD, CHUNK])
        X = sb("X", [P, TILES, D])
        HT = sb("HT", [P, KD, TOK])
        gate = sb("gate", [P, 2, D])
        cst = sb("cst", [P, C_W])
        SC = sb("SC", [P, KD, 32])
        PC = sb("PC", [P, DEPTH, 15])
        NC = sb("NC", [P, DEPTH, 5])
        CW = sb("CW", [P, 2, DEPTH * KCONV])
        rw = sb("rw", [P, KD, E_N])
        rb = sb("rb", [P, E_N])
        sink = sb("sink", [P, DEPTH, 4])
        lamx = sb("lamx", [P, DEPTH, 2])
        neglam = sb("neglam", [P, DEPTH])
        AB = sb("AB", [P, DEPTH, 2, 2, KD])
        half = sb("half", [P, 1])
        ss = sb("ss", [P, TILES])
        ms = sb("ms", [P, TILES])
        rstd = sb("rstd", [P, TILES])
        mx = sb("mx", [P, 2, 2])
        nm = sb("nm", [P, 2, 2])
        sums = sb("sums", [P, 2, 2])
        es = sb("es", [P, 2, 2])
        rec = sb("rec", [P, 4, 2])
        cf = sb("cf", [P, 2])
        ss4 = sb("ss4", [P, 2, 4])
        ms4 = sb("ms4", [P, 2, 4])
        rs4 = sb("rs4", [P, 2, 4])
        AW = 2560 + 2 * 3072 + 1024 + 1144 + 1024 + 3840
        area = sb("area", [P, AW])
        at = [0]

        def cut(width, start=None):
            if start is not None:
                at[0] = start
            piece = area[:, at[0]:at[0] + width]
            at[0] += width
            assert at[0] <= AW, at[0]
            return piece

        V = cut(TILES * VW, 0).rearrange("p (t w) -> p t w", t=TILES)
        qT = cut(BLK * TOK).rearrange("p (b t) -> p b t", b=BLK)
        kT = cut(BLK * TOK).rearrange("p (b t) -> p b t", b=BLK)
        G = cut(2 * TOK).rearrange("p (c t) -> p c t", c=2)
        ZP_AT = at[0]
        zpad = cut(2 * 2 * (S_LAT + 2 * PADC)).rearrange("p (c s t) -> p c s t", c=2, s=2)
        acc = cut(2 * TOK).rearrange("p (c t) -> p c t", c=2)
        S1 = at[0]
        PB = cut(2048, S1).rearrange("p (b m k) -> p b m k", b=2, m=2)
        aT = cut(1024).rearrange("p (b k) -> p b k", b=2)
        O = [cut(BLK * P), area[:, ZP_AT:ZP_AT + BLK * P]]
        RT = cut(1024, S1).rearrange("p (b k) -> p b k", b=2)
        ST = cut(1024).rearrange("p (b k) -> p b k", b=2)
        bias12 = cut(1024).rearrange("p (b k) -> p b k", b=2)
        mst, mst0 = gate[:, 1, 0:CHUNK], gate[:, 0, 0:CHUNK]
        YS = cut(TILES * D, 0).rearrange("p (t d) -> p t d", t=TILES)
        bias0 = cut(512)
        PR = cut(128)
        CR = cut(128)
        CRS = cut(128)
        CWR = cut(256)
        DL = cut(DEPTH * 4 * HD).rearrange("p (l a d) -> p l a d", l=DEPTH, a=4)
        DLP = cut(DEPTH * 2 * HD).rearrange("p (l a d) -> p l a d", l=DEPTH, a=2)
        SI = cut(512).bitcast(i32)
        BC = cut(2 * 2 * D, 0).rearrange("p (c v d) -> p c v d", c=2, v=2)
        GF = cut(D)
        H2 = cut(TILES * D).rearrange("p (t d) -> p t d", t=TILES)
        hTr = cut(KD * P).rearrange("p (k t) -> p k t", k=KD)
        tmp = cut(2 * CHUNK).rearrange("p (b k) -> p b k", b=2)
        R_AT = at[0]
        RW = 64

        def rt_tile(width):
            return cut(width)

        e_s, e_b, e_v, e_t, e_eq = (rt_tile(RW).rearrange("p (t e) -> p t e", e=E_N) for _ in range(5))
        oh = [rt_tile(RW).rearrange("p (t e) -> p t e", e=E_N) for _ in range(2)]
        MM = rt_tile(RW).rearrange("p (t e) -> p t e", e=E_N)
        PM = rt_tile((TILES + 1) * E_N).rearrange("p (t e) -> p t e", e=E_N)
        hl = rt_tile(4 * 16).rearrange("p (a g) -> p a g", a=4)
        grp, geq, gcd, gone, gneg = (rt_tile(16).rearrange("p (t g) -> p t g", g=E_G) for _ in range(5))
        gm, cm, vm, cmk0, cmk1, w0, w1k, wsum = (rt_tile(TILES) for _ in range(8))
        rkf = rt_tile(2 * TILES).rearrange("p (k t) -> p k t", k=2)
        rowf = rt_tile(2 * TILES).rearrange("p (k t) -> p k t", k=2)
        rki = rt_tile(2 * TILES).bitcast(i32).rearrange("p (k t) -> p k t", k=2)
        ji = rt_tile(2 * TILES).bitcast(i32).rearrange("p (k t) -> p k t", k=2)
        pi = rt_tile(2 * TILES).bitcast(i32).rearrange("p (k t) -> p k t", k=2)
        ROWI = rt_tile(2 * TILES).bitcast(i32).rearrange("p (k t) -> p k t", k=2)
        PLf = rt_tile(2 * TILES * 4).rearrange("p (k t w) -> p k t w", k=2, w=4)
        PLi = PLf.bitcast(i32)
        nbi = rt_tile(E_N).bitcast(i32)
        nb = rt_tile(E_N).bitcast(i32)
        TBf = cut(E_N * JMAX * 4)
        TBi = TBf.bitcast(i32)
        DR = cut(4).bitcast(i32)
        gidx = cut(1).bitcast(i32)
        sidx = cut(1).bitcast(i32)
        xg = cut(D)
        YM_AT = at[0]
        xT = cut(KD * SLOT, 0).rearrange("p (k s) -> p k s", k=KD)
        sg = cut(E_F)
        gg = cut(E_F)
        gT = cut(4 * SLOT).rearrange("p (k s) -> p k s", k=4)
        ym = cut(D)
        EX_AT = at[0]
        assert EX_AT + 2 * 4096 <= R_AT
        Y = cut(2 * TILES * D, 0).rearrange("p (t k d) -> p t k d", t=TILES, k=2)
        GFIN = cut(D)
        SQ = cut(TILES * D).rearrange("p (t d) -> p t d", t=TILES)

        ps = ctx.enter_context(nc.psum_tensor("ps", [P, 8, CHUNK], fp32))
        B_XT, B_GT, B_W13, B_W2 = 0, 1, 2, 3

        modD = nc.dram_tensor("mod_rows", [DEPTH, 2, 6 * D], fp32).ap()
        h2D = [nc.dram_tensor(f"h2_rows_{l}", [routed(l), D], fp32).ap() for l in range(DEPTH)]
        yD = [nc.dram_tensor(f"expert_rows_{l}", [2 * routed(l), D], fp32).ap() for l in range(DEPTH)]
        slotD = [nc.dram_tensor(f"slot_rows_{l}", [SLOT * E_N * JMAX, 4], i32).ap() for l in range(DEPTH)]

        full = sems("bank_full", 8)
        evict = sems("bank_evicted", 8)
        ring_full = sems("ring_full", RING + EXTRA)
        ring_free = sems("ring_free", RING + EXTRA)
        cst_in = sem("constants_in")
        par_in = sem("parameters_in")
        x_in = sem("x_in")
        c_silu = sem("c_silu")
        setup = sem("setup_done")
        si_out = sem("slot_tables_cleared")
        lam_sum = sem("lambda_sums")
        lam_exp = sem("lambda_exps")
        phase = sem("phase")
        c_in = sem("c_in")
        bias_in = sems("bias_in", 2)
        mod_sb = sem("mod_rows_made")
        mod_out = {(l, q): sem(f"mod_rows_stored_{l}_{q}") for l in range(DEPTH) for q in (1, 2)}
        ss_done = sem("squares_summed")
        rs_done = sem("rstd_made")
        y_done = sem("normed")
        ab_done = sem("columns_made")
        pads = sem("pads_zero")
        g_exp = sem("conv_gate_exp")
        cv_d = sem("conv_done")
        ln_d = sem("ln_centred")
        ln_sq = sem("ln_squares")
        ln_v = sem("ln_variance")
        ln_r = sem("ln_rstd")
        ln_n = sem("ln_normed")
        ln_e = sem("ln_exp")
        nm_done = sems("negmax", DEPTH)
        ex_done = sems("exps_b", DEPTH)
        pr_done = sems("probs", DEPTH)
        o_ss = sems("head_squares", DEPTH)
        o_rs = sems("head_rstd", DEPTH)
        o_done = sems("heads_normed", DEPTH)
        gate_in = sems("gate_in", DEPTH)
        gate2_in = sem("ffn_gate_in")
        bc_in = sems("ffn_rows_in", DEPTH)
        bc_done = sems("ffn_scale_made", DEPTH)
        x_add = sems("residual_added", DEPTH)
        ss2 = sems("squares2", DEPTH)
        rs2 = sems("rstd2", DEPTH)
        h2_done = sems("h2_made", DEPTH)
        h2_out = sems("h2_stored", DEPTH)
        m_done = sem("choices_made")
        pl_done = sem("slots_made")
        slot_out = sems("slots_scattered", DEPTH)
        tb_in = sems("slot_table_in", DEPTH)
        nb_ready = sem("counts_ready")
        gath = sems("tokens_gathered", DEPTH)
        xt_full = sems("xT_product", DEPTH)
        xt_rdy = sems("xT_copied", DEPTH)
        gt_full = sems("gT_product", DEPTH)
        gt_rdy = sems("gT_copied", DEPTH)
        w13_full = sems("w13_product", DEPTH)
        si_rdy = sems("silu_made", DEPTH)
        g_rdy = sems("hidden_made", DEPTH)
        w2_full = sems("w2_product", DEPTH)
        y_rdy = sems("y_copied", DEPTH)
        scat = sems("y_scattered", DEPTH)
        y_in = sems("y_in", TILES)
        comb = sems("y_added", DEPTH)
        pool_chain = sem("pool_chain")
        gidx_set = sems("gather_rows_set", DEPTH)
        sidx_set = sems("scatter_rows_set", DEPTH)
        sp_passed = sem("sp_waits_passed")
        pe_passed = sem("pe_waits_passed")
        pool_passed = sem("pool_waits_passed")
        fin_g = sem("final_gain_in")
        fin_o = sem("final_made")
        stored = sem("output_stored")

        def bank(key):
            return ps[:, PLAN[key][0], :]

        def claim(pe, key):
            b, u = PLAN[key]
            if u:
                pe.wait_ge(evict[b], u)

        def made(ins, key):
            ins.then_inc(full[PLAN[key][0]], 1)

        def wait_made(e, key):
            b, u = PLAN[key]
            e.wait_ge(full[b], u + 1)

        def taken(ins, key):
            ins.then_inc(evict[PLAN[key][0]], 1)

        def wait_taken(e, key):
            b, u = PLAN[key]
            e.wait_ge(evict[b], u + 1)

        def barrier(e, n):
            e.drain().then_inc(phase, 1)
            e.wait_ge(phase, 4 * n)

        def hold(e, semaphore, value, passed):
            e.wait_ge(semaphore, value)
            e.sem_inc(passed, 1)

        def bar(l, k):
            return 5 * l + k

        ident = cst[:, C_ID:C_ID + P]
        tri = cst[:, C_TRI:C_TRI + P]
        ones = cst[:, C_ONE:C_ONE + P]

        MODS = [(l, q) for l in range(DEPTH) for q in range(QUADS)]

        def bias_of(n):
            return bias0 if n == 0 else bias12[:, n % 2]

        IN_COL = {"qa": 0, "ka": 1, "va": 2, "b": 3, "uc": 4}

        FRONT, EXPERTS = ring_plan()
        extra = [HT[:].rearrange("p k t -> p (k t)"), area[:, EX_AT:EX_AT + 4096], area[:, EX_AT + 4096:EX_AT + 8192]]

        def unit_of_slot(x):
            return ring[:, x] if x < RING else extra[x - RING].rearrange("p (k n) -> p k n", k=KD)

        def slot(l, n):
            return FRONT[l][n][0]

        def use(l, n):
            return FRONT[l][n][1]

        def arrived(e, l, n):
            e.wait_ge(ring_full[slot(l, n)], 16 * (use(l, n) + 1))

        def expert_slots(l, e):
            return EXPERTS[l][0][e % GROUPS]

        def expert_uses(l, e, x, turn=0):
            return EXPERTS[l][1][x] + e // GROUPS + turn

        w_ada_v = A["w_ada"].rearrange("l (k p) n -> l p k n", p=P)
        w_in_v = A["w_in"].rearrange("l (k p) n -> l p k n", p=P)
        w_out_v = A["w_out"].rearrange("l (k p) n -> l p k n", p=P)
        w13_v = [A[w].rearrange("l e (k p) n -> l e p k n", p=P) for w in ("w1", "w3")]
        w2_v = A["w2"].rearrange("l e (k p) n -> l e p k n", p=P)

        block = ctx.enter_context(nc.Block())

        @block.sync
        def _(sp):
            def load(l, n, src):
                if use(l, n):
                    sp.wait_ge(ring_free[slot(l, n)], use(l, n))
                if n == ("ada", 0, 2):
                    sp.wait_ge(par_in, 16 * N_PAR)
                sp.dma_start(ring[:, slot(l, n)], src).then_inc(ring_full[slot(l, n)], 16)

            sp.dma_start(X[:, 0:2], A["x"].rearrange("b (t p) d -> p (b t) d", p=P)).then_inc(x_in, 16)
            sp.dma_start(X[:, 2:4], A["ctx"].rearrange("b (t p) d -> p (b t) d", p=P)).then_inc(x_in, 16)
            for l in range(DEPTH):
                for name in front_units(l):
                    if name[0] == "ada":
                        src = w_ada_v[name[1], :, :, name[2] * CHUNK:(name[2] + 1) * CHUNK]
                    elif name[0] == "out":
                        src = w_out_v[l, :, :, name[1] * CHUNK:(name[1] + 1) * CHUNK]
                    else:
                        src = w_in_v[l, :, :, IN_COL[name[0]] * CHUNK:(IN_COL[name[0]] + 1) * CHUNK]
                    load(l, name, src)

                def load_expert(e, turn, at_e):
                    for w, x in enumerate(expert_slots(l, e)):
                        if isinstance(turn, int) and e == 2 and w == 0:
                            sp.wait_ge(x_add[l], routed(l) // P)
                        if isinstance(turn, int) and e == 2 and w == 1:
                            sp.wait_ge(phase, 4 * bar(l, 4))
                            sp.wait_ge(h2_out[l], 16 * (routed(l) // P))
                            sp.wait_ge(gath[l], 16)
                        n = expert_uses(l, e, x, turn)
                        if not (isinstance(turn, int) and e < 2):
                            y, ey = (expert_slots(l, e - 1)[w + 1], e - 1) if w < 2 else (expert_slots(l, e)[0], e)
                            hold(sp, ring_full[y], 16 * expert_uses(l, ey, y, turn) + 16, sp_passed)
                        if not isinstance(n, int) or n > 0:
                            hold(sp, ring_free[x], n, sp_passed)
                        src = w13_v[w][l, bass.ds(at_e, 1)].squeeze(0) if w < 2 else w2_v[l, bass.ds(at_e, 1)].squeeze(0)
                        dst = unit_of_slot(x)
                        if w == 2:
                            dst = dst.rearrange("p k n -> p (k n)").rearrange("p (k n) -> p k n", k=4)
                        sp.dma_start(dst, src).then_inc(ring_full[x], 16)

                for e in range(GROUPS + 1):
                    load_expert(e, 0, e)
                with sp.Fori(1, (E_N - 1) // GROUPS) as i:
                    for q in range(GROUPS):
                        load_expert(1 + q, i, 3 * i + 1 + q)
                for cnd in range(routed(l) // S_LAT):
                    sp.dma_start(gate[:, cnd], modD[l, cnd:cnd + 1, 5 * D:6 * D].broadcast_to([P, D])).then_inc(gate2_in, 16)
                if l < DEPTH - 1:
                    sp.wait_ge(y_in[1], 32 * (l + 1))

        @block.gpsimd
        def _(pool):
            g = nc.gpsimd
            chain = [0]

            def link(ins):
                chain[0] += 1
                ins.then_inc(pool_chain, 1)
                pool.wait_ge(pool_chain, chain[0])

            g.memset(half[:], -0.5)
            g.memset(SC[:], 0.0)
            sv = SI.rearrange("p (r w) -> p r w", w=4)
            link(g.memset(sv, 0))
            g.memset(sv[:, :, 0:2], NO_ROW)
            pool.drain().then_inc(setup, 1)
            pool.wait_ge(setup, 1)
            for l in range(DEPTH):
                pool.dma_start(slotD[l].rearrange("(p r) w -> p (r w)", p=SLOT), SI[0:SLOT, :]).then_inc(si_out, 16)

            def rsqrt(out, s_, m_, n):
                link(g.tensor_scalar(m_, s_, 1.0 / n, EPS, ALU.mult, ALU.add))
                return g.tensor_tensor(out, m_, half[:].to_broadcast(list(out.shape)), ALU.pow)

            def load_bias(n):
                l_, q = MODS[n]
                for j in range(4):
                    col = (4 * q + j) * CHUNK
                    pool.dma_start(bias_of(n)[32 * j:32 * j + 32, :],
                                   A["b_ada"][l_:l_ + 1, col:col + CHUNK].broadcast_to([32, CHUNK])).then_inc(bias_in[n % 2], 16)

            def store_mod(n):
                l_, q = MODS[n]
                for j in range(4):
                    col = (4 * q + j) * CHUNK
                    pool.dma_start(modD[l_, :, col:col + CHUNK], mst[32 * j:32 * j + 2, :]).then_inc(mod_out[MODS[n]], 16)

            for l in range(DEPTH):
                nq = TILES if l == 0 else 2
                conds = 2 if l == 0 else 1

                if l == 0:
                    load_bias(0)
                if l == 0:
                    for i in range(TILES):
                        pool.wait_ge(ss_done, i + 1)
                        rsqrt(rstd[:, i:i + 1], ss[:, i:i + 1], ms[:, i:i + 1], D).then_inc(rs_done, 1)
                    pool.wait_ge(si_out, 32)
                barrier(pool, bar(l, 1))
                g.memset(zpad[:, :, :, 0:PADC], 0.0)
                g.memset(zpad[:, :, :, PADC + S_LAT:], 0.0).then_inc(pads, 1)
                if l == 0:
                    load_bias(1)
                    load_bias(2)
                    for n in range(1, len(MODS)):
                        pool.wait_ge(mod_sb, n + 1)
                        if MODS[n] in mod_out:
                            store_mod(n)
                        if n + 2 < len(MODS):
                            load_bias(n + 2)
                pool.sem_inc(phase, 1)
                pool.wait_ge(phase, 4 * bar(l, 2))
                if l == 0:
                    for m in mod_out.values():
                        pool.wait_ge(m, 64)
                for cnd in range(conds):
                    pool.dma_start(gate[:, cnd], modD[l, cnd:cnd + 1, 2 * D:3 * D].broadcast_to([P, D])).then_inc(gate_in[l], 16)
                for i in range(nq):
                    pool.wait_ge(o_ss[l], i + 1)
                    rsqrt(rs4[:, i % 2], ss4[:, i % 2], ms4[:, i % 2], 2 * HD).then_inc(o_rs[l], 1)
                barrier(pool, bar(l, 3))
                g.memset(DR[0:SLOT, :], NO_ROW)
                link(g.memset(xg[0:SLOT, :], 0.0))
                for cnd in range(conds):
                    for v in range(2):
                        pool.dma_start(BC[:, cnd, v], modD[l, cnd:cnd + 1, (3 + v) * D:(4 + v) * D].broadcast_to([P, D])).then_inc(bc_in[l], 16)
                pool.dma_start(GF, A["g_ffn"][l:l + 1, :].broadcast_to([P, D])).then_inc(bc_in[l], 16)
                for i in range(nq):
                    pool.wait_ge(ss2[l], i + 1)
                    rsqrt(rstd[:, i:i + 1], ss[:, i:i + 1], ms[:, i:i + 1], D).then_inc(rs2[l], 1)
                pool.wait_ge(h2_done[l], nq)
                link(g.memset(ym[0:SLOT, :], 0.0))
                pool.wait_ge(pl_done, l + 1)
                for k in range(2):
                    for i in range(nq):
                        pool.indirect_dma_start(slotD[l], bass.IndirectOffsetOnAxis(ap=ROWI[:, k, i:i + 1], axis=0),
                                                PLi[:, k, i, :], None).then_inc(slot_out[l], 16)
                pool.wait_ge(slot_out[l], 16 * 2 * nq)
                pool.dma_start(TBi[0:SLOT, :], slotD[l].rearrange("(p r) w -> p (r w)", p=SLOT)).then_inc(tb_in[l], 16)
                barrier(pool, bar(l, 4))
                pool.wait_ge(tb_in[l], 16)
                pool.wait_ge(h2_out[l], 16 * nq)
                done = pool.alloc_register(f"pool_blocks_{l}")
                pool.reg_mov(done, 0)

                def scatter(b):
                    g.tensor_copy(sidx[0:SLOT, :], DR[0:SLOT, bass.ds((b + 2) % 4, 1)]).then_inc(sidx_set[l], 1)
                    hold(pool, sidx_set[l], b + 1, pool_passed)
                    pool.indirect_dma_start(yD[l], bass.IndirectOffsetOnAxis(ap=sidx[0:SLOT, :], axis=0), ym[0:SLOT, :], None,
                                            bounds_check=2 * routed(l) - 1, oob_is_err=False).then_inc(scat[l], 16)

                def step(col):
                    b = pool.snap(done)
                    hold(pool, xt_full[l], b + 1, pool_passed)
                    pool.reg_add(done, done, 1)
                    g.tensor_copy(gidx[0:SLOT, :], TBi[0:SLOT, bass.ds(4 * col, 1)]).then_inc(gidx_set[l], 1)
                    g.tensor_copy(DR[0:SLOT, bass.ds(b % 4, 1)], TBi[0:SLOT, bass.ds(4 * col + 1, 1)]).then_inc(gidx_set[l], 1)
                    hold(pool, gidx_set[l], 2 * b + 2, pool_passed)
                    pool.indirect_dma_start(xg[0:SLOT, :], None, h2D[l], bass.IndirectOffsetOnAxis(ap=gidx[0:SLOT, :], axis=0),
                                            bounds_check=routed(l) - 1, oob_is_err=False).then_inc(gath[l], 16)
                    hold(pool, y_rdy[l], b + 1, pool_passed)
                    scatter(b)

                with pool.Fori(0, E_N) as e:
                    blocks = pool.value_load(nb[0:1, bass.ds(e, 1)], min_val=0, max_val=JMAX)
                    step(e * JMAX)
                    with pool.If(blocks > 1):
                        with pool.Fori(1, blocks) as j:
                            step(e * JMAX + j)
                b = pool.snap(done)
                hold(pool, y_rdy[l], b + 1, pool_passed)
                scatter(b)
                hold(pool, y_rdy[l], b + 2, pool_passed)
                scatter(b + 1)
                hold(pool, scat[l], 16 * b + 32, pool_passed)
                barrier(pool, bar(l, 5))
                if l == DEPTH - 1:
                    pool.dma_start(GFIN, A["g_final"].rearrange("(a n) -> a n", a=1).broadcast_to([P, D])).then_inc(fin_g, 16)
                for i in range(nq):
                    pool.wait_ge(ss_done, TILES * (l + 1) + i + 1)
                    rsqrt(rstd[:, i:i + 1], ss[:, i:i + 1], ms[:, i:i + 1], D).then_inc(rs_done, 1)
                if l == DEPTH - 1:
                    barrier(pool, bar(l, 6))

        @block.scalar
        def _(act):
            s = nc.scalar
            act.dma_start(CR[0:8, :], A["c"].rearrange("b (r n) -> (b r) n", n=P)).then_inc(c_in, 16)
            act.dma_start(CR[8:16, :], A["c_ctx"].rearrange("(r n) -> r n", n=P)).then_inc(c_in, 16)
            act.dma_start(cst[:], A["cst"]).then_inc(cst_in, 16)

            def par(dst, src):
                act.dma_start(dst, src).then_inc(par_in, 16)

            for l in range(DEPTH):
                r0 = 15 * l
                for at_, name, rows in ((0, "g_mix", 8), (8, "diff_norm_g", 1), (9, "conv_b", 2), (11, "conv_ln_g", 2), (13, "conv_ln_b", 2)):
                    par(PR[r0 + at_:r0 + at_ + rows, :], A[name][l].rearrange("(r n) -> r n", n=P))
            par(CWR[0:DEPTH * KCONV, :], A["conv_w"].rearrange("l k c -> (l k) c"))
            par(DL.rearrange("p l a d -> p (l a d)"),
                A["diff_lambda"].rearrange("l a d -> (l a d)").rearrange("(o n) -> o n", o=1).broadcast_to([P, DEPTH * 4 * HD]))
            par(rw[:], A["router_w"].rearrange("(k p) e -> p k e", p=P))
            par(rb[:], A["router_bias"].rearrange("(o n) -> o n", o=1).broadcast_to([P, E_N]))
            par(sink[:].rearrange("p l h -> p (l h)"), A["attn_sink"].rearrange("l h -> (l h)").rearrange("(o n) -> o n", o=1).broadcast_to([P, DEPTH * 4]))
            act.wait_ge(c_in, 32)
            s.activation(CRS[0:16, :], CR[0:16, :], ACT.Silu).then_inc(c_silu, 1)

            for l in range(DEPTH):
                nq = TILES if l == 0 else 2
                n_ln = TOK if l == 0 else S_LAT
                if l == 0:
                    act.wait_ge(x_in, 32)
                    for t in range(TILES):
                        s.activation(YS[:, t], X[:, t], ACT.Square, accum_out=ss[:, t:t + 1]).then_inc(ss_done, 1)
                    act.wait_ge(lam_sum, 1)
                    s.activation(lamx[:], lamx[:], ACT.Exp).then_inc(lam_exp, 1)
                act.wait_ge(ab_done, l + 1)
                for q in range(1, 8, 2):
                    key = ("nT", l, q)
                    wait_made(act, key)
                    cnd, kk = q // 4, 2 * (q % 4)
                    for a in range(2):
                        last = s.activation(HT[:, kk + a, cnd * 256:cnd * 256 + 256], bank(key)[:, a * 256:a * 256 + 256], ACT.Identity,
                                            bias=AB[:, l, cnd, 0, kk + a:kk + a + 1], scale=AB[:, l, cnd, 1, kk + a:kk + a + 1])
                    taken(last, key)
                barrier(act, bar(l, 1))

                staged = [j for j in in_jobs(l) if j[0] in ("ka", "b", "qa")]

                def st_free(job):
                    k = staged.index(job)
                    if k >= 2:
                        wait_made(act, ("inT", l) + staged[k - 2])

                def copy_T(job):
                    seg, t = job
                    key = ("inT", l) + job
                    wait_made(act, key)
                    src = bank(key).rearrange("p (b t) -> p b t", b=4)
                    cols = slice(t * P, (t + 1) * P)
                    if seg == "b":
                        if t < 2 or l == 0:
                            s.activation(qT[:, 4:6, cols], src[:, 0:2], ACT.Identity)
                        last = s.activation(kT[:, 4:6, cols], src[:, 2:4], ACT.Identity)
                    else:
                        last = s.activation((qT if seg == "qa" else kT)[:, 0:4, cols], src, ACT.Identity)
                    taken(last, key)

                prev = None
                for job in in_jobs(l):
                    seg, t = job
                    key = ("in", l) + job
                    stg = ST[:, staged.index(job) % 2] if job in staged else None
                    if seg == "uc" and t >= 2:
                        wait_made(act, key)
                        taken(s.activation(G[:, t - 2, 0:n_ln], bank(key)[:, 0:n_ln], ACT.Exp, scale=-1.0), key)
                        if t == 3:
                            act.drain().then_inc(g_exp, 1)
                    elif seg == "va":
                        wait_made(act, key)
                        taken(s.activation(V[:, t, 0:512], bank(key), ACT.Identity), key)
                        if t == 1:
                            act.wait_ge(ln_d, l + 1)
                            s.activation(G[:, :, 0:n_ln], acc[:, :, 0:n_ln], ACT.Square).then_inc(ln_sq, 1)
                        if t == 3:
                            act.wait_ge(ln_v, l + 1)
                            s.activation(G[:, 1, 0:n_ln], G[:, 0, 0:n_ln], ACT.Sqrt).then_inc(ln_r, 1)
                            act.wait_ge(ln_n, l + 1)
                            for c2 in range(2):
                                last = s.activation(G[:, c2, 0:n_ln], acc[:, c2, 0:n_ln], ACT.Exp, bias=NC[:, l, 2 + c2:3 + c2], scale=NC[:, l, c2:c2 + 1])
                            last.then_inc(ln_e, 1)
                    elif seg in ("ka", "qa") and t >= 2:
                        wait_made(act, key)
                        st_free(job)
                        taken(s.activation(stg, bank(key), ACT.Identity), key)
                    elif seg == "b" and t >= 2:
                        wait_made(act, key)
                        st_free(job)
                        if l == 0:
                            s.activation(stg[:, 0:256], bank(key)[:, 0:256], ACT.Identity)
                        for a in range(2):
                            s.activation(stg[:, 256 + a * 64:].rearrange("p (j d) -> p j d", d=64)[:, 0::2],
                                         bank(key)[:, 256:384].rearrange("p (j d) -> p j d", d=64), ACT.Identity)
                        taken(s.activation(V[:, t, 512:640], bank(key)[:, 384:512], ACT.Identity), key)
                    if prev:
                        copy_T(prev)
                    prev = job if job in staged else None
                if prev:
                    copy_T(prev)
                barrier(act, bar(l, 2))

                units, tj = units_of(l), t_jobs(l)

                def exps(n):
                    i, u = units[n]
                    kw = TOK if i < 2 else S_CTX
                    b = n % 2
                    act.wait_ge(nm_done[l], n + 1)
                    if u < BLK_A:
                        prior = [k for k, (a, _) in enumerate(tj) if a == n - 2]
                        if prior:
                            wait_made(act, ("T", l, prior[-1]))
                        for m in range(2):
                            key = ("S", l, n, m)
                            taken(s.activation(PB[:, b, m, 0:kw], bank(key)[:, 0:kw], ACT.Exp, bias=nm[:, b, m:m + 1], scale=HD ** -0.5,
                                               accum_out=sums[:, b, m:m + 1]), key)
                    else:
                        for m in range(2):
                            h = 2 * (u - BLK_A) + m
                            s.activation(es[:, b, m:m + 1], sink[:, l, h:h + 1], ACT.Exp, bias=nm[:, b, m:m + 1])
                            last = s.activation(PB[:, b, m, 0:kw], PB[:, b, m, 0:kw], ACT.Exp, bias=nm[:, b, m:m + 1],
                                                accum_out=sums[:, b, m:m + 1])
                        last.then_inc(ex_done[l], 1)

                def copy_aT(k):
                    n, m = tj[k]
                    kw = TOK if units[n][0] < 2 else S_CTX
                    key = ("T", l, k)
                    wait_made(act, key)
                    if k >= 2:
                        wait_made(act, ("O", l, k - 2))
                    taken(s.activation(aT[:, k % 2, 0:kw], bank(key)[:, 0:kw], ACT.Identity), key)

                def mixed(i):
                    cols = slice(i * P, (i + 1) * P)
                    wait_made(act, ("MA", l, i))
                    taken(s.activation(HT[:, 0:4, cols], bank(("MA", l, i)).rearrange("p (b t) -> p b t", b=4), ACT.Identity,
                                       scale=NC[:, l, 4:5]), ("MA", l, i))
                    wait_made(act, ("MB", l, i))
                    taken(s.activation(HT[:, 4:6, cols], bank(("MB", l, i))[:, 0:256].rearrange("p (b t) -> p b t", b=2), ACT.Identity), ("MB", l, i))

                exps(0)
                exps(1)
                for st_ in attention_steps(l):
                    if st_[0] == "T":
                        copy_aT(st_[1])
                        n, m = tj[st_[1]]
                        if n + 2 < len(units) and m == (0 if units[n][1] < BLK_A else 1):
                            exps(n + 2)
                    elif st_[0] == "M":
                        mixed(st_[1])
                barrier(act, bar(l, 3))

                def second(i):
                    act.wait_ge(x_add[l], i + 1)
                    s.activation(H2[:, i], X[:, i], ACT.Square, accum_out=ss[:, i:i + 1]).then_inc(ss2[l], 1)

                def route(i):
                    act.wait_ge(h2_done[l], i + 1)
                    act.dma_start(h2D[l].rearrange("(t p) d -> t p d", p=P)[i], H2[:, i]).then_inc(h2_out[l], 16)
                    for h in range(2):
                        key = ("h2T", l, i, h)
                        wait_made(act, key)
                        if i:
                            wait_made(act, ("rt", l, i - 1))
                        taken(s.activation(hTr[:, 4 * h:4 * h + 4], bank(key).rearrange("p (b t) -> p b t", b=4), ACT.Identity), key)
                    key = ("rt", l, i)
                    wait_made(act, key)
                    taken(s.activation(e_t[:, i], bank(key)[:, 0:E_N], ACT.Exp, scale=-1.0), key)

                for i in range(nq):
                    second(i)
                    if i:
                        route(i - 1)
                route(nq - 1)
                act.drain().then_inc(h2_done[l], 1)
                barrier(act, bar(l, 4))

                act.wait_ge(nb_ready, l + 1)
                done = act.alloc_register(f"act_blocks_{l}")
                act.reg_mov(done, 0)

                def step():
                    b = act.snap(done)
                    act.wait_ge(w13_full[l], b + 1)
                    s.activation(sg[0:SLOT, :], ps[0:SLOT, B_W13, :], ACT.Silu).then_inc(si_rdy[l], 1)
                    act.reg_add(done, done, 1)

                with act.Fori(0, E_N) as e:
                    blocks = act.value_load(nb[0:1, bass.ds(e, 1)], min_val=0, max_val=JMAX)
                    step()
                    with act.If(blocks > 1):
                        with act.Fori(1, blocks):
                            step()
                barrier(act, bar(l, 5))
                y_v = yD[l].rearrange("(k t p) d -> p t k d", k=2, p=P)
                for i in range(nq):
                    for k in range(2):
                        act.dma_start(Y[:, i, k], y_v[:, i, k]).then_inc(y_in[i], 16)
                for i in range(nq):
                    act.wait_ge(comb[l], i + 1)
                    s.activation(SQ[:, i], X[:, i], ACT.Square, accum_out=ss[:, i:i + 1]).then_inc(ss_done, 1)
                if l == DEPTH - 1:
                    for i in range(2):
                        act.wait_ge(fin_o, i + 1)
                        act.dma_start(A["out"].rearrange("b (t p) d -> p (b t) d", p=P)[:, i], X[:, i]).then_inc(stored, 16)
                    act.wait_ge(stored, 32)
                    barrier(act, bar(l, 6))

        @block.vector
        def _(dve):
            v = nc.vector
            wait_made(dve, ("c",))
            dve.wait_ge(setup, 1)
            taken(v.tensor_copy(SC[:, :, 0:2], bank(("c",))[:, 0:16].rearrange("p (c k) -> p k c", c=2)), ("c",))

            def parameters():
                wait_made(dve, ("par",))
                taken(v.tensor_copy(PC[:].rearrange("p l a -> p (l a)"), bank(("par",))[:, 0:DEPTH * 15]), ("par",))
                wait_made(dve, ("cw",))
                taken(v.tensor_copy(CW[:].rearrange("p c k -> p (c k)"), bank(("cw",))[:, 0:2 * DEPTH * KCONV]), ("cw",))
                dve.wait_ge(par_in, 16 * N_PAR)
                v.tensor_tensor(DLP, DL[:, :, 0::2], DL[:, :, 1::2], ALU.mult)
                dve.drain()
                for l in range(DEPTH):
                    v.tensor_scalar(NC[:, l, 0:4], PC[:, l, 11:15], -1.0, None, ALU.mult)
                    v.tensor_scalar(NC[:, l, 4:5], PC[:, l, 8:9], 1.0 - lambda_init(l), None, ALU.mult)
                v.tensor_reduce(lamx[:], DLP, AX.X, ALU.add).then_inc(lam_sum, 1)
                dve.wait_ge(lam_exp, 1)
                for l in range(DEPTH):
                    v.scalar_tensor_tensor(neglam[:, l:l + 1], lamx[:, l, 1:2], -lambda_init(l), lamx[:, l, 0:1], ALU.add, ALU.subtract)

            def mod_rows(key):
                n = MODS.index(key)
                wait_made(dve, ("ada",) + key)
                dve.wait_ge(bias_in[n % 2], 64 * (n // 2 + 1))
                stored_before = [k for k in MODS[:n] if k in mod_out]
                if key in mod_out and stored_before:
                    dve.wait_ge(mod_out[stored_before[-1]], 64)
                taken(v.tensor_tensor(mst if key in mod_out else mst0, bank(("ada",) + key), bias_of(n), ALU.add), ("ada",) + key)
                dve.drain().then_inc(mod_sb, 1)

            def mod_columns(l):
                key = ("modc", l)
                wait_made(dve, key)
                cols = bank(key).rearrange("p (b j r) -> p b j r", b=4, j=4)
                for cnd in range(2):
                    dst = [AB[:, l, cnd, w].rearrange("p (j b) -> p b j", b=4) for w in range(2)]
                    v.tensor_copy(dst[0], cols[:, :, 0:2, cnd])
                    last = v.scalar_tensor_tensor(dst[1], cols[:, :, 2:4, cnd], 1.0, PC[:, l, 0:8].rearrange("p (j b) -> p b j", b=4), ALU.add, ALU.mult)
                taken(last, key)
                dve.drain().then_inc(ab_done, 1)

            for l in range(DEPTH):
                nq = TILES if l == 0 else 2
                conds = nq // 2
                n_ln = TOK if l == 0 else S_LAT
                n_seq = conds

                for t in range(TILES):
                    dve.wait_ge(rs_done, TILES * l + t + 1)
                    last = v.tensor_scalar(YS[:, t], X[:, t], rstd[:, t:t + 1], None, ALU.mult)
                last.then_inc(y_done, 1)
                if l == 0:
                    parameters()
                    mod_rows((0, 0))
                    mod_columns(0)
                for q in range(0, 8, 2):
                    key = ("nT", l, q)
                    wait_made(dve, key)
                    cnd, kk = q // 4, 2 * (q % 4)
                    for a in range(2):
                        last = v.tensor_scalar(HT[:, kk + a, cnd * 256:cnd * 256 + 256], bank(key)[:, a * 256:a * 256 + 256],
                                               AB[:, l, cnd, 1, kk + a:kk + a + 1], AB[:, l, cnd, 0, kk + a:kk + a + 1], ALU.mult, ALU.add)
                    taken(last, key)
                barrier(dve, bar(l, 1))

                staged = [j for j in in_jobs(l) if j[0] in ("ka", "b", "qa")]

                def conv_taps():
                    for k in range(KCONV):
                        for c2 in range(2):
                            src = zpad[:, c2, 0:n_seq, k:k + S_LAT]
                            dst = acc[:, c2, 0:n_ln].rearrange("p (s t) -> p s t", s=n_seq)
                            w = CW[:, c2, l * KCONV + k:l * KCONV + k + 1]
                            if k == 0:
                                v.tensor_scalar(dst, src, w, PC[:, l, 9 + c2:10 + c2], ALU.mult, ALU.add)
                            else:
                                v.scalar_tensor_tensor(dst, src, w, dst, ALU.mult, ALU.add)
                            if c2 == 1:
                                dve.drain()
                            yield

                taps = conv_taps()

                def conv(n):
                    for _ in range(n):
                        next(taps, None)

                def rope(job, n_heads, outs):
                    dve.drain()
                    key = ("in", l) + job
                    t = job[1]
                    w = n_heads * HD
                    cosv = cst[:, C_ROPE + t * 128:C_ROPE + t * 128 + 64].unsqueeze(1).to_broadcast([P, n_heads, 64])
                    x_ = bank(key)[:, 0:w]
                    v.tensor_tensor(RT[:, 0, 0:w].rearrange("p (h d) -> p h d", d=64), x_.rearrange("p (h d) -> p h d", d=64), cosv, ALU.mult)
                    xs = x_.rearrange("p (h a f) -> p h a f", a=4, f=16)
                    r1 = RT[:, 1, 0:w].rearrange("p (h a f) -> p h a f", a=4, f=16)
                    sn = cst[:, C_ROPE + t * 128 + 64:C_ROPE + t * 128 + 128].rearrange("p (a f) -> p a f", f=16).unsqueeze(1)
                    for hh in range(2):
                        v.tensor_tensor(r1[:, :, hh::2], xs[:, :, 1 - hh::2], sn[:, :, hh::2].to_broadcast([P, n_heads, 2, 16]), ALU.mult)
                    dve.drain()
                    last = None
                    for dst, c0, c1 in outs:
                        a0, a1 = RT[:, 0, c0:c1], RT[:, 1, c0:c1]
                        if len(dst.shape) == 3:
                            a0, a1 = (a_.rearrange("p (j d) -> p j d", d=64) for a_ in (a0, a1))
                        last = v.tensor_tensor(dst, a0, a1, ALU.add)
                    return last

                dve.wait_ge(pads, l + 1)
                plan_taps = iter((10, 10, 24, 8))

                def layer_norm():
                    conv(2 * KCONV)
                    dve.drain().then_inc(cv_d, 1)
                    if l == 0:
                        mod_rows((1, 0))
                    key = ("mu", l)
                    wait_made(dve, key)
                    for c2 in range(2):
                        last = v.scalar_tensor_tensor(acc[:, c2, 0:n_ln], bank(key)[:, 0:n_ln], -1.0 / CH, acc[:, c2, 0:n_ln], ALU.mult, ALU.add)
                    taken(last, key)
                    dve.drain().then_inc(ln_d, 1)
                    key = ("var", l)
                    wait_made(dve, key)
                    taken(v.tensor_scalar(G[:, 0, 0:n_ln], bank(key)[:, 0:n_ln], 1.0 / CH, EPS, ALU.mult, ALU.add), key)
                    dve.drain().then_inc(ln_v, 1)
                    if l == 0:
                        mod_rows((1, 1))
                    dve.wait_ge(ln_r, l + 1)
                    v.reciprocal(G[:, 1, 0:n_ln], G[:, 1, 0:n_ln])
                    dve.drain()
                    for c2 in range(2):
                        last = v.tensor_tensor(acc[:, c2, 0:n_ln], acc[:, c2, 0:n_ln], G[:, 1, 0:n_ln], ALU.mult)
                    last.then_inc(ln_n, 1)

                for job in in_jobs(l):
                    seg, t = job
                    key = ("in", l) + job
                    if seg == "uc" and t < 2:
                        if t == 0:
                            dve.wait_ge(g_exp, l + 1)
                            v.tensor_scalar(G[:, :, 0:n_ln], G[:, :, 0:n_ln], 1.0, None, ALU.add)
                            dve.drain()
                            v.reciprocal(G[:, :, 0:n_ln], G[:, :, 0:n_ln])
                            dve.drain()
                        wait_made(dve, key)
                        taken(v.tensor_tensor(zpad[:, t, 0:n_seq, PADC:PADC + S_LAT], bank(key)[:, 0:n_ln].rearrange("p (s t) -> p s t", s=n_seq),
                                              G[:, t, 0:n_ln].rearrange("p (s t) -> p s t", s=n_seq), ALU.mult), key)
                        if t == 1:
                            dve.drain()
                    elif seg in ("ka", "b", "qa") and t < 2:
                        if seg != "qa":
                            conv(next(plan_taps))
                        if l == 0 and t == 0 and seg in ("ka", "b"):
                            mod_rows((0, 1) if seg == "ka" else (0, 2))
                        if seg == "qa" and t == 0:
                            layer_norm()
                        wait_made(dve, key)
                        k = staged.index(job)
                        if k >= 2:
                            wait_made(dve, ("inT", l) + staged[k - 2])
                        stg = ST[:, k % 2]
                        if seg == "b":
                            v.tensor_copy(V[:, t, 512:640], bank(key)[:, 384:512])
                            dup = [stg[:, 256 + a * 64:].rearrange("p (j d) -> p j d", d=64)[:, 0::2] for a in range(2)]
                            last = rope(job, 6, [(stg[:, 0:256], 0, 256), (dup[0], 256, 384), (dup[1], 256, 384)])
                        else:
                            last = rope(job, 8, [(stg, 0, 512)])
                        taken(last, key)
                dve.wait_ge(ln_e, l + 1)
                v.tensor_scalar(G[:, :, 0:n_ln], G[:, :, 0:n_ln], 1.0, None, ALU.add)
                for c2 in range(2):
                    v.tensor_scalar(acc[:, c2, 0:n_ln], acc[:, c2, 0:n_ln], PC[:, l, 11 + c2:12 + c2], PC[:, l, 13 + c2:14 + c2], ALU.mult, ALU.add)
                dve.drain()
                v.reciprocal(G[:, :, 0:n_ln], G[:, :, 0:n_ln])
                dve.drain()
                if l == 0:
                    mod_rows((1, 2))
                    mod_columns(1)
                wait_made(dve, ("in", l) + in_jobs(l)[-1])
                v.tensor_tensor(HT[:, 6:8, 0:n_ln], acc[:, :, 0:n_ln], G[:, :, 0:n_ln], ALU.mult)
                barrier(dve, bar(l, 2))

                units, tj = units_of(l), t_jobs(l)

                def maxima(n):
                    i, u = units[n]
                    kw = TOK if i < 2 else S_CTX
                    b = n % 2
                    pair = ps[:, 2 * b:2 * b + 2, :]
                    for m in range(2):
                        wait_made(dve, ("S", l, n, m))
                    if u < BLK_A:
                        v.tensor_reduce(mx[:, b], pair[:, :, 0:kw], AX.X, ALU.max)
                        dve.drain()
                        v.tensor_scalar(nm[:, b], mx[:, b], -HD ** -0.5, None, ALU.mult).then_inc(nm_done[l], 1)
                        return
                    prior = [k for k, (a, _) in enumerate(tj) if a == n - 2]
                    wait_made(dve, ("T", l, prior[-1]))
                    for m in range(2):
                        if i < 2:
                            v.scalar_tensor_tensor(PB[:, b, m, 0:256], pair[:, m, 0:256], HD ** -0.5,
                                                   cst[:, C_MASK + i * 256:C_MASK + (i + 1) * 256], ALU.mult, ALU.add)
                        last = v.tensor_scalar(PB[:, b, m, kw - 256:kw], pair[:, m, kw - 256:kw], HD ** -0.5, None, ALU.mult)
                        taken(last, ("S", l, n, m))
                    dve.drain()
                    v.tensor_reduce(mx[:, b], PB[:, b, :, 0:kw], AX.X, ALU.max)
                    dve.drain()
                    h = 2 * (u - BLK_A)
                    v.tensor_tensor(mx[:, b], mx[:, b], sink[:, l, h:h + 2], ALU.max)
                    dve.drain()
                    v.tensor_scalar(nm[:, b], mx[:, b], -1.0, None, ALU.mult).then_inc(nm_done[l], 1)

                def probs(n):
                    i, u = units[n]
                    kw = TOK if i < 2 else S_CTX
                    b = n % 2
                    if u < BLK_A:
                        wait_taken(dve, ("S", l, n, 1))
                        v.reciprocal(rec[:, n % 4], sums[:, b])
                        dve.drain()
                        v.scalar_tensor_tensor(cf[:, b:b + 1], sums[:, b, 0:1], neglam[:, l:l + 1], rec[:, n % 4, 1:2], ALU.mult, ALU.mult)
                        dve.drain()
                        v.scalar_tensor_tensor(PB[:, b, 0, 0:kw], PB[:, b, 1, 0:kw], cf[:, b:b + 1], PB[:, b, 0, 0:kw], ALU.mult, ALU.add).then_inc(pr_done[l], 1)
                    else:
                        dve.wait_ge(ex_done[l], sum(1 for _, x_ in units[:n + 1] if x_ >= BLK_A))
                        v.tensor_tensor(sums[:, b], sums[:, b], es[:, b], ALU.add)
                        dve.drain()
                        v.reciprocal(rec[:, n % 4], sums[:, b]).then_inc(pr_done[l], 1)

                def take_o(k):
                    n, m = tj[k]
                    i, u = units[n]
                    key = ("O", l, k)
                    wait_made(dve, key)
                    if u == 0 and i >= 2:
                        wait_made(dve, ("MB", l, i - 2))
                    w = P if u < BLK_A else HD
                    taken(v.tensor_scalar(O[i % 2][:, u * P + m * HD:u * P + m * HD + w], bank(key)[:, 0:w], rec[:, n % 4, m:m + 1], None, ALU.mult), key)
                    if u == BLK - 1 and m == 1:
                        dve.drain()
                        v.tensor_tensor(G[:, 0], O[i % 2][:, 0:512], O[i % 2][:, 0:512], ALU.mult)
                        dve.drain()
                        v.tensor_reduce(ss4[:, i % 2], G[:, 0].rearrange("p (h d) -> p h d", h=4), AX.X, ALU.add).then_inc(o_ss[l], 1)

                def head_norm(i):
                    dve.wait_ge(o_rs[l], i + 1)
                    oa = O[i % 2][:, 0:512].rearrange("p (h d) -> p h d", h=4)
                    v.tensor_tensor(oa, oa, rs4[:, i % 2].unsqueeze(2).to_broadcast([P, 4, P]), ALU.mult).then_inc(o_done[l], 1)

                maxima(0)
                maxima(1)
                for st_ in attention_steps(l):
                    if st_[0] == "T" and tj[st_[1]][1] == 0:
                        n = tj[st_[1]][0]
                        probs(n)
                        if n + 2 < len(units):
                            maxima(n + 2)
                    elif st_[0] == "O":
                        take_o(st_[1])
                    elif st_[0] == "M":
                        head_norm(st_[1])
                barrier(dve, bar(l, 3))

                def add_out(i):
                    cnd = i // 2
                    if i == 0:
                        dve.wait_ge(gate_in[l], 16 * conds)
                    for h in range(OUT_N):
                        key = ("wo", l, i, h)
                        wait_made(dve, key)
                        taken(v.tensor_tensor(tmp[:, h], bank(key), gate[:, cnd, h * CHUNK:(h + 1) * CHUNK], ALU.mult), key)
                    dve.drain()
                    v.tensor_tensor(X[:, i], X[:, i], tmp.rearrange("p b k -> p (b k)"), ALU.add)
                    dve.drain().then_inc(x_add[l], 1)

                def make_h2(i):
                    cnd = i // 2
                    dve.wait_ge(rs2[l], i + 1)
                    v.scalar_tensor_tensor(H2[:, i], X[:, i], rstd[:, i:i + 1], BC[:, cnd, 1], ALU.mult, ALU.mult)
                    dve.drain()
                    v.tensor_tensor(H2[:, i], H2[:, i], BC[:, cnd, 0], ALU.add).then_inc(h2_done[l], 1)

                dve.wait_ge(bc_in[l], 16 * (2 * conds + 1))
                for cnd in range(conds):
                    v.scalar_tensor_tensor(BC[:, cnd, 1], BC[:, cnd, 1], 1.0, GF, ALU.add, ALU.mult)
                dve.drain()
                for i in range(nq):
                    add_out(i)
                    if i:
                        make_h2(i - 1)
                make_h2(nq - 1)

                def T3(x_, n=E_N):
                    return x_[:, 0:nq]

                def over(x_, n):
                    return x_[:, 0:nq].unsqueeze(2).to_broadcast([P, nq, n])

                def consts(c0, n):
                    return cst[:, c0:c0 + n].unsqueeze(1).to_broadcast([P, nq, n])

                dve.wait_ge(h2_done[l], nq + 1)
                v.tensor_scalar(T3(e_s), T3(e_t), 1.0, None, ALU.add)
                dve.drain()
                v.reciprocal(T3(e_s), T3(e_s))
                dve.drain()
                v.tensor_tensor(T3(e_b), T3(e_s), rb[:].unsqueeze(1).to_broadcast([P, nq, E_N]), ALU.add)
                dve.drain()
                four = T3(e_b).rearrange("p t (g e) -> p (t g) e", e=4)
                ng = nq * E_G
                for a in range(2):
                    for o_, op in ((0, ALU.max), (1, ALU.min)):
                        v.tensor_tensor(hl[:, 2 * o_ + a, 0:ng], four[:, :, 2 * a], four[:, :, 2 * a + 1], op)
                dve.drain()
                gv = T3(grp).rearrange("p t g -> p (t g)")
                v.tensor_tensor(gv, hl[:, 0, 0:ng], hl[:, 1, 0:ng], ALU.max)
                v.tensor_tensor(T3(geq).rearrange("p t g -> p (t g)"), hl[:, 0, 0:ng], hl[:, 1, 0:ng], ALU.min)
                v.tensor_tensor(T3(gcd).rearrange("p t g -> p (t g)"), hl[:, 2, 0:ng], hl[:, 3, 0:ng], ALU.max)
                dve.drain()
                v.tensor_tensor(T3(geq), T3(geq), T3(gcd), ALU.max)
                dve.drain()
                v.tensor_tensor(T3(grp), T3(grp), T3(geq), ALU.add)
                dve.drain()

                def first_max(val, n, c_iota, mxv, eq, cand, low, out):
                    v.tensor_reduce(mxv[:, 0:nq], T3(val), AX.X, ALU.max)
                    dve.drain()
                    v.tensor_tensor(T3(eq), T3(val), over(mxv, n), ALU.is_ge)
                    dve.drain()
                    v.scalar_tensor_tensor(T3(cand), T3(eq), -float(n), consts(c_iota, n), ALU.mult, ALU.add)
                    dve.drain()
                    v.tensor_reduce(low[:, 0:nq], T3(cand), AX.X, ALU.min)
                    dve.drain()
                    v.tensor_tensor(T3(out), T3(cand), over(low, n), ALU.is_equal)
                    dve.drain()

                first_max(grp, E_G, C_I4, gm, geq, gcd, cm, gone)
                v.tensor_scalar(T3(gneg), T3(gone), BIG, -BIG, ALU.mult, ALU.add)
                e4 = [T3(x_).rearrange("p t (g e) -> p (t g) e", e=4) for x_ in (e_v, e_b)]
                gb = [T3(x_).rearrange("p t g -> p (t g)").unsqueeze(2).to_broadcast([P, ng, 4]) for x_ in (gone, gneg)]
                dve.drain()
                v.tensor_tensor(e4[0], e4[1], gb[0], ALU.mult)
                dve.drain()
                v.tensor_tensor(e4[0], e4[0], gb[1], ALU.add)
                dve.drain()
                first_max(e_v, E_N, C_I16, vm, e_eq, e_t, cmk0, oh[0])
                v.scalar_tensor_tensor(T3(e_v), T3(oh[0]), -3.0 * BIG, T3(e_v), ALU.mult, ALU.add)
                dve.drain()
                first_max(e_v, E_N, C_I16, vm, e_eq, e_t, cmk1, oh[1])
                v.tensor_tensor(T3(MM), T3(oh[0]), T3(oh[1]), ALU.add).then_inc(m_done, 1)
                v.memset(PM[:, 0], 0.0)
                for i in range(nq):
                    dve.drain()
                    last = v.tensor_tensor(PM[:, i + 1], PM[:, i], MM[:, i], ALU.add)
                last.then_inc(m_done, 1)
                for k, wk in ((0, w0), (1, w1k)):
                    v.tensor_tensor(T3(e_t), T3(e_s), T3(oh[k]), ALU.mult)
                    dve.drain()
                    v.tensor_reduce(wk[:, 0:nq], T3(e_t), AX.X, ALU.add)
                    dve.drain()
                v.tensor_tensor(wsum[:, 0:nq], w0[:, 0:nq], w1k[:, 0:nq], ALU.add)
                dve.drain()
                v.reciprocal(wsum[:, 0:nq], wsum[:, 0:nq])
                v.memset(PLi[:, :, :, 3:4], 0)
                dve.drain()
                for k, wk in ((0, w0), (1, w1k)):
                    v.tensor_tensor(PLf[:, k, 0:nq, 2], wk[:, 0:nq], wsum[:, 0:nq], ALU.mult)
                    v.tensor_copy(PLi[:, k, 0:nq, 0], cst[:, C_TOK:C_TOK + nq])
                    v.tensor_scalar(PLi[:, k, 0:nq, 1], cst[:, C_TOK:C_TOK + nq], float(k * routed(l)), None, ALU.add)
                key = ("rk", l)
                wait_made(dve, key)
                for k in range(2):
                    v.tensor_tensor(T3(e_t), bank(key)[:, 0:nq * E_N].rearrange("p (t e) -> p t e", e=E_N), T3(oh[k]), ALU.mult)
                    dve.drain()
                    v.tensor_reduce(rkf[:, k, 0:nq], T3(e_t), AX.X, ALU.add)
                    dve.drain()
                taken(v.tensor_copy(nbi[0:1, :], bank(key)[0:1, TILES * E_N:(TILES + 1) * E_N]), key)
                v.tensor_copy(rki[:, :, 0:nq], rkf[:, :, 0:nq])
                dve.drain()
                v.tensor_scalar(nbi[0:1, :], nbi[0:1, :], float(SLOT - 1), None, ALU.add)
                v.tensor_scalar(ji[:, :, 0:nq], rki[:, :, 0:nq], 6, None, ALU.arith_shift_right)
                v.tensor_scalar(pi[:, :, 0:nq], rki[:, :, 0:nq], SLOT - 1, None, ALU.bitwise_and)
                dve.drain()
                v.tensor_scalar(nb[0:1, :], nbi[0:1, :], 6, None, ALU.arith_shift_right)
                v.scalar_tensor_tensor(rowf[:, :, 0:nq], pi[:, :, 0:nq], float(E_N * JMAX), ji[:, :, 0:nq], ALU.mult, ALU.add)
                dve.drain()
                for k, low in ((0, cmk0), (1, cmk1)):
                    v.scalar_tensor_tensor(rowf[:, k, 0:nq], low[:, 0:nq], float(JMAX), rowf[:, k, 0:nq], ALU.mult, ALU.add)
                dve.drain()
                v.tensor_scalar(ROWI[:, :, 0:nq], rowf[:, :, 0:nq], float(E_N * JMAX), None, ALU.add)
                dve.drain().then_inc(pl_done, 1)
                barrier(dve, bar(l, 4))
                dve.drain().then_inc(nb_ready, 1)

                dve.wait_ge(tb_in[l], 16)
                dve.sem_inc(y_rdy[l], 1)
                done = dve.alloc_register(f"dve_blocks_{l}")
                dve.reg_mov(done, 0)

                def copy_gT(b):
                    dve.wait_ge(gt_full[l], b)
                    v.tensor_copy(gT.rearrange("p k s -> p (k s)"), ps[:, B_GT, 0:4 * SLOT]).then_inc(gt_rdy[l], 1)

                def copy_y(b):
                    dve.wait_ge(w2_full[l], b)
                    dve.wait_ge(scat[l], 16 * b + 16)
                    v.tensor_copy(ym[0:SLOT, 0:CHUNK], ps[0:SLOT, B_W2, :])
                    v.tensor_copy(ym[0:SLOT, CHUNK:D], ps[SLOT:P, B_W2, :]).then_inc(y_rdy[l], 1)

                def step(col, first=False):
                    b = dve.snap(done)
                    dve.wait_ge(xt_full[l], b + 2)
                    v.tensor_copy(xT.rearrange("p k s -> p (k s)"), ps[:, B_XT, :]).then_inc(xt_rdy[l], 1)
                    if not first:
                        copy_gT(b)
                    dve.wait_ge(si_rdy[l], b + 1)
                    v.scalar_tensor_tensor(gg[0:SLOT, :], sg[0:SLOT, :], TBf[0:SLOT, bass.ds(4 * col + 2, 1)], ps[SLOT:P, B_W13, :],
                                           ALU.mult, ALU.mult).then_inc(g_rdy[l], 1)
                    if first:
                        dve.wait_ge(scat[l], 16)
                        dve.sem_inc(y_rdy[l], 1)
                    else:
                        copy_y(b)
                    dve.reg_add(done, done, 1)

                def expert(e, first=False):
                    blocks = dve.value_load(nb[0:1, bass.ds(e, 1)], min_val=0, max_val=JMAX)
                    step(e * JMAX, first)
                    with dve.If(blocks > 1):
                        with dve.Fori(1, blocks) as j:
                            step(e * JMAX + j)

                expert(0, True)
                with dve.Fori(1, E_N) as e:
                    expert(e)
                b = dve.snap(done)
                copy_gT(b)
                copy_y(b)
                barrier(dve, bar(l, 5))

                dve.wait_ge(gate2_in, 16 * (2 * l + conds))
                for i in range(nq):
                    dve.wait_ge(y_in[i], 32 * (l + 1))
                    v.tensor_tensor(Y[:, i, 0], Y[:, i, 0], Y[:, i, 1], ALU.add)
                    dve.drain()
                    v.tensor_tensor(Y[:, i, 0], Y[:, i, 0], gate[:, i // 2], ALU.mult)
                    dve.drain()
                    v.tensor_tensor(X[:, i], X[:, i], Y[:, i, 0], ALU.add).then_inc(comb[l], 1)
                if l == DEPTH - 1:
                    dve.wait_ge(fin_g, 16)
                    for i in range(2):
                        dve.wait_ge(rs_done, TILES * DEPTH + i + 1)
                        v.scalar_tensor_tensor(X[:, i], X[:, i], rstd[:, i:i + 1], GFIN, ALU.mult, ALU.mult).then_inc(fin_o, 1)
                if l == DEPTH - 1:
                    barrier(dve, bar(l, 6))

        @block.tensor
        def _(pe):
            t_ = nc.tensor

            def mm(out, lhsT, rhs, first, last_):
                return t_.matmul(out, lhsT, rhs, start=first, stop=last_)

            pe.wait_ge(cst_in, 16)
            pe.wait_ge(c_silu, 1)
            made(t_.transpose(bank(("c",))[:, 0:16], CRS[0:16, :], ident[0:16, 0:16]), ("c",))

            def parameters():
                pe.wait_ge(par_in, 16 * N_PAR)
                made(t_.transpose(bank(("par",))[:, 0:DEPTH * 15], PR[0:DEPTH * 15, :], ident[0:DEPTH * 15, 0:DEPTH * 15]), ("par",))
                nk = DEPTH * KCONV
                for c2 in range(2):
                    last = t_.transpose(bank(("cw",))[:, c2 * nk:(c2 + 1) * nk], CWR[0:nk, c2 * P:(c2 + 1) * P], ident[0:nk, 0:nk])
                made(last, ("cw",))

            def mod_columns(l):
                key = ("modc", l)
                pe.wait_ge(mod_sb, MODS.index((l, 0)) + 1)
                claim(pe, key)
                for b in range(4):
                    last = t_.transpose(bank(key)[:, b * P:(b + 1) * P], mst0[:, b * P:(b + 1) * P], ident)
                made(last, key)

            def ada(l, q):
                key = ("ada", l, q)
                claim(pe, key)
                for j in range(4):
                    arrived(pe, 0, ("ada", l, 4 * q + j))
                for k in range(KD):
                    for j in range(4):
                        last = mm(bank(key)[32 * j:32 * j + 32, :], SC[:, k], ring[:, slot(0, ("ada", l, 4 * q + j)), k], k == 0, k == KD - 1)
                made(last, key)
                for j in range(4):
                    pe.drain().then_inc(ring_free[slot(0, ("ada", l, 4 * q + j))], 1)

            for l in range(DEPTH):
                nq = TILES if l == 0 else 2
                n_ln = TOK if l == 0 else S_LAT
                pe.wait_ge(y_done, l + 1)
                for q in range(8):
                    if l == 0 and q == 4:
                        parameters()
                        wait_taken(pe, ("c",))
                        ada(0, 0)
                        mod_columns(0)
                    key = ("nT", l, q)
                    claim(pe, key)
                    cnd, kk = q // 4, 2 * (q % 4)
                    for a in range(2):
                        for t in range(2):
                            last = t_.transpose(bank(key)[:, a * 256 + t * P:a * 256 + (t + 1) * P],
                                                YS[:, 2 * cnd + t, (kk + a) * P:(kk + a + 1) * P], ident)
                    made(last, key)
                barrier(pe, bar(l, 1))

                def transposes(job):
                    key = ("inT", l) + job
                    wait_taken(pe, ("in", l) + job)
                    claim(pe, key)
                    stg = ST[:, staged.index(job) % 2]
                    for b in range(2 if job[0] == "b" and job[1] >= 2 and l else 0, 4):
                        last = t_.transpose(bank(key)[:, b * P:(b + 1) * P], stg[:, b * P:(b + 1) * P], ident)
                    made(last, key)

                def channel_sums(name):
                    if name == "mu":
                        pe.wait_ge(cv_d, l + 1)
                    else:
                        pe.wait_ge(ln_sq, l + 1)
                    src = acc if name == "mu" else G
                    claim(pe, (name, l))
                    for c2 in range(2):
                        last = mm(bank((name, l))[:, 0:n_ln], ones, src[:, c2, 0:n_ln], c2 == 0, c2 == 1)
                    made(last, (name, l))

                staged = [j for j in in_jobs(l) if j[0] in ("ka", "b", "qa")]
                prev, jobs = None, in_jobs(l)
                for x_, job in enumerate(jobs):
                    seg, t = job
                    key = ("in", l) + job
                    unit = ring[:, slot(l, (seg,))]
                    if x_ == 0 or jobs[x_ - 1][0] != seg:
                        arrived(pe, l, (seg,))
                    claim(pe, key)
                    for k in range(KD):
                        if seg == "uc":
                            last = mm(bank(key)[:, 0:n_ln], unit[:, k, t * P:(t + 1) * P], HT[:, k, 0:n_ln], k == 0, k == KD - 1)
                        elif seg == "b" and l and t >= 2:
                            last = mm(bank(key)[:, 256:512], HT[:, k, t * P:(t + 1) * P], unit[:, k, 256:512], k == 0, k == KD - 1)
                        else:
                            last = mm(bank(key), HT[:, k, t * P:(t + 1) * P], unit[:, k], k == 0, k == KD - 1)
                    made(last, key)
                    if x_ == len(jobs) - 1 or jobs[x_ + 1][0] != seg:
                        pe.drain().then_inc(ring_free[slot(l, (seg,))], 1)
                    if prev:
                        transposes(prev)
                    prev = job if job in staged else None
                    if quad_after(l, job):
                        ada(*quad_after(l, job))
                    if job in SUMS_AFTER:
                        channel_sums(SUMS_AFTER[job])
                if prev:
                    transposes(prev)
                if l == 0:
                    mod_columns(1)
                barrier(pe, bar(l, 2))

                units, tj = units_of(l), t_jobs(l)
                for st_ in attention_steps(l):
                    what, x_ = st_
                    if what == "S":
                        i, u = units[x_]
                        k0 = 0 if i < 2 else S_LAT
                        for m in range(2):
                            claim(pe, ("S", l, x_, m))
                        for m in range(2):
                            rows = slice(64 * m, 64 * m + 64)
                            made(mm(bank(("S", l, x_, m))[:, 0:TOK - k0], qT[rows, u, i * P:(i + 1) * P], kT[rows, u, k0:TOK], True, True), ("S", l, x_, m))
                    elif what == "T":
                        n, m = tj[x_]
                        i, u = units[n]
                        key = ("T", l, x_)
                        pe.wait_ge(pr_done[l], n + 1)
                        claim(pe, key)
                        for kt in range(4 if i < 2 else 2):
                            last = t_.transpose(bank(key)[:, kt * P:(kt + 1) * P], PB[:, n % 2, m, kt * P:(kt + 1) * P], ident)
                        made(last, key)
                    elif what == "O":
                        n, m = tj[x_]
                        i, u = units[n]
                        key = ("O", l, x_)
                        wait_taken(pe, ("T", l, x_))
                        claim(pe, key)
                        c0, w = (u * P, P) if u < BLK_A else (512 + (u - BLK_A) * HD, HD)
                        nkt = 4 if i < 2 else 2
                        for kt in range(nkt):
                            last = mm(bank(key)[:, 0:w], aT[:, x_ % 2, kt * P:(kt + 1) * P], V[:, 4 - nkt + kt, c0:c0 + w], kt == 0, kt == nkt - 1)
                        made(last, key)
                    else:
                        pe.wait_ge(o_done[l], x_ + 1)
                        for name, b0, b1 in (("MA", 0, 4), ("MB", 4, 6)):
                            key = (name, l, x_)
                            claim(pe, key)
                            for b in range(b0, b1):
                                last = t_.transpose(bank(key)[:, (b - b0) * P:(b - b0 + 1) * P], O[x_ % 2][:, b * P:(b + 1) * P], ident)
                            made(last, key)
                barrier(pe, bar(l, 3))

                def route(i):
                    pe.wait_ge(h2_done[l], i + 1)
                    for h in range(2):
                        key = ("h2T", l, i, h)
                        claim(pe, key)
                        for b in range(4):
                            k = 4 * h + b
                            last = t_.transpose(bank(key)[:, b * P:(b + 1) * P], H2[:, i, k * P:(k + 1) * P], ident)
                        made(last, key)
                    for h in range(2):
                        wait_taken(pe, ("h2T", l, i, h))
                    key = ("rt", l, i)
                    claim(pe, key)
                    for k in range(KD):
                        last = mm(bank(key)[:, 0:E_N], hTr[:, k], rw[:, k], k == 0, k == KD - 1)
                    made(last, key)

                for h in range(OUT_N):
                    arrived(pe, l, ("out", h))
                for i in range(nq):
                    for h in range(OUT_N):
                        key = ("wo", l, i, h)
                        claim(pe, key)
                        for k in range(KD):
                            last = mm(bank(key), HT[:, k, i * P:(i + 1) * P], ring[:, slot(l, ("out", h)), k], k == 0, k == KD - 1)
                        made(last, key)
                        if i == nq - 1:
                            pe.drain().then_inc(ring_free[slot(l, ("out", h))], 1)
                    if i:
                        route(i - 1)
                route(nq - 1)
                key = ("rk", l)
                pe.wait_ge(m_done, 2 * l + 1)
                claim(pe, key)
                out = bank(key)[:, 0:nq * E_N]
                mm(out, tri, MM[:, 0:nq].rearrange("p t e -> p (t e)"), True, False)
                pe.wait_ge(m_done, 2 * l + 2)
                mm(out, ones, PM[:, 0:nq].rearrange("p t e -> p (t e)"), False, True)
                made(mm(bank(key)[:, TILES * E_N:(TILES + 1) * E_N], ones, PM[:, nq], True, True), key)
                barrier(pe, bar(l, 4))

                pe.wait_ge(nb_ready, l + 1)
                pe.sem_inc(xt_full[l], 1)
                done = pe.alloc_register(f"pe_blocks_{l}")
                pe.reg_mov(done, 0)

                def gT_product(b, free=()):
                    hold(pe, g_rdy[l], b, pe_passed)
                    for k in range(4):
                        last = t_.transpose(ps[:, B_GT, k * SLOT:(k + 1) * SLOT], gg[0:SLOT, k * P:(k + 1) * P], ident[0:SLOT, 0:SLOT])
                        if k < len(free):
                            last.then_inc(ring_free[free[k]], 1)
                    last.then_inc(gt_full[l], 1)

                def w2_product(b, sl, until=None):
                    pe.wait_ge(gt_rdy[l], b)
                    pe.wait_ge(y_rdy[l], b + 1)
                    if until is not None:
                        pe.wait_ge(ring_full[sl], until)
                    w = unit_of_slot(sl).rearrange("p k n -> p (k n)").rearrange("p (k n) -> p k n", k=4)
                    for k in range(4):
                        for h in range(2):
                            last = mm(ps[64 * h:64 * h + 64, B_W2, :], gT[:, k], w[:, k, h * CHUNK:(h + 1) * CHUNK], k == 0, k == 3)
                    last.then_inc(w2_full[l], 1)

                def step(slots, prev_slot, waits, free=(), first=False):
                    b = pe.snap(done)
                    hold(pe, gath[l], 16 * b + 16, pe_passed)
                    for k in range(KD):
                        last = t_.transpose(ps[:, B_XT, k * SLOT:(k + 1) * SLOT], xg[0:SLOT, k * P:(k + 1) * P], ident[0:SLOT, 0:SLOT])
                        if k < len(free):
                            last.then_inc(ring_free[free[k]], 1)
                    last.then_inc(xt_full[l], 1)
                    if not first:
                        gT_product(b)
                    pe.wait_ge(xt_rdy[l], b + 1)
                    if waits:
                        for q in range(2):
                            pe.wait_ge(ring_full[slots[q]], waits[q])
                    for k in range(KD):
                        for h in range(2):
                            last = mm(ps[64 * h:64 * h + 64, B_W13, :], xT[:, k], unit_of_slot(slots[h])[:, k], k == 0, k == KD - 1)
                    last.then_inc(w13_full[l], 1)
                    if not first:
                        w2_product(b, prev_slot, waits[2] if waits else None)
                    pe.reg_add(done, done, 1)

                def expert(e, turn, at_e, first=False):
                    sl, before = expert_slots(l, e), expert_slots(l, e - 1)
                    waits = [16 * expert_uses(l, e, x, turn) + 16 for x in sl[:2]]
                    free = []
                    if not first:
                        waits.append(16 * expert_uses(l, e - 1, before[2], turn) + 16)
                        free = [before[0], before[1]]
                        if not (isinstance(turn, int) and e < 2):
                            free.append(expert_slots(l, e - 2)[2])
                    else:
                        waits.append(None)
                    blocks = pe.value_load(nb[0:1, bass.ds(at_e, 1)], min_val=0, max_val=JMAX)
                    step(sl, before[2], waits, free, first)
                    with pe.If(blocks > 1):
                        hold(pe, ring_full[sl[2]], 16 * expert_uses(l, e, sl[2], turn) + 16, pe_passed)
                        with pe.Fori(1, blocks):
                            step(sl, sl[2], None)

                expert(0, 0, 0, True)
                for e in range(1, GROUPS + 1):
                    expert(e, 0, e)
                with pe.Fori(1, (E_N - 1) // GROUPS) as i:
                    for q in range(GROUPS):
                        expert(1 + q, i, 3 * i + 1 + q)
                b = pe.snap(done)
                last_e = E_N - 1
                sl = expert_slots(l, last_e)
                gT_product(b, [sl[0], sl[1], expert_slots(l, last_e - 1)[2]])
                w2_product(b, sl[2], 16 * expert_uses(l, last_e, sl[2]) + 16)
                pe.drain().then_inc(ring_free[sl[2]], 1)
                barrier(pe, bar(l, 5))
                if l == DEPTH - 1:
                    barrier(pe, bar(l, 6))


N_PAR = 5 * DEPTH + 5

_NAMES = ["x", "c", "ctx", "c_ctx", "w_ada", "b_ada", "g_mix", "w_in", "diff_lambda", "diff_norm_g", "attn_sink", "conv_w", "conv_b",
          "conv_ln_g", "conv_ln_b", "w_out", "g_ffn", "router_w", "router_bias", "w1", "w3", "w2", "g_final"]


def kernel(**inputs):
    import concourse.bacc as bacc
    from concourse.bass_utils import run_bass_kernel_spmd

    nc = bacc.Bacc("TRN2", target_bir_lowering=False, num_devices=1)
    arrays, A = {}, {}
    for name in _NAMES:
        a = np.ascontiguousarray(inputs[name])
        arrays[f"in_{name}"] = a
        A[name] = nc.dram_tensor(f"in_{name}", a.shape, mybir.dt.from_np(a.dtype), kind="ExternalInput").ap()
    arrays["in_cst"] = constants()
    A["cst"] = nc.dram_tensor("in_cst", arrays["in_cst"].shape, mybir.dt.float32, kind="ExternalInput").ap()
    A["out"] = nc.dram_tensor("out", (1, S_LAT, D), mybir.dt.float32, kind="ExternalOutput").ap()
    hybrid_moe_kernel(nc, A)
    return run_bass_kernel_spmd(nc, [arrays], core_ids=[0]).results[0]["out"]
```
